# Optimizing a Trainium2 kernel written in Bass

```python
import math
import jax, jax.numpy as jnp
from jax import lax
import numpy as np

D_MODEL = 1024
BATCH = 1
SEQ = 1024
DEPTH = 1

ATTN_HEADS = 8
ATTN_KV_GROUPS = 2
HEAD_DIM = 64
IDX_HEADS = 4
IDX_DIM = 64
TOPK_MAX = 256
Q_BLOCK = 128
NUM_BUCKETS = 32
MAX_DISTANCE = 128
HGRN_HEADS = 4
HGRN_DIM = 128
HGRN_CHUNK = 64
CONV_W = 512
CONV_K = 3
D_FF = 4 * D_MODEL

ATTN_W = ATTN_HEADS * HEAD_DIM
KV_W = ATTN_KV_GROUPS * HEAD_DIM
HGRN_W = HGRN_HEADS * HGRN_DIM
N_BRANCH = 3
EPS = 1e-6
SPLITS = (ATTN_W, KV_W, KV_W,
          IDX_HEADS * IDX_DIM, IDX_DIM, IDX_HEADS,
          HGRN_W, HGRN_W, HGRN_W, HGRN_W,
          CONV_W, CONV_W, CONV_W,
          N_BRANCH * D_MODEL)
D_IN_PROJ = sum(SPLITS)


def _rmsnorm(x, g):
    xf = x.astype(jnp.float32)
    y = xf * lax.rsqrt(jnp.mean(xf * xf, axis=-1, keepdims=True) + EPS)
    return (y * g.astype(jnp.float32)).astype(x.dtype)

def _split_cols(p):
    offs, acc = [], 0
    for w in SPLITS[:-1]:
        acc += w
        offs.append(acc)
    return jnp.split(p, offs, axis=-1)

def _t5_bucket(dist):
    max_exact = NUM_BUCKETS // 2
    d = jnp.maximum(dist, 0)
    df = jnp.maximum(d, 1).astype(jnp.float32)
    large = max_exact + (jnp.log(df / max_exact) / math.log(MAX_DISTANCE / max_exact)
                         * (NUM_BUCKETS - max_exact)).astype(jnp.int32)
    large = jnp.minimum(large, NUM_BUCKETS - 1)
    return jnp.where(d < max_exact, d, large)

def _dsa_attention(q, k, v, qi, ki, wi, rel_bias):
    b, s = q.shape[0], q.shape[1]
    n_sel = min(TOPK_MAX, s // 4)
    nb = s // Q_BLOCK
    npg = ATTN_HEADS // ATTN_KV_GROUPS
    scale = HEAD_DIM ** -0.5
    wi = wi * (IDX_HEADS ** -0.5 * IDX_DIM ** -0.5)
    key_pos = jnp.arange(s)
    bidx = jnp.arange(b)[:, None, None]

    def blocks(a):
        return jnp.moveaxis(a.reshape((b, nb, Q_BLOCK) + a.shape[2:]), 1, 0)

    def one_block(args):
        blk, q_b, qi_b, wi_b = args
        t = blk * Q_BLOCK + jnp.arange(Q_BLOCK)
        sc = jax.nn.relu(jnp.einsum('bqhd,bsd->bqhs', qi_b, ki))
        sc = jnp.einsum('bqhs,bqh->bqs', sc, wi_b).astype(jnp.float32)
        causal = key_pos[None, :] <= t[:, None]
        sc = jnp.where(causal[None], sc, -jnp.inf)
        _, idx = lax.top_k(sc, n_sel)
        valid = idx <= t[None, :, None]
        k_sel = k[bidx, idx]
        v_sel = v[bidx, idx]
        qg = q_b.reshape(b, Q_BLOCK, ATTN_KV_GROUPS, npg, HEAD_DIM)
        logits = jnp.einsum('bqgnd,bqkgd->bqgnk', qg, k_sel).astype(jnp.float32) * scale
        bias = rel_bias[_t5_bucket(t[None, :, None] - idx)]
        bias = jnp.moveaxis(bias, -1, 2).reshape(b, Q_BLOCK, ATTN_KV_GROUPS, npg, n_sel)
        logits = jnp.where(valid[:, :, None, None, :], logits + bias.astype(jnp.float32), -jnp.inf)
        p = jax.nn.softmax(logits, axis=-1).astype(v.dtype)
        o = jnp.einsum('bqgnk,bqkgd->bqgnd', p, v_sel)
        return o.reshape(b, Q_BLOCK, ATTN_W)

    out = lax.map(one_block, (jnp.arange(nb), blocks(q), blocks(qi), blocks(wi)))
    return jnp.moveaxis(out, 0, 1).reshape(b, s, ATTN_W)

def _hgrn2(q, f_logit, i, lb):
    b, s = q.shape[0], q.shape[1]
    nc = s // HGRN_CHUNK
    f32 = jnp.float32
    z = f_logit.astype(f32)
    lb = lb.astype(f32).reshape(HGRN_HEADS, HGRN_DIM)
    log_f = jnp.logaddexp(jnp.log(lb), jnp.log1p(-lb) + jax.nn.log_sigmoid(z))
    kk = (1.0 - lb) * jax.nn.sigmoid(-z)

    def chunks(a):
        return a.reshape(b, nc, HGRN_CHUNK, HGRN_HEADS, HGRN_DIM).transpose(1, 0, 3, 2, 4)

    tri = jnp.tril(jnp.ones((HGRN_CHUNK, HGRN_CHUNK), dtype=bool))

    def step(state, inp):
        qc, kc, ic, gc = inp
        G = jnp.cumsum(gc, axis=2)
        diff = G[:, :, :, None, :] - G[:, :, None, :, :]
        decay = jnp.exp(jnp.where(tri[:, :, None], diff, -jnp.inf))
        attn = jnp.einsum('bhtd,bhsd,bhtsd->bhts', qc, kc, decay)
        o = attn @ ic + jnp.einsum('bhtd,bhdv->bhtv', qc * jnp.exp(G), state)
        g_last = G[:, :, -1:, :]
        state = (jnp.exp(g_last[:, :, 0, :, None]) * state
                 + jnp.einsum('bhsd,bhsv->bhdv', kc * jnp.exp(g_last - G), ic))
        return state, o

    s0 = jnp.zeros((b, HGRN_HEADS, HGRN_DIM, HGRN_DIM), f32)
    _, o = lax.scan(step, s0, (chunks(q.astype(f32)), chunks(kk), chunks(i.astype(f32)), chunks(log_f)))
    return o.transpose(1, 0, 3, 2, 4).reshape(b, s, HGRN_HEADS, HGRN_DIM)

def _short_conv(u, w):
    kern = w[:, None, :].astype(u.dtype)
    return lax.conv_general_dilated(u, kern, (1,), [(CONV_K - 1, 0)],
                                    dimension_numbers=('NWC', 'WIO', 'NWC'),
                                    feature_group_count=u.shape[-1])

def first_inputs(seed: int = 0) -> dict:
    key = jax.random.key(seed)
    ks = jax.random.split(key, 16)
    f32 = jnp.float32

    def nrm(k, shape, scale):
        return jax.random.normal(k, shape, f32) * scale

    def gain(k, shape):
        return 1.0 + 0.02 * jax.random.normal(k, shape, f32)

    return {
        'x': nrm(ks[0], (BATCH, SEQ, D_MODEL), 1.0),
        'rel_bias': nrm(ks[1], (NUM_BUCKETS, ATTN_HEADS), 0.5),
        'hgrn_lb': nrm(ks[2], (DEPTH, HGRN_W), 1.0),
        'ln_mix_g': gain(ks[3], (DEPTH, D_MODEL)),
        'w_in': nrm(ks[4], (DEPTH, D_MODEL, D_IN_PROJ), D_MODEL ** -0.5),
        'q_norm_g': gain(ks[5], (DEPTH, HEAD_DIM)),
        'k_norm_g': gain(ks[6], (DEPTH, HEAD_DIM)),
        'hgrn_norm_g': gain(ks[7], (DEPTH, HGRN_DIM)),
        'conv_w': nrm(ks[8], (DEPTH, CONV_K, CONV_W), CONV_K ** -0.5),
        'w_up_attn': nrm(ks[9], (DEPTH, ATTN_W, D_MODEL), ATTN_W ** -0.5),
        'w_up_hgrn': nrm(ks[10], (DEPTH, HGRN_W, D_MODEL), HGRN_W ** -0.5),
        'w_up_conv': nrm(ks[11], (DEPTH, CONV_W, D_MODEL), CONV_W ** -0.5),
        'w_out': nrm(ks[12], (DEPTH, D_MODEL, D_MODEL), D_MODEL ** -0.5),
        'ln_mlp_g': gain(ks[13], (DEPTH, D_MODEL)),
        'w_mlp_up': nrm(ks[14], (DEPTH, D_MODEL, D_FF), D_MODEL ** -0.5),
        'w_mlp_down': nrm(ks[15], (DEPTH, D_FF, D_MODEL), D_FF ** -0.5),
    }

def first_block(x, rel_bias, hgrn_lb, ln_mix_g, w_in, q_norm_g, k_norm_g, hgrn_norm_g,
              conv_w, w_up_attn, w_up_hgrn, w_up_conv, w_out, ln_mlp_g, w_mlp_up, w_mlp_down):
    b, s, _ = x.shape
    lb_all = jnp.cumsum(jax.nn.softmax(hgrn_lb.astype(jnp.float32), axis=0), axis=0)
    lb_all = lb_all - lb_all[0]
    for l in range(DEPTH):
        h = _rmsnorm(x, ln_mix_g[l])
        proj = h @ w_in[l]
        (aq, ak, av, iq, ik, iw, hq, hf, hi, hg, cb, cc, ch, gates) = _split_cols(proj)
        q = _rmsnorm(aq.reshape(b, s, ATTN_HEADS, HEAD_DIM), q_norm_g[l])
        k = _rmsnorm(ak.reshape(b, s, ATTN_KV_GROUPS, HEAD_DIM), k_norm_g[l])
        v = av.reshape(b, s, ATTN_KV_GROUPS, HEAD_DIM)
        y_attn = _dsa_attention(q, k, v, iq.reshape(b, s, IDX_HEADS, IDX_DIM), ik, iw, rel_bias)
        o = _hgrn2(hq.reshape(b, s, HGRN_HEADS, HGRN_DIM), hf.reshape(b, s, HGRN_HEADS, HGRN_DIM),
                   hi.reshape(b, s, HGRN_HEADS, HGRN_DIM), lb_all[l])
        y_hgrn = (_rmsnorm(o, hgrn_norm_g[l]).astype(x.dtype)
                  * jax.nn.silu(hg.reshape(b, s, HGRN_HEADS, HGRN_DIM))).reshape(b, s, HGRN_W)
        y_conv = cb * _short_conv(cc * ch, conv_w[l])
        g = jax.nn.sigmoid(gates.reshape(b, s, N_BRANCH, D_MODEL))
        mixed = (g[:, :, 0] * (y_attn @ w_up_attn[l])
                 + g[:, :, 1] * (y_hgrn @ w_up_hgrn[l])
                 + g[:, :, 2] * (y_conv @ w_up_conv[l]))
        x = x + mixed @ w_out[l]
        h = _rmsnorm(x, ln_mlp_g[l])
        x = x + jnp.square(jax.nn.relu(h @ w_mlp_up[l])) @ w_mlp_down[l]
    return x


MLA_HEADS = 4
QK_NOPE_DIM = 128
QK_ROPE_DIM = 64
QK_DIM = QK_NOPE_DIM + QK_ROPE_DIM
V_HEAD_DIM = 128
Q_LORA_RANK = 512
KV_LORA_RANK = 256
MLA_WIDTH = MLA_HEADS * V_HEAD_DIM
ROPE_THETA = 10000.0
POOL_WINDOWS = (2, 4, 8, 16)
POOL_GROUPS = len(POOL_WINDOWS)
POOL_WIDTH = D_MODEL - MLA_WIDTH
POOL_GROUP_DIM = POOL_WIDTH // POOL_GROUPS
MIX_WIDTH = MLA_WIDTH + POOL_WIDTH
IN_SPLITS = (Q_LORA_RANK, KV_LORA_RANK, QK_ROPE_DIM, MLA_WIDTH, POOL_WIDTH, POOL_WIDTH)
IN_WIDTH = sum(IN_SPLITS)
RMS_EPS = 1e-6
LN_EPS = 1e-5


def rms_norm(x, g):
    xf = x.astype(jnp.float32)
    inv = lax.rsqrt(jnp.mean(xf * xf, axis=-1, keepdims=True) + RMS_EPS)
    return (xf * inv).astype(x.dtype) * g

def layer_norm(x, g, b):
    xf = x.astype(jnp.float32)
    mu = jnp.mean(xf, axis=-1, keepdims=True)
    var = jnp.mean(jnp.square(xf - mu), axis=-1, keepdims=True)
    return ((xf - mu) * lax.rsqrt(var + LN_EPS)).astype(x.dtype) * g + b

def rope_cos_sin(positions, dtype):
    half = QK_ROPE_DIM // 2
    inv_freq = ROPE_THETA ** (-jnp.arange(half, dtype=jnp.float32) / half)
    ang = positions.astype(jnp.float32)[..., None] * inv_freq
    return jnp.cos(ang).astype(dtype), jnp.sin(ang).astype(dtype)

def apply_rope(t, cos, sin):
    t1, t2 = jnp.split(t, 2, axis=-1)
    return jnp.concatenate([t1 * cos - t2 * sin, t1 * sin + t2 * cos], axis=-1)

def mla_branch(x_q, x_kv, k_rope_raw, positions, q_norm_g, w_uq, kv_norm_g, w_ukv):
    B, S, _ = x_q.shape
    cos, sin = rope_cos_sin(positions, x_q.dtype)
    q = (rms_norm(x_q, q_norm_g) @ w_uq).reshape(B, S, MLA_HEADS, QK_DIM)
    q_nope, q_rope = q[..., :QK_NOPE_DIM], q[..., QK_NOPE_DIM:]
    q_rope = apply_rope(q_rope, cos[:, :, None, :], sin[:, :, None, :])
    kv = (rms_norm(x_kv, kv_norm_g) @ w_ukv).reshape(B, S, MLA_HEADS, QK_NOPE_DIM + V_HEAD_DIM)
    k_nope, v = kv[..., :QK_NOPE_DIM], kv[..., QK_NOPE_DIM:]
    k_rope = apply_rope(k_rope_raw, cos, sin)
    scale = QK_DIM ** -0.5
    nb = S // Q_BLOCK
    qn_b = q_nope.reshape(B, nb, Q_BLOCK, MLA_HEADS, QK_NOPE_DIM).transpose(1, 0, 2, 3, 4)
    qr_b = q_rope.reshape(B, nb, Q_BLOCK, MLA_HEADS, QK_ROPE_DIM).transpose(1, 0, 2, 3, 4)
    pos_b = positions.reshape(B, nb, Q_BLOCK).transpose(1, 0, 2)
    neg = jnp.finfo(jnp.float32).min

    def attend(args):
        qn, qr, pq = args
        s = (jnp.einsum('bqhd,bkhd->bhqk', qn, k_nope)
             + jnp.einsum('bqhr,bkr->bhqk', qr, k_rope)).astype(jnp.float32) * scale
        mask = pq[:, None, :, None] >= positions[:, None, None, :]
        p = jax.nn.softmax(jnp.where(mask, s, neg), axis=-1)
        return jnp.einsum('bhqk,bkhd->bqhd', p.astype(v.dtype), v)

    o = lax.map(attend, (qn_b, qr_b, pos_b))
    return o.transpose(1, 0, 2, 3, 4).reshape(B, S, MLA_WIDTH)

def pool_branch(u, pool_w, pool_scale):
    B, S, _ = u.shape
    uf = u.astype(jnp.float32).reshape(B, S, POOL_GROUPS, POOL_GROUP_DIM)
    cs = jnp.concatenate([jnp.zeros((B, 1, POOL_GROUPS, POOL_GROUP_DIM), jnp.float32),
                          jnp.cumsum(uf, axis=1)], axis=1)
    hi = jnp.arange(S) + 1
    means = []
    for g, w in enumerate(POOL_WINDOWS):
        lo = jnp.maximum(hi - w, 0)
        cnt = (hi - lo).astype(jnp.float32)[None, :, None]
        means.append((cs[:, hi, g] - cs[:, lo, g]) / cnt)
    pooled = jnp.stack(means, axis=2) - uf
    mixed = jnp.einsum('bsgc,gcd->bsgd', pooled.astype(u.dtype), pool_w)
    return mixed.reshape(B, S, POOL_WIDTH) * pool_scale

def second_inputs(seed: int = 0) -> dict:
    key = jax.random.key(seed)
    ks = jax.random.split(key, 12)
    beta = (8.0 * DEPTH) ** -0.25
    nrm = jax.random.normal
    return {
        "x": nrm(ks[0], (BATCH, SEQ, D_MODEL), jnp.float32),
        "positions": jnp.broadcast_to(jnp.arange(SEQ, dtype=jnp.int32), (BATCH, SEQ)),
        "w_in": nrm(ks[1], (D_MODEL, IN_WIDTH), jnp.float32) * D_MODEL ** -0.5,
        "q_norm_g": 1.0 + 0.05 * nrm(ks[2], (Q_LORA_RANK,), jnp.float32),
        "w_uq": nrm(ks[3], (Q_LORA_RANK, MLA_HEADS * QK_DIM), jnp.float32) * Q_LORA_RANK ** -0.5,
        "kv_norm_g": 1.0 + 0.05 * nrm(ks[4], (KV_LORA_RANK,), jnp.float32),
        "w_ukv": nrm(ks[5], (KV_LORA_RANK, MLA_HEADS * (QK_NOPE_DIM + V_HEAD_DIM)), jnp.float32) * KV_LORA_RANK ** -0.5,
        "pool_w": nrm(ks[6], (POOL_GROUPS, POOL_GROUP_DIM, POOL_GROUP_DIM), jnp.float32) * POOL_GROUP_DIM ** -0.5,
        "pool_scale": 1.0 + 0.1 * nrm(ks[7], (POOL_WIDTH,), jnp.float32),
        "w_out": nrm(ks[8], (MIX_WIDTH, D_MODEL), jnp.float32) * (MIX_WIDTH ** -0.5) * beta,
        "ln_g": 1.0 + 0.05 * nrm(ks[9], (DEPTH, D_MODEL), jnp.float32),
        "ln_b": 0.02 * nrm(ks[10], (DEPTH, D_MODEL), jnp.float32),
    }

def second_block(x, positions, w_in, q_norm_g, w_uq, kv_norm_g, w_ukv, pool_w, pool_scale, w_out, ln_g, ln_b):
    alpha = (2.0 * DEPTH) ** 0.25
    splits = [int(c) for c in np.cumsum(IN_SPLITS)[:-1]]
    for layer in range(DEPTH):
        h = x @ w_in
        x_q, x_kv, k_rope_raw, gate_a, u_pool, gate_b = jnp.split(h, splits, axis=-1)
        y_a = mla_branch(x_q, x_kv, k_rope_raw, positions, q_norm_g, w_uq, kv_norm_g, w_ukv) * jax.nn.silu(gate_a)
        y_b = pool_branch(u_pool, pool_w, pool_scale) * jax.nn.silu(gate_b)
        mix = jnp.concatenate([y_a, y_b], axis=-1) @ w_out
        x = layer_norm(alpha * x + mix, ln_g[layer], ln_b[layer])
    return x


def setup_inputs(seed=0):
    out = dict(first_inputs(seed))
    for name, value in second_inputs(seed + 1).items():
        if name != "x":
            out[name + "_2"] = value
    return out


def reference(
    x, rel_bias, hgrn_lb, ln_mix_g, w_in, q_norm_g, k_norm_g, hgrn_norm_g, conv_w, w_up_attn,
    w_up_hgrn, w_up_conv, w_out, ln_mlp_g, w_mlp_up, w_mlp_down, positions_2, w_in_2,
    q_norm_g_2, w_uq_2, kv_norm_g_2, w_ukv_2, pool_w_2, pool_scale_2, w_out_2, ln_g_2, ln_b_2,
):
    x = first_block(
        x, rel_bias, hgrn_lb, ln_mix_g, w_in, q_norm_g, k_norm_g, hgrn_norm_g, conv_w,
        w_up_attn, w_up_hgrn, w_up_conv, w_out, ln_mlp_g, w_mlp_up, w_mlp_down,
    )
    return second_block(
        x, positions_2, w_in_2, q_norm_g_2, w_uq_2, kv_norm_g_2, w_ukv_2, pool_w_2,
        pool_scale_2, w_out_2, ln_g_2, ln_b_2,
    )


_drawn_inputs = setup_inputs


def setup_inputs(seed=0):
    import zlib

    import numpy as np

    out = dict(_drawn_inputs(seed))
    spreads = {}
    factors = {'q_norm_g': 8.0,
     'k_norm_g': 8.0,
     'hgrn_norm_g': 8.0,
     'ln_mlp_g': 3.107,
     'q_norm_g_2': 8.0,
     'kv_norm_g_2': 8.0,
     'ln_b_2': 2.87}
    for name, (base, spread) in spreads.items():
        noise = np.random.default_rng([zlib.crc32(name.encode()), seed]).standard_normal(out[name].shape)
        drawn = base * np.exp(spread * noise) if base else spread * noise
        out[name] = __import__('jax').numpy.asarray(drawn.astype(out[name].dtype))
    for name, factor in factors.items():
        out[name] = (out[name] * factor).astype(out[name].dtype)
    return out
```

```python
from contextlib import ExitStack

import numpy as np
import concourse.bass as bass
from concourse import mybir

F32 = mybir.dt.float32
F32R = mybir.dt.float32r
I32 = mybir.dt.int32
ACT = mybir.ActivationFunctionType
ALU = mybir.AluOpType
AX = mybir.AxisListType

P = 128
S = 1024
D = 1024
NT = D // P
NB = S // P
HALF = 512
EPS = 1e-6
LN_EPS = 1e-5

HEADS, HD, TOPK = 8, 64, 256
IDX_HEADS = 4
BUCKETS, MAX_DIST = 32, 128
HG_HEADS = 4
LEVELS = 7
CONV_T = 4
D_FF = 4096
MLA_HEADS = 4
POOL_WINDOWS = (2, 4, 8, 16)
ROPE_HALF = 32

NEG = -1.0e30
FILL = -1.0e38
PICKED = -3.0e38
TWO_PI = 2.0 * np.pi
MAGIC = 1.5 * 2.0 ** 23

N_QK, N_CONV, N_HG, N_GATE = 9, 12, 16, 24
N_IN = N_QK + N_CONV + N_HG + N_GATE
N_UP = 24
N_OUT = 8
N_GROUP = 4
N_MLP = 16 * N_GROUP
N_IN2 = 19
N_UQ = 6
N_UKV = 8
N_OUT2 = 8
FIRST = {}
_n = 0
for _name, _count in (("in", N_IN), ("up", N_UP), ("out", N_OUT), ("mlp", N_MLP), ("in2", N_IN2),
                      ("uq", N_UQ), ("ukv", N_UKV), ("out2", N_OUT2)):
    FIRST[_name] = _n
    _n += _count
N_UNITS = _n

CST = {}
_c = 0
for _name, _w in (("ident", P), ("mean64", P), ("mean128", P), ("mean256", P), ("mean512", P),
                  ("mean1024", P), ("causal", P), ("causal_neg", P), ("reset", S), ("bucket", 384),
                  ("pool", 4 * 16), ("rope", 8), ("swap", P)):
    CST[_name] = (_c, _w)
    _c += _w
N_CST = _c


def shape_constants():
    c = np.zeros((P, N_CST), np.float32)

    def put(name, value):
        a, w = CST[name]
        c[:value.shape[0], a:a + w] = value

    i = np.arange(P)
    put("ident", np.eye(P, dtype=np.float32))
    put("mean64", ((i[:, None] // 64) == (i[None, :] // 64)) / np.float32(64))
    for n in (128, 256, 512, 1024):
        put(f"mean{n}", np.full((P, P), 1.0 / n, np.float32))
    put("causal", np.where(i[None, :] > i[:, None], FILL, 0.0).astype(np.float32))
    put("causal_neg", np.where(i[None, :] > i[:, None], NEG, 0.0).astype(np.float32))
    put("reset", np.broadcast_to((np.arange(S) % P != 0).astype(np.float32), (P, S)))
    j = np.arange(384)
    d = np.maximum(255 - j, 0)
    half = BUCKETS // 2
    far = half + (np.log(np.maximum(d, 1).astype(np.float32) / np.float32(half))
                  / np.float32(np.log(MAX_DIST / half)) * np.float32(BUCKETS - half)).astype(np.int32)
    b = np.where(d < half, d, np.minimum(far, BUCKETS - 1))
    hot = np.zeros((BUCKETS, 384), np.float32)
    hot[b, j] += 1.0
    hot[BUCKETS - 1, :] -= 1.0
    put("bucket", hot)
    pool = np.zeros((P, 4, 16), np.float32)
    for g, w in enumerate(POOL_WINDOWS):
        pool[:, g, :] = 1.0 / np.minimum(np.arange(16) + 1, w)
    put("pool", pool.reshape(P, 64))
    rope = np.zeros((P, 8), np.float32)
    rope[:, 0] = (np.float32(10000.0) ** (-(i % ROPE_HALF).astype(np.float32) / ROPE_HALF))
    rope[:, 1] = EPS
    rope[:, 2] = LN_EPS
    put("rope", rope)
    swap = np.zeros((P, P), np.float32)
    for o in range(P):
        swap[o ^ ROPE_HALF, o] = 1.0 if o & ROPE_HALF else -1.0
    put("swap", swap)
    masks = np.zeros((P, LEVELS + 1, P), np.int32)
    for lv in range(LEVELS):
        m = 64 >> lv
        same = (i[:, None] // (2 * m)) == (i[None, :] // (2 * m))
        masks[:, lv, :] = same & ((i[:, None] // m) % 2 == 0) & ((i[None, :] // m) % 2 == 1)
    masks[:, LEVELS, :] = np.eye(P, dtype=np.int32)
    return c, masks.reshape(P, -1)


SMALL = {}
_c = 0
for _name, _w in (("ln_mix", 8), ("ln_mlp", 8), ("hg_norm", 1), ("q_norm", 1), ("k_norm", 1), ("conv", 12),
                  ("pool_scale", 4), ("q_norm_2", 4), ("kv_norm_2", 2), ("ln_g", 8), ("ln_b", 8)):
    SMALL[_name] = (_c, _w)
    _c += _w
N_SMALL = _c



def attention_uses(st, heads):
    uses, n = [("qk", st, 0)], NB * heads
    for i in range(n + 3):
        uses += [("qk", st, i + 1)] * (i + 1 < n)
        uses += [("yT", st, (i - 2) // heads - 1)] * (i >= 3 and (i - 2) % heads == 0)
    return uses


def misc_plan():
    uses = [("stat", "x"), "iwT"]
    uses += [("idx", b, h) for b in range(2, NB) for h in range(IDX_HEADS)]
    uses += ["vT"] + [("bias", h) for h in range(HEADS)]
    uses += [("stat", "qk", j) for j in range(5)]
    for h in range(HG_HEADS):
        uses += [("iT", h)] + [("lv", h, lv) for lv in range(LEVELS + 1)]
        uses += [("kT", h), ("dS", h), ("o", h), ("stat", "hg", h)]
    uses += attention_uses(0, HEADS)
    uses += [("stat", "x1")]
    uses += [("pool", g) for g in range(4)]
    uses += [("stat", "xq"), ("stat", "xkv"), ("swap", 0), ("swap", 1), ("swap", 2)]
    uses += [("v2T", h) for h in range(MLA_HEADS)]
    uses += attention_uses(1, MLA_HEADS)
    uses += ["mu", ("stat", "var")]
    plan, ready, free = {}, [0, 0], [0, 0]
    for m, key in enumerate(uses):
        s = m % 2
        ready[s] += not (isinstance(key, tuple) and key[0] == "stat")
        plan[key] = (s, ready[s], free[s])
        free[s] += 1
    return plan


STATS = [("x", NT)] + [(("qk", j), 1) for j in range(5)] + [(("hg", h), 1) for h in range(HG_HEADS)]
STATS += [("x1", NT), ("xq", 4), ("xkv", 2), ("var", NT)]
STAT_BASE, STAT_NO = {}, {}
_c = 0
for _i, (_k, _w) in enumerate(STATS):
    STAT_BASE[_k], STAT_NO[_k] = _c, _i
    _c += _w


def build(nc, t):
    with ExitStack() as ctx:
        BASE = 16512
        MISC = misc_plan()

        def sem(name):
            return ctx.enter_context(nc.semaphore(name))

        def at(name, kb, shape, dt=F32):
            return nc.alloc_sbuf_tensor_at(name, shape, dt, offset=BASE + int(kb * 1024))

        raw = at("raw", 0, [P, 2, 1024])
        w_hi = at("w_hi", 8, [P, 2, 1024], F32R)
        w_lo = at("w_lo", 16, [P, 2, 1024], F32R)
        actA = at("actA", 24, [P, 2, NT, S], F32R)
        X0 = at("X0", 88, [P, NT, S])
        att = at("att", 88, [P, N_QK, S])
        pen = at("pen", 124, [P, 4608])
        toep = at("toep", 142, [P, HEADS, 256])
        V1 = at("V1", 150, [P, NB, P])
        ik_up = at("ik_up", 154, [P, S])
        stage = at("stage", 158, [P, 4, S])
        sq = at("sq", 176, [P, 2, S])
        cst = at("cst", 184, [P, N_CST])
        small = at("small", 194.5, [P, N_SMALL])
        iw = at("iw", 195, [P, NB, IDX_HEADS])
        tiny = at("tiny", 195.125, [P, 32])
        top8 = at("top8", 195.25, [P, 8])
        rb = at("rb", 195.3125, [BUCKETS, HEADS])
        hmask = at("hmask", 195.5, [P, LEVELS + 1, P], I32)
        rstd = at("rstd", 199.5, [P, S])
        assert 184 * 1024 + N_CST * 4 <= 194.5 * 1024 and N_SMALL * 4 <= 512
        hq = at("hq", 24, [P, 4, S])
        hG = at("hG", 40, [P, S])
        hk = at("hk", 44, [P, S])
        hE = at("hE", 48, [P, 2, S])
        hW = at("hW", 56, [P, 2, S])
        hattn = at("hattn", 64, [P, NB, P])
        hiT = at("hiT", 68, [P, NB, P])
        hkT = at("hkT", 72, [P, NB, P])
        hS = at("hS", 76, [P, NB, P])
        hqG = at("hqG", 80, [P, S])
        hy = at("hy", 84, [P, S])
        at1 = dict(L=at("a_L", 24, [P, 2, S]), Pm=at("a_P", 32, [P, 2, S]), PT=at("a_PT", 40, [P, 2, S]),
                   O=at("a_O", 48, [P, 2, HALF]))
        yT = at("yT", 158, [P, 4, S])
        ysp = at("ysp", 24, [P, 12, 2, S], F32R)
        gates = at("gates", 120, [P, 2, 3, S])
        prod = at("prod", 144, [P, 2, S])
        mixed = at("mixed", 152, [P, NT, S])
        xB = at("xB", 88, [P, NT, S])
        tmpn = at("tmpn", 158, [P, 2, S])
        uB = at("uB", 120, [P, 2, NT, S], F32R)
        mt = at("mt", 199.5, [P, 2, S])
        u2 = at("u2", 120, [P, 4, S])
        gb = at("gb", 136, [P, 4, S])
        xq = at("xq", 152, [P, 4, S])
        xkv = at("xkv", 168, [P, 2, S])
        poolw = at("poolw", 195.5, [P, 4, P])
        kr = at("kr", 195.5, [P, S])
        posb = at("posb", 203.5, [P, S])
        posi = at("posi", 203.5, [P, S], I32)
        xqS = at("xqS", 24, [P, 2, 4, S], F32R)
        xkvS = at("xkvS", 56, [P, 2, 2, S], F32R)
        tmp2 = at("tmp2", 72, [P, 2, S])
        kn = at("kn", 72, [P, 4, S])
        v4 = at("v4", 24, [P, 4, S])
        V2 = at("V2", 40, [P, NB, HALF])
        qr = at("qr", 176, [P, 2, S])
        cs = at("cs", 168, [P, 2, S])
        pen2 = at("pen2", 168, [P, 2, S])
        ang = at("ang", 80, [P, 2, S])
        at2 = dict(L=at("b_L", 56, [P, 2, S]), Pm=at("b_P", 64, [P, 2, S]), PT=at("b_PT", 24, [P, 2, S]),
                   O=at("b_O", 32, [P, 2, HALF]))
        fin = at("fin", 24, [P, 2, S])
        rtmp = at("rtmp", 40, [P, S])
        mu = at("mu", 120, [P, S])
        pad = at("pad", 195.46875, [P, 2])
        posqi = at("posqi", 195.375, [P, NB], I32)
        posqf = at("posqf", 195.4375, [P, NB])
        pair = [ctx.enter_context(nc.psum_tensor(f"pair{i}", [P, 2 * HALF], F32)) for i in range(4)]

        proj = nc.dram_tensor("proj", (N_CONV + N_HG + N_GATE, P, S), F32, kind="Internal").ap()
        ydram = nc.dram_tensor("ydram", (8, P, S), F32, kind="Internal").ap()
        skew = nc.dram_tensor("skew", (HEADS, P, 384), F32, kind="Internal")

        consts_in = sem("consts_in")
        x_in = [sem(f"x_in{i}") for i in range(2)]
        w_in = [sem("w_in0"), sem("w_in1")]
        w_split = sem("w_split")
        w_hi_ok = sem("w_hi_ok")
        unit_mm = sem("unit_mm")
        unit_out = [sem("unit_out0"), sem("unit_out1")]
        ready = [sem("ready0"), sem("ready1")]
        free = [sem("free0"), sem("free1")]
        spilled = [sem(f"spilled{i}") for i in range(4)]
        squares = sem("squares")
        squares_used = sem("squares_used")
        rstd_ok = sem("rstd_ok")
        rstd_used = sem("rstd_used")
        dve_step = sem("dve_step")
        act_step = sem("act_step")
        pool_step = sem("pool_step")
        nrm = sem("nrm")
        hi_ok = sem("hi_ok")
        lo_ok = sem("lo_ok")
        ik_copied = sem("ik_copied")
        idx_used = sem("idx_used")
        topk = sem("topk")
        pen_ok = sem("pen_ok")
        skew_out = sem("skew_out")
        toep_in = sem("toep_in")
        head_in = sem("head_in")
        y_out = sem("y_out")
        y_made = sem("y_made")
        lsg = sem("lsg")
        hk_raw = sem("hk_raw")
        hk_ok = sem("hk_ok")
        expo = sem("expo")
        decay = sem("decay")
        weighted = sem("weighted")
        hfin = sem("hfin")
        l_ok = sem("l_ok")
        nm_ok = sem("nm_ok")
        p_ok = sem("p_ok")
        pT_ps = sem("pT_ps")
        pT_ok = sem("pT_ok")
        pv_ok = sem("pv_ok")
        o_ok = sem("o_ok")
        yin_in = [sem("yin_in0"), sem("yin_in1")]
        gates_in = [sem("gates_in0"), sem("gates_in1")]
        mixed_ok = sem("mixed_ok")
        relu_ok = sem("relu_ok")
        u_ok = sem("u_ok")
        pooled_ok = sem("pooled_ok")
        poolw_in = sem("poolw_in")
        pos_in = sem("pos_in")
        trig = sem("trig")
        trig_in = sem("trig_in")
        roped = sem("roped")
        swapped_in = sem("swapped_in")
        pen2_ok = sem("pen2_ok")
        centred = sem("centred")
        fin_ok = sem("fin_ok")
        fin_out = [sem("fin_out0"), sem("fin_out1")]

        def C(name, rows=P):
            a, w = CST[name]
            return cst[0:rows, a:a + w]

        def SM(name, j=0):
            a = SMALL[name][0]
            return small[:, a + j:a + j + 1]

        EPSV = C("rope")[:, 1:2]
        LNEPSV = C("rope")[:, 2:3]

        def mpair(key):
            return pair[2 + MISC[key][0]]

        def wait_ready(eng, key):
            s, r, _ = MISC[key]
            eng.wait_ge(ready[s], r)

        def wait_done(eng, key):
            s, _, f = MISC[key]
            eng.wait_ge(free[s], f + 1)

        def wait_room(pe, key):
            s, _, f = MISC[key]
            if f > 0:
                pe.wait_ge(free[s], f)

        def R(key):
            return ready[MISC[key][0]]

        def F(key):
            return free[MISC[key][0]]

        def units(eng, first, count, width, body):
            k = count % width
            for n in range(first, first + k):
                body(n, n % 2, n // 2, n - first)
            start = first + k
            with eng.Fori(0, (count - k) // width) as i:
                for u in range(width):
                    n = start + u
                    if width % 2 == 0:
                        body(i * width + n, n % 2, i * (width // 2) + n // 2, i * width + (k + u))

        block = ctx.enter_context(nc.Block())

        @block.sync
        def _(sp):
            def load_units(name, first, count, kt):
                src = t[name]

                def body(n, par, hn, rel):
                    if isinstance(n, int) and n < 2:
                        pass
                    else:
                        sp.wait_ge(w_split, n - 1)
                    row = src[rel, :, :] if isinstance(rel, int) else \
                        src[bass.ds(rel, 1), :, :].rearrange("a p n -> p (a n)")
                    sp.dma_start(raw[:, par, 0:kt * P], row).then_inc(w_in[par], 16)
                units(sp, first, count, 2, body)

            sp.dma_start(cst[:, :], t["cst"]).then_inc(consts_in, 16)
            sp.dma_start(small[:, :], t["small"]).then_inc(consts_in, 16)
            sp.dma_start(rb[:, :], t["rel_bias"]).then_inc(consts_in, 16)
            sp.dma_start(hmask[:, :, :].rearrange("p a b -> p (a b)"), t["masks"]).then_inc(consts_in, 16)
            for j in range(NT):
                sp.dma_start(X0[:, j, :], t["xT"][j * P:(j + 1) * P, :]).then_inc(x_in[0], 16)
            load_units("w_in", 0, N_IN, 8)
            sp.wait_ge(skew_out, 16 * HEADS)
            for h in range(HEADS):
                src = bass.AP(skew, h * P * 384 + 127, [[383, P], [1, 256]])
                sp.dma_start(toep[:, h, :], src).then_inc(toep_in, 16)
            for s in range(4):
                sp.wait_ge(spilled[s], 16 * ((N_CONV + N_HG + N_GATE) // 4))
            sp.wait_ge(unit_mm, N_IN)
            for j in range(CONV_T + HG_HEADS):
                if j < CONV_T:
                    sp.dma_start(hq[:, 0:3, :], proj[3 * j:3 * j + 3].rearrange("a p n -> p a n")) \
                      .then_inc(head_in, 16)
                else:
                    a = N_CONV + 4 * (j - CONV_T)
                    sp.dma_start(hq[:, :, :], proj[a:a + 4].rearrange("a p n -> p a n")) \
                      .then_inc(head_in, 16)
                sp.wait_ge(y_made, j + 1)
                k = 4 + j if j < CONV_T else j - CONV_T
                sp.dma_start(ydram[k], hy[:, :]).then_inc(y_out, 16)
            sp.wait_ge(y_out, 16 * 8)
            for k in range(8):
                if k >= 2:
                    sp.wait_ge(lo_ok, NT + 4 + k - 1)
                sp.dma_start(sq[:, k % 2, :], ydram[k]).then_inc(yin_in[k % 2], 16)
            first = FIRST["up"]
            for j in range(2):
                for b in range(3):
                    sp.dma_start(gates[:, j, b, :], proj[N_CONV + N_HG + 8 * b + j]).then_inc(gates_in[j], 16)

            def up_pair(i, more):
                for u in range(6):
                    n = first + u
                    sp.wait_ge(w_split, i * 6 + (n - 1))
                    src = t["w_up"][i * 6 + u] if isinstance(i, int) else \
                        t["w_up"][bass.ds(i * 6 + u, 1), :, :].rearrange("a p n -> p (a n)")
                    sp.dma_start(raw[:, n % 2, 0:HALF], src).then_inc(w_in[n % 2], 16)
                for jj in range(2 if more else 0):
                    sp.wait_ge(mixed_ok, i * 2 + (jj + 1))
                    g0 = N_CONV + N_HG + 2 + jj
                    for b in range(3):
                        sp.dma_start(gates[:, jj, b, :],
                                     proj[bass.ds(i * 2 + (g0 + 8 * b), 1), :, :].rearrange("a p n -> p (a n)")) \
                          .then_inc(gates_in[jj], 16)

            with sp.Fori(0, 3) as i:
                up_pair(i, True)
            up_pair(3, False)
            sp.wait_ge(mixed_ok, NT)
            for j in range(NT):
                sp.dma_start(xB[:, j, :], t["xT"][j * P:(j + 1) * P, :]).then_inc(x_in[1], 16)
            load_units("w_out", FIRST["out"], N_OUT, 8)
            load_units("w_mlp", FIRST["mlp"], N_MLP, 8)
            load_units("w_in2", FIRST["in2"], N_IN2, 8)
            load_units("w_uq", FIRST["uq"], N_UQ, 4)
            load_units("w_ukv", FIRST["ukv"], N_UKV, 2)
            load_units("w_out2", FIRST["out2"], N_OUT2, 8)
            for k in range(NT):
                sp.wait_ge(fin_ok, k + 1)
                sp.dma_start(t["outT"][k * P:(k + 1) * P, :], fin[:, k % 2, :]).then_inc(fin_out[k % 2], 16)
            for k in range(2):
                sp.wait_ge(fin_out[k], 16 * (NT // 2))

        @block.gpsimd
        def _(pool):
            def split_units(first, count, kt):
                def body(n, par, hn, rel):
                    pool.wait_ge(w_in[par], (hn + 1) * 16)
                    if not isinstance(n, int) or n >= 2:
                        pool.wait_ge(unit_mm, n - 1)
                    nc.gpsimd.tensor_tensor(pad[:, 0:1], pad[:, 1:2], pad[:, 1:2], ALU.add)
                    w = kt * P
                    nc.gpsimd.tensor_copy(w_hi[:, par, 0:w], raw[:, par, 0:w]).then_inc(w_hi_ok, 1)
                    pool.wait_ge(w_hi_ok, n + 1)
                    nc.gpsimd.tensor_tensor(w_lo[:, par, 0:w], raw[:, par, 0:w],
                                            w_hi[:, par, 0:w].bitcast(F32), ALU.subtract).then_inc(w_split, 1)
                units(pool, first, count, 2, body)

            nc.gpsimd.memset(pad[:, :], 0.0).then_inc(pool_step, 1)
            pool.wait_ge(pool_step, 1)
            split_units(0, N_IN, 8)
            split_units(FIRST["up"], N_UP, 4)
            split_units(FIRST["out"], N_OUT + N_MLP + N_IN2, 8)
            split_units(FIRST["uq"], N_UQ, 4)
            split_units(FIRST["ukv"], N_UKV, 2)
            split_units(FIRST["out2"], N_OUT2, 8)

        @block.tensor
        def _(pe):
            def product(n, par, hn, kt, hi, lo):
                pe.wait_ge(w_split, n + 1)
                if not isinstance(n, int) or n >= 2:
                    pe.wait_ge(unit_out[par], hn)
                last = None
                for half in range(2):
                    cols = slice(half * HALF, (half + 1) * HALF)
                    for k in range(kt):
                        wk = slice(k * P, (k + 1) * P)
                        for i, (w, x) in enumerate(((w_hi, hi(k)), (w_hi, lo(k)), (w_lo, hi(k)))):
                            last = nc.tensor.matmul(pair[par][:, cols], w[:, par, wk], x[:, cols],
                                                    start=(k == 0 and i == 0), stop=(k == kt - 1 and i == 2))
                last.then_inc(unit_mm, 1)

            def products(first, count, kt, hi, lo, width=2):
                units(pe, first, count, width, lambda n, par, hn, rel: product(n, par, hn, kt, hi, lo))

            def stat(key, name, srcs_n):
                base = STAT_BASE[key]
                wait_room(pe, stat_key(key))
                for k in range(srcs_n):
                    c = base + k
                    pe.wait_ge(squares, c + 1)
                    for half in range(2):
                        cols = slice(half * HALF, (half + 1) * HALF)
                        mm = nc.tensor.matmul(mpair(stat_key(key))[:, cols], C(name), sq[:, c % 2, cols],
                                              start=(k == 0), stop=(k == srcs_n - 1))
                    mm.then_inc(squares_used, 1)

            def transposes(key, src, count):
                wait_room(pe, key)
                for c in range(count):
                    mm = nc.tensor.transpose(mpair(key)[:, c * P:(c + 1) * P], src(c), C("ident"))
                mm.then_inc(R(key), 1)

            hA = lambda k: actA[:, 0, k, :]
            lA = lambda k: actA[:, 1, k, :]
            pe.wait_ge(consts_in, 64)
            stat("x", "mean1024", NT)
            pe.wait_ge(lo_ok, NT)
            for n in range(3):
                product(n, n % 2, n // 2, 8, hA, lA)
            pe.wait_ge(unit_out[0], 2)
            pe.wait_ge(unit_out[1], 1)
            transposes("iwT", lambda c: att[:, 0, c * P:(c + 1) * P], NB)
            pe.wait_ge(ik_copied, 16)
            for b in range(2, NB):
                for h in range(IDX_HEADS):
                    key = ("idx", b, h)
                    wait_room(pe, key)
                    lo_p = (h % 2) * 64
                    ks = att[0:64, 0, :] if h % 2 == 0 else ik_up[64:128, :]
                    for c0 in range(0, P * (b + 1), HALF):
                        c1 = min(c0 + HALF, P * (b + 1))
                        mm = nc.tensor.matmul(mpair(key)[:, c0:c1],
                                              att[lo_p:lo_p + 64, 1 + h // 2, b * P:(b + 1) * P],
                                              ks[:, c0:c1], start=True, stop=True)
                    mm.then_inc(R(key), 1)
            for n in range(3, N_QK):
                product(n, n % 2, n // 2, 8, hA, lA)
            pe.wait_ge(unit_out[0], 5)
            transposes("vT", lambda c: att[:, 8, c * P:(c + 1) * P], NB)
            for h in range(HEADS):
                key = ("bias", h)
                wait_room(pe, key)
                nc.tensor.matmul(mpair(key)[:, 0:384], rb[:, h:h + 1].broadcast_to([BUCKETS, P]),
                                 C("bucket", BUCKETS), start=True, stop=True).then_inc(R(key), 1)
            products(N_QK, N_IN - N_QK, 8, hA, lA, 4)
            for j in range(5):
                stat(("qk", j), "mean64", 1)
            for h in range(HG_HEADS):
                pe.wait_ge(head_in, 16 * (CONV_T + h + 1))
                transposes(("iT", h), lambda c: hq[:, 2, c * P:(c + 1) * P], NB)
                for lv in range(LEVELS + 1):
                    key = ("lv", h, lv)
                    if lv < LEVELS:
                        pe.wait_ge(weighted, h * (LEVELS + 1) + lv + 1)
                        ks, qs = hW[:, lv % 2, :], hW[:, lv % 2, :]
                    else:
                        pe.wait_ge(hk_ok, h + 1)
                        ks, qs = hk[:, :], hq[:, 0, :]
                    wait_room(pe, key)
                    for c in range(NB):
                        cc = slice(c * P, (c + 1) * P)
                        mm = nc.tensor.matmul(mpair(key)[:, cc], ks[:, cc], qs[:, cc], start=True, stop=True)
                    mm.then_inc(R(key), 1)
                pe.wait_ge(weighted, (h + 1) * (LEVELS + 1))
                transposes(("kT", h), lambda c: hW[:, 1, c * P:(c + 1) * P], NB)
                wait_done(pe, ("kT", h))
                wait_done(pe, ("iT", h))
                wait_room(pe, ("dS", h))
                for c in range(NB - 1):
                    mm = nc.tensor.matmul(mpair(("dS", h))[:, c * P:(c + 1) * P], hkT[:, c, :], hiT[:, c, :],
                                          start=True, stop=True)
                mm.then_inc(R(("dS", h)), 1)
                wait_done(pe, ("dS", h))
                wait_done(pe, ("lv", h, LEVELS))
                wait_done(pe, ("lv", h, LEVELS - 1))
                pe.wait_ge(hfin, h + 1)
                wait_room(pe, ("o", h))
                for c in range(NB):
                    out = mpair(("o", h))[:, c * P:(c + 1) * P]
                    mm = nc.tensor.matmul(out, hiT[:, c, :], hattn[:, c, :], start=True, stop=(c == 0))
                    if c:
                        mm = nc.tensor.matmul(out, hS[:, c, :], hqG[:, c * P:(c + 1) * P],
                                              start=False, stop=True)
                mm.then_inc(R(("o", h)), 1)
                stat(("hg", h), "mean128", 1)

            def attention(st, heads, dv, buf, logits, values, i0, b0):
                N = NB * heads

                def qk(i):
                    key = ("qk", st, i)
                    wait_room(pe, key)
                    logits(i // heads, i % heads, mpair(key)).then_inc(R(key), 1)

                def turn(i):
                    pe.wait_ge(p_ok, i0 + i + 1)
                    if i0 + i > 0:
                        pe.wait_ge(pT_ok, i0 + i)
                    for kb in range(n_keys(st, i // heads) // P):
                        mm = nc.tensor.transpose(pair[0][:, kb * P:(kb + 1) * P],
                                                 buf["Pm"][:, i % 2, kb * P:(kb + 1) * P], C("ident"))
                    mm.then_inc(pT_ps, 1)

                def pv(i):
                    b, h = i // heads, i % heads
                    pe.wait_ge(pT_ok, i0 + i + 1)
                    if i0 + i >= 2:
                        pe.wait_ge(o_ok, i0 + i - 1)
                    nk = n_keys(st, b) // P
                    for kb in range(nk):
                        a = (i % 2) * HALF
                        mm = nc.tensor.matmul(pair[1][:, a:a + dv], buf["PT"][:, i % 2, kb * P:(kb + 1) * P],
                                              values(kb, h), start=(kb == 0), stop=(kb == nk - 1))
                    mm.then_inc(pv_ok, 1)

                def turn_out(b):
                    pe.wait_ge(o_ok, i0 + (b + 1) * heads)
                    transposes(("yT", st, b), lambda c: buf["O"][:, b % 2, c * P:(c + 1) * P], 4)

                qk(0)
                for i in range(N + 3):
                    if i + 1 < N:
                        qk(i + 1)
                    if i < N:
                        turn(i)
                    if 1 <= i <= N:
                        pv(i - 1)
                    if 3 <= i and (i - 2) % heads == 0:
                        turn_out((i - 2) // heads - 1)

            def logits1(b, h, out):
                n, lo_p = P * (b + 1), (h // 4) * 64
                w = min(n, 2 * P)
                for c0 in range(0, n, HALF):
                    c1 = min(c0 + HALF, n)
                    near = max(c0, n - w)
                    mm = nc.tensor.matmul(out[:, c0:c1], att[lo_p:lo_p + 64, 3 + h % 4, b * P:(b + 1) * P],
                                          att[lo_p:lo_p + 64, 7, c0:c1], start=True, stop=(near >= c1))
                    if near < c1:
                        a = near - n + 2 * P
                        mm = nc.tensor.matmul(out[:, near:c1], C("ident"), toep[:, h, a:a + c1 - near],
                                              start=False, stop=True)
                return mm

            pe.wait_ge(rstd_used, 5)
            pe.wait_ge(toep_in, 16 * HEADS)
            wait_done(pe, "vT")
            pe.wait_ge(unit_out[0], (N_IN + 1) // 2)
            pe.wait_ge(unit_out[1], N_IN // 2)
            attention(0, HEADS, HD, at1, logits1, lambda kb, h: V1[:, kb, (h // 4) * 64:(h // 4) * 64 + 64], 0, 0)

            base = NT + 12
            pe.wait_ge(lo_ok, base)
            with pe.Fori(0, N_UP // 6) as i:
                for u in range(6):
                    n = FIRST["up"] + u
                    br = u % 3
                    product(i * 6 + n, n % 2, i * 3 + n // 2, 4,
                            lambda k: ysp[:, 4 * br + k, 0, :], lambda k: ysp[:, 4 * br + k, 1, :])
            pe.wait_ge(lo_ok, base + NT)
            products(FIRST["out"], N_OUT, 8, hA, lA)
            stat("x1", "mean1024", NT)
            pe.wait_ge(lo_ok, base + 2 * NT)
            hU = lambda k: uB[:, 0, k, :]
            lU = lambda k: uB[:, 1, k, :]
            for g in range(N_GROUP):
                n0 = FIRST["mlp"] + 16 * g
                products(n0, 8, 8, hA, lA)
                pe.wait_ge(u_ok, 8 * (g + 1))
                products(n0 + 8, 8, 8, hU, lU)
            base += 3 * NT
            pe.wait_ge(lo_ok, base)
            products(FIRST["in2"], 14, 8, hA, lA)
            pe.wait_ge(poolw_in, 16)
            for g in range(4):
                key = ("pool", g)
                pe.wait_ge(pooled_ok, g + 1)
                wait_room(pe, key)
                for half in range(2):
                    cols = slice(half * HALF, (half + 1) * HALF)
                    mm = nc.tensor.matmul(mpair(key)[:, cols], poolw[:, g, :], u2[:, g, cols],
                                          start=True, stop=True)
                mm.then_inc(R(key), 1)
            products(FIRST["in2"] + 14, 5, 8, hA, lA)
            stat("xq", "mean512", 4)
            stat("xkv", "mean256", 2)
            pe.wait_ge(lo_ok, base + 4)
            products(FIRST["uq"], N_UQ, 4, lambda k: xqS[:, 0, k, :], lambda k: xqS[:, 1, k, :])
            pe.wait_ge(lo_ok, base + 6)
            products(FIRST["ukv"], N_UKV, 2, lambda k: xkvS[:, 0, k, :], lambda k: xkvS[:, 1, k, :])
            for par in range(2):
                pe.wait_ge(unit_out[par], (FIRST["ukv"] + 1 - par) // 2)
            for r in range(3):
                key = ("swap", r)
                src = qr[:, r, :] if r < 2 else kr[:, :]
                wait_room(pe, key)
                for half in range(2):
                    cols = slice(half * HALF, (half + 1) * HALF)
                    mm = nc.tensor.matmul(mpair(key)[:, cols], C("swap"), src[:, cols], start=True, stop=True)
                mm.then_inc(R(key), 1)
            for par in range(2):
                pe.wait_ge(unit_out[par], (FIRST["out2"] + 1 - par) // 2)
            for h in range(MLA_HEADS):
                transposes(("v2T", h), lambda c: v4[:, h, c * P:(c + 1) * P], NB)

            def logits2(b, h, out):
                lo_p = (h % 2) * 64
                q = slice(b * P, (b + 1) * P)
                for half in range(2):
                    cols = slice(half * HALF, (half + 1) * HALF)
                    nc.tensor.matmul(out[:, cols], xq[:, h, q], kn[:, h, cols], start=True, stop=False)
                    mm = nc.tensor.matmul(out[:, cols], qr[lo_p:lo_p + 64, h // 2, q],
                                          kr[lo_p:lo_p + 64, cols], start=False, stop=True)
                return mm

            pe.wait_ge(roped, 3)
            for h in range(2, 4):
                wait_done(pe, ("v2T", h))
            attention(1, MLA_HEADS, P, at2, logits2, lambda kb, h: V2[:, kb, h * P:(h + 1) * P],
                      NB * HEADS, NB)
            pe.wait_ge(lo_ok, base + 6 + NT)
            products(FIRST["out2"], N_OUT2, 8, hA, lA)
            for par in range(2):
                pe.wait_ge(unit_out[par], (N_UNITS + 1 - par) // 2)
            wait_room(pe, "mu")
            for half in range(2):
                cols = slice(half * HALF, (half + 1) * HALF)
                for k in range(NT):
                    mm = nc.tensor.matmul(mpair("mu")[:, cols], C("mean1024"), xB[:, k, cols],
                                          start=(k == 0), stop=(k == NT - 1))
            mm.then_inc(R("mu"), 1)
            stat("var", "mean1024", NT)

        @block.scalar
        def _(act):
            steps = [0]

            def step(ins):
                steps[0] += 1
                ins.then_inc(act_step, 1)
                act.wait_ge(act_step, steps[0])

            def stat(key, srcs, room, eps=EPSV, src_ok=None):
                base = STAT_BASE[key]
                mk = stat_key(key)
                for k, src in enumerate(srcs):
                    c = base + k
                    if c >= 2:
                        act.wait_ge(squares_used, c - 1)
                    if src_ok:
                        act.wait_ge(src_ok[0], src_ok[1] + k)
                    nc.scalar.activation(sq[:, c % 2, :], src, ACT.Square).then_inc(squares, 1)
                act.wait_ge(squares_used, base + len(srcs))
                if room:
                    act.wait_ge(*room)
                nc.scalar.activation(rstd[:, :], mpair(mk)[:, :], ACT.Ln, bias=eps).then_inc(F(mk), 1)
                wait_done(act, mk)
                nc.scalar.activation(rstd[:, :], rstd[:, :], ACT.Exp, scale=-0.5).then_inc(rstd_ok, 1)

            def his(c0, dsts, srcs, src_ok):
                for k, (d, s) in enumerate(zip(dsts, srcs)):
                    if src_ok:
                        act.wait_ge(src_ok[0], src_ok[1] + k)
                    nc.scalar.copy(d, s).then_inc(hi_ok, 1)

            act.wait_ge(consts_in, 64)
            act.wait_ge(x_in[0], 16 * NT)
            stat("x", [X0[:, j, :] for j in range(NT)], None)
            his(0, [actA[:, 0, j, :] for j in range(NT)], [tmpn[:, j % 2, :] for j in range(NT)], (nrm, 1))

            def read_unit(n, par, hn, dst, func):
                act.wait_ge(unit_mm, n + 1)
                nc.scalar.activation(dst, pair[par][:, :], func).then_inc(unit_out[par], 1)

            for n in range(N_QK):
                if n == 0:
                    act.wait_ge(lo_ok, NT)
                read_unit(n, n % 2, n // 2, att[:, n, :], ACT.Copy)
                if n == 0:
                    act.wait_ge(unit_out[0], 1)
                    act.dma_start(ik_up[64:128, :], att[0:64, 0, :]).then_inc(ik_copied, 16)
                if n == 2:
                    c = 0
                    for b in range(2, NB):
                        for h in range(IDX_HEADS):
                            wait_ready(act, ("idx", b, h))
                            if c >= 2:
                                act.wait_ge(idx_used, c - 1)
                            w = P * (b + 1)
                            nc.scalar.activation(sq[:, c % 2, 0:w], mpair(("idx", b, h))[:, 0:w], ACT.Relu) \
                              .then_inc(F(("idx", b, h)), 1)
                            c += 1
            wait_ready(act, "vT")
            nc.scalar.copy(V1[:, :, :].rearrange("p a b -> p (a b)"), mpair("vT")[:, :]).then_inc(F("vT"), 1)
            act.wait_ge(idx_used, 6 * IDX_HEADS)
            for h in range(HEADS):
                key = ("bias", h)
                wait_ready(act, key)
                if h >= 2:
                    act.wait_ge(skew_out, 16 * h)
                nc.scalar.mul(sq[:, h % 2, 0:384], mpair(key)[:, 0:384], float(HD) ** 0.5).then_inc(F(key), 1)
                wait_done(act, key)
                act.dma_start(skew.ap()[h], sq[:, h % 2, 0:384]).then_inc(skew_out, 16)

            def spill(first, quads, funcs, peel):
                def quad(i, q):
                    for s in range(4):
                        n = first + s
                        a = i * 4 + n
                        rel = i * 4 + (n - N_QK)
                        if q != 0:
                            act.wait_ge(spilled[s], (i + (first - N_QK) // 4) * 16)
                        par, hn = n % 2, i * 2 + n // 2
                        read_unit(a, par, hn, stage[:, s, :], funcs[s])
                        act.wait_ge(unit_out[par], hn + 1)
                        dst = proj[rel, :, :] if isinstance(rel, int) else \
                            proj[bass.ds(rel, 1), :, :].rearrange("a p n -> p (a n)")
                        act.dma_start(dst, stage[:, s, :]).then_inc(spilled[s], 16)
                if peel:
                    quad(0, 0)
                with act.Fori(int(peel), quads) as i:
                    quad(i, None)

            spill(N_QK, N_CONV // 4, [ACT.Copy] * 4, True)
            spill(N_QK + N_CONV, N_HG // 4, [ACT.Copy] * 3 + [ACT.Silu], False)
            spill(N_QK + N_CONV + N_HG, N_GATE // 4, [ACT.Sigmoid] * 4, False)
            act.wait_ge(skew_out, 16 * HEADS)
            for j in range(5):
                stat(("qk", j), [att[:, 3 + j, :]], (rstd_used, j) if j else None)
            for h in range(HG_HEADS):
                act.wait_ge(head_in, 16 * (CONV_T + h + 1))
                step(nc.scalar.activation(hE[:, 1, :], hq[:, 1, :], ACT.Abs))
                step(nc.scalar.activation(hE[:, 1, :], hE[:, 1, :], ACT.Exp, scale=-1.0))
                nc.scalar.activation(hE[:, 1, :], hE[:, 1, :], ACT.Ln, bias=1.0).then_inc(lsg, 1)
                wait_ready(act, ("iT", h))
                nc.scalar.copy(hiT[:, :, :].rearrange("p a b -> p (a b)"), mpair(("iT", h))[:, :]) \
                  .then_inc(F(("iT", h)), 1)
                act.wait_ge(hk_raw, h + 1)
                nc.scalar.activation(hk[:, :], hk[:, :], ACT.Exp, scale=-1.0).then_inc(hk_ok, 1)
                for lv in range(LEVELS):
                    act.wait_ge(expo, h * (LEVELS + 1) + lv + 1)
                    nc.scalar.activation(hE[:, lv % 2, :], hE[:, lv % 2, :], ACT.Exp).then_inc(decay, 1)
                nc.scalar.activation(hqG[:, :], hG[:, :], ACT.Exp).then_inc(decay, 1)
                act.wait_ge(expo, (h + 1) * (LEVELS + 1))
                nc.scalar.activation(hE[:, 1, :], hE[:, 1, :], ACT.Exp).then_inc(decay, 1)
                wait_ready(act, ("kT", h))
                nc.scalar.copy(hkT[:, :, :].rearrange("p a b -> p (a b)"), mpair(("kT", h))[:, :]) \
                  .then_inc(F(("kT", h)), 1)
                wait_ready(act, ("o", h))
                stat(("hg", h), [mpair(("o", h))[:, :]], (rstd_used, 5) if h == 0 else (y_made, CONV_T + h))

            def attention(st, heads, buf, i0):
                N = NB * heads
                for i in range(N + 1):
                    if i < N:
                        w = n_keys(st, i // heads)
                        act.wait_ge(nm_ok, i0 + i + 1)
                        if i >= 2:
                            act.wait_ge(pT_ps, i0 + i - 1)
                        nc.scalar.activation(buf["Pm"][:, i % 2, 0:w], buf["L"][:, i % 2, 0:w], ACT.Exp,
                                             bias=tiny[:, 12 + i % 4:13 + i % 4],
                                             accum_out=tiny[:, 16 + i % 4:17 + i % 4]).then_inc(p_ok, 1)
                    if i >= 1:
                        w = n_keys(st, (i - 1) // heads)
                        act.wait_ge(pT_ps, i0 + i)
                        if i >= 3:
                            act.wait_ge(pv_ok, i0 + i - 2)
                        nc.scalar.copy(buf["PT"][:, (i - 1) % 2, 0:w], pair[0][:, 0:w]).then_inc(pT_ok, 1)

            attention(0, HEADS, at1, 0)
            for b in (NB - 2, NB - 1):
                wait_done(act, ("yT", 0, b))
            base = NT
            his(base, [ysp[:, k, 0, :] for k in range(4)], [yT[:, k, :] for k in range(4)], None)
            for k in range(8):
                act.wait_ge(yin_in[k % 2], 16 * (k // 2 + 1))
                nc.scalar.copy(ysp[:, 4 + k, 0, :], sq[:, k % 2, :]).then_inc(hi_ok, 1)
            act.wait_ge(mixed_ok, NT)
            his(0, [actA[:, 0, j, :] for j in range(NT)], [mixed[:, j, :] for j in range(NT)],
                None)
            for par in range(2):
                act.wait_ge(unit_out[par], (FIRST["mlp"] + 1 - par) // 2)
            act.dma_start(poolw[:, :, :], t["pool_w"]).then_inc(poolw_in, 16)
            stat("x1", [xB[:, j, :] for j in range(NT)], (y_made, CONV_T + HG_HEADS))
            his(0, [actA[:, 0, j, :] for j in range(NT)], [tmpn[:, j % 2, :] for j in range(NT)], (nrm, NT + 1))
            for g in range(N_GROUP):
                n0 = FIRST["mlp"] + 16 * g

                def relu(n, par, hn, rel):
                    act.wait_ge(unit_mm, n + 1)
                    c = n - FIRST["mlp"] - 8 * g
                    if not isinstance(n, int) or c >= 2:
                        act.wait_ge(u_ok, c - 1)
                    nc.scalar.activation(mt[:, par, :], pair[par][:, :], ACT.Relu).then_inc(unit_out[par], 1)
                    act.wait_ge(unit_out[par], hn + 1)
                    nc.scalar.activation(mt[:, par, :], mt[:, par, :], ACT.Square).then_inc(relu_ok, 1)
                if g == 0:
                    act.wait_ge(lo_ok, 3 * NT + 12)
                    for n in range(n0, n0 + 8):
                        relu(n, n % 2, n // 2, n - n0)
                else:
                    units(act, n0, 8, 2, relu)
            base = 3 * NT + 12

            def high_x(n, par, hn, rel):
                act.wait_ge(unit_out[par], hn + 1)
                dst, src = tile(actA, rel, 0), tile(xB, rel)
                nc.scalar.copy(dst, src).then_inc(hi_ok, 1)
            units(act, FIRST["mlp"] + N_MLP - 8, 8, 2, high_x)
            act.dma_start(posqi[:, :], t["pos_q"]).then_inc(pos_in, 16)
            base += NT
            n = FIRST["in2"]
            outs = [(u2[:, g, :], ACT.Copy) for g in range(4)] + [(gb[:, g, :], ACT.Silu) for g in range(4)]
            outs += [(xq[:, g, :], ACT.Copy) for g in range(4)] + [(xkv[:, g, :], ACT.Copy) for g in range(2)]
            outs += [(u2[:, g, :], ACT.Silu) for g in range(4)] + [(kr[:, :], ACT.Copy)]
            for dst, func in outs:
                if n == FIRST["in2"] + 14:
                    for g in range(4):
                        wait_ready(act, ("pool", g))
                read_unit(n, n % 2, n // 2, dst, func)
                n += 1
            act.dma_start(posi[:, :], t["pos_row"].partition_broadcast(P)).then_inc(pos_in, 16)
            stat("xq", [xq[:, g, :] for g in range(4)], (lo_ok, 3 * NT + 12))
            his(0, [xqS[:, 0, g, :] for g in range(4)], [tmp2[:, g % 2, :] for g in range(4)], (nrm, 2 * NT + 1))
            stat("xkv", [xkv[:, g, :] for g in range(2)], (rstd_used, 6))
            his(0, [xkvS[:, 0, g, :] for g in range(2)], [tmp2[:, g % 2, :] for g in range(2)], (nrm, 2 * NT + 5))
            n = FIRST["uq"]
            act.wait_ge(lo_ok, base + 6)
            for dst in [xq[:, h, :] for h in range(4)] + [qr[:, r, :] for r in range(2)]:
                read_unit(n, n % 2, n // 2, dst, ACT.Copy)
                n += 1
            act.wait_ge(trig_in, 2)
            nc.scalar.activation(cs[:, 0, :], cs[:, 0, :], ACT.Sin).then_inc(trig, 1)
            nc.scalar.activation(cs[:, 1, :], cs[:, 1, :], ACT.Sin).then_inc(trig, 1)
            for dst in [kn[:, h, :] for h in range(4)] + [v4[:, h, :] for h in range(4)]:
                read_unit(n, n % 2, n // 2, dst, ACT.Copy)
                n += 1
            for h in range(MLA_HEADS):
                key = ("v2T", h)
                wait_ready(act, key)
                if h == 0:
                    act.wait_ge(roped, 3)
                nc.scalar.copy(V2[:, :, h * P:(h + 1) * P],
                               mpair(key)[:, :].rearrange("p (a b) -> p a b", b=P)).then_inc(F(key), 1)
            attention(1, MLA_HEADS, at2, NB * HEADS)
            for b in (NB - 2, NB - 1):
                wait_done(act, ("yT", 1, b))
            his(0, [actA[:, 0, j, :] for j in range(NT)],
                [u2[:, j, :] for j in range(4)] + [gb[:, j, :] for j in range(4)], None)
            stat("var", [xB[:, j, :] for j in range(NT)], (roped, 3), LNEPSV, (centred, 1))

        @block.vector
        def _(dve):
            steps = [0]

            def step(ins):
                steps[0] += 1
                ins.then_inc(dve_step, 1)
                dve.wait_ge(dve_step, steps[0])

            V = nc.vector

            def low(c, dst, src, hi):
                dve.wait_ge(hi_ok, c + 1)
                V.tensor_tensor(dst, src, hi.bitcast(F32), ALU.subtract).then_inc(lo_ok, 1)

            def norm_split(c0, q0, tiles, gains, tmp, dst):
                for k in range(len(tiles) + 1):
                    if k < len(tiles):
                        if k >= 2:
                            dve.wait_ge(lo_ok, c0 + k - 1)
                        V.scalar_tensor_tensor(tmp[:, k % 2, :], tiles[k], gains[k], rstd[:, :],
                                               ALU.mult, ALU.mult).then_inc(nrm, 1)
                    if k >= 1:
                        dve.wait_ge(nrm, q0 + k)
                        low(c0 + k - 1, dst[:, 1, k - 1, :], tmp[:, (k - 1) % 2, :], dst[:, 0, k - 1, :])

            dve.wait_ge(consts_in, 64)
            dve.wait_ge(x_in[0], 16 * NT)
            dve.wait_ge(rstd_ok, 1)
            norm_split(0, 0, [X0[:, j, :] for j in range(NT)], [SM("ln_mix", j) for j in range(NT)], tmpn, actA)
            wait_ready(dve, "iwT")
            V.tensor_scalar(iw[:, :, :], mpair("iwT")[:, :].rearrange("p (a b) -> p a b", b=P)[:, :, 64:68],
                            float(IDX_HEADS) ** -0.5 * float(HD) ** -0.5, None, ALU.mult).then_inc(F("iwT"), 1)
            wait_done(dve, "iwT")
            c = 0
            off = lambda b: P * b * (b + 1) // 2
            for b in range(2, NB):
                w = P * (b + 1)
                sc = pen[:, off(b):off(b) + w]
                for h in range(IDX_HEADS):
                    wait_done(dve, ("idx", b, h))
                    src = sq[:, c % 2, 0:w]
                    if h == 0:
                        V.tensor_scalar(sc, src, iw[:, b, h:h + 1], None, ALU.mult).then_inc(idx_used, 1)
                    else:
                        dve.wait_ge(idx_used, c)
                        V.scalar_tensor_tensor(sc, src, iw[:, b, h:h + 1], sc, ALU.mult, ALU.add) \
                         .then_inc(idx_used, 1)
                    c += 1
                dve.wait_ge(idx_used, c)
                step(V.tensor_tensor(sc[:, w - P:w], sc[:, w - P:w], C("causal"), ALU.add))
            V.tensor_copy(pen[:, 0:P], C("causal_neg")).then_inc(pen_ok, 1)
            V.memset(pen[:, P:2 * P], 0.0).then_inc(pen_ok, 1)
            V.tensor_copy(pen[:, 2 * P:3 * P], C("causal_neg")).then_inc(pen_ok, 1)
            rounds = TOPK // 8
            for b in range(2, NB):
                w = P * (b + 1)
                sc = pen[:, off(b):off(b) + w]
                done = (b - 2) * 2 * rounds
                for u in range(rounds):
                    V.max(top8[:, :], sc).then_inc(topk, 1)
                    dve.wait_ge(topk, done + 2 * u + 1)
                    V.match_replace(sc, top8[:, :], sc, PICKED).then_inc(topk, 1)
                    dve.wait_ge(topk, done + 2 * u + 2)
                V.tensor_scalar(sc, sc, 2 * FILL, NEG, ALU.is_gt, ALU.mult).then_inc(pen_ok, 1)
            for j in range(5):
                dve.wait_ge(rstd_ok, 2 + j)
                g = SM("q_norm") if j < 4 else SM("k_norm")
                if j == 0:
                    dve.wait_ge(unit_out[0], 5)
                V.scalar_tensor_tensor(att[:, 3 + j, :], att[:, 3 + j, :], g, rstd[:, :],
                                       ALU.mult, ALU.mult).then_inc(rstd_used, 1)
            for j in range(CONV_T):
                dve.wait_ge(head_in, 16 * (j + 1))
                step(V.tensor_tensor(hG[:, :], hq[:, 0, :], hq[:, 1, :], ALU.mult))
                step(V.tensor_scalar(hk[:, :], hG[:, :], SM("conv", 2 * 4 + j), None, ALU.mult))
                for d in (1, 2):
                    step(V.scalar_tensor_tensor(hk[:, d:S], hG[:, 0:S - d], SM("conv", (2 - d) * 4 + j),
                                                hk[:, d:S], ALU.mult, ALU.add))
                if j:
                    dve.wait_ge(y_out, 16 * j)
                V.tensor_tensor(hy[:, :], hk[:, :], hq[:, 2, :], ALU.mult).then_inc(y_made, 1)
            step(V.memset(hattn[:, :, :], 0.0))
            for h in range(HG_HEADS):
                e0 = h * (LEVELS + 1)

                def exponents(lv):
                    dst = hE[:, lv % 2, :]
                    if lv < LEVELS:
                        m = 64 >> lv
                        gv = hG[:, :].rearrange("p (n x m) -> p n x m", x=2, m=m)
                        dv = dst.rearrange("p (n x m) -> p n x m", x=2, m=m)
                        mid = gv[:, :, 0, m - 1:m].broadcast_to([P, S // (2 * m), m])
                        V.tensor_tensor(dv[:, :, 1, :], gv[:, :, 1, :], mid, ALU.subtract)
                        V.tensor_tensor(dv[:, :, 0, :], mid, gv[:, :, 0, :], ALU.subtract).then_inc(expo, 1)
                    else:
                        gv = hG[:, :].rearrange("p (n m) -> p n m", m=P)
                        V.tensor_tensor(dst.rearrange("p (n m) -> p n m", m=P),
                                        gv[:, :, P - 1:P].broadcast_to([P, NB, P]), gv,
                                        ALU.subtract).then_inc(expo, 1)

                def keep(lv):
                    key = ("lv", h, lv)
                    wait_ready(dve, key)
                    if lv:
                        wait_done(dve, ("lv", h, lv - 1))
                    V.copy_predicated(hattn[:, :, :],
                                      hmask[:, lv:lv + 1, :].broadcast_to([P, NB, P]),
                                      mpair(key)[:, :].rearrange("p (a b) -> p a b", b=P)).then_inc(F(key), 1)

                dve.wait_ge(lsg, h + 1)
                V.scalar_tensor_tensor(hk[:, :], hq[:, 1, :], 0.0, hE[:, 1, :], ALU.max, ALU.add) \
                 .then_inc(hk_raw, 1)
                step(V.scalar_tensor_tensor(hE[:, 0, :], hq[:, 1, :], 0.0, hE[:, 1, :],
                                            ALU.min, ALU.subtract))
                dve.wait_ge(hk_raw, h + 1)
                step(V.tensor_tensor_scan(hG[:, :], C("reset"), hE[:, 0, :], 0.0, ALU.mult, ALU.add))
                exponents(0)
                exponents(1)
                dve.wait_ge(hk_ok, h + 1)
                for lv in range(LEVELS):
                    dve.wait_ge(decay, h * (LEVELS + 2) + lv + 1)
                    if lv >= 2:
                        wait_ready(dve, ("lv", h, lv - 2))
                    m = 64 >> lv
                    v = lambda a: a.rearrange("p (n x m) -> p n x m", x=2, m=m)
                    wv, ev = v(hW[:, lv % 2, :]), v(hE[:, lv % 2, :])
                    V.tensor_tensor(wv[:, :, 1, :], v(hq[:, 0, :])[:, :, 1, :], ev[:, :, 1, :], ALU.mult)
                    V.tensor_tensor(wv[:, :, 0, :], v(hk[:, :])[:, :, 0, :], ev[:, :, 0, :],
                                    ALU.mult).then_inc(weighted, 1)
                    if lv + 2 <= LEVELS:
                        dve.wait_ge(weighted, e0 + lv + 1)
                        exponents(lv + 2)
                    if lv >= 1:
                        keep(lv - 1)
                dve.wait_ge(decay, h * (LEVELS + 2) + LEVELS + 1)
                step(V.tensor_copy(tiny[:, 0:8], hqG[:, P - 1:S:P]))
                V.tensor_tensor(hqG[:, :], hqG[:, :], hq[:, 0, :], ALU.mult).then_inc(hfin, 1)
                dve.wait_ge(decay, (h + 1) * (LEVELS + 2))
                wait_ready(dve, ("lv", h, LEVELS - 2))
                V.tensor_tensor(hW[:, 1, :], hk[:, :], hE[:, 1, :], ALU.mult).then_inc(weighted, 1)
                keep(LEVELS - 1)
                keep(LEVELS)
                wait_ready(dve, ("dS", h))
                dS = mpair(("dS", h))
                step(V.tensor_copy(hS[:, 1, :], dS[:, 0:P]))
                for c in range(1, NB - 1):
                    ins = V.scalar_tensor_tensor(hS[:, c + 1, :], hS[:, c, :], tiny[:, c:c + 1],
                                                 dS[:, c * P:(c + 1) * P], ALU.mult, ALU.add)
                    if c < NB - 2:
                        step(ins)
                    else:
                        ins.then_inc(F(("dS", h)), 1)
                wait_ready(dve, ("o", h))
                dve.wait_ge(squares, STAT_BASE[("hg", h)] + 1)
                dve.wait_ge(y_out, 16 * (CONV_T + h))
                V.scalar_tensor_tensor(hy[:, :], mpair(("o", h))[:, :], SM("hg_norm"), hq[:, 3, :],
                                       ALU.mult, ALU.mult).then_inc(F(("o", h)), 1)
                wait_done(dve, ("o", h))
                dve.wait_ge(rstd_ok, 7 + h)
                V.tensor_tensor(hy[:, :], hy[:, :], rstd[:, :], ALU.mult).then_inc(y_made, 1)

            def attention(st, heads, dv, scale, buf, i0, b0, mask, write):
                N = NB * heads
                for i in range(N + 4):
                    if i < N:
                        b, h = i // heads, i % heads
                        w, key = n_keys(st, b), ("qk", st, i)
                        m = mask(b, h)
                        wait_ready(dve, key)
                        if i >= 2:
                            dve.wait_ge(p_ok, i0 + i - 1)
                        V.tensor_tensor_reduce(buf["L"][:, i % 2, 0:w], mpair(key)[:, 0:w], m, scale, -3.0e38,
                                               ALU.add, ALU.max, tiny[:, 8 + i % 4:9 + i % 4]) \
                         .then_inc(F(key), 1)
                        wait_done(dve, key)
                        V.tensor_scalar(tiny[:, 12 + i % 4:13 + i % 4], tiny[:, 8 + i % 4:9 + i % 4], -1.0,
                                        None, ALU.mult).then_inc(nm_ok, 1)
                    if 2 <= i < N + 2:
                        j = i - 2
                        b, h = j // heads, j % heads
                        dve.wait_ge(p_ok, i0 + j + 1)
                        step(V.reciprocal(tiny[:, 20 + j % 4:21 + j % 4], tiny[:, 16 + j % 4:17 + j % 4]))
                        dve.wait_ge(pv_ok, i0 + j + 1)
                        if h == 0 and b >= 2:
                            wait_ready(dve, ("yT", st, b - 2))
                        a = (j % 2) * HALF
                        V.tensor_scalar(buf["O"][:, b % 2, h * dv:(h + 1) * dv], pair[1][:, a:a + dv],
                                        tiny[:, 20 + j % 4:21 + j % 4], None, ALU.mult).then_inc(o_ok, 1)
                    if i >= 4 and (i - 3) % heads == 0:
                        b = (i - 3) // heads - 1
                        key = ("yT", st, b)
                        wait_ready(dve, key)
                        src = mpair(key)[:, 0:HALF].rearrange("p (a b) -> p a b", b=P)
                        write(b, src).then_inc(F(key), 1)

            dve.wait_ge(pen_ok, 9)
            attention(0, HEADS, HD, float(HD) ** -0.5, at1, 0, 0,
                      lambda b, h: pen[:, off(b):off(b) + P * (b + 1)],
                      lambda b, src: V.tensor_copy(yT[:, :, b * P:(b + 1) * P], src))
            for b in (NB - 2, NB - 1):
                wait_done(dve, ("yT", 0, b))
            for k in range(12):
                low(NT + k, ysp[:, k, 1, :], yT[:, k, :] if k < 4 else sq[:, k % 2, :], ysp[:, k, 0, :])
            first = FIRST["up"]
            with dve.Fori(0, 4) as i:
                for jj in range(2):
                    mx = mixed[:, bass.ds(i * 2 + jj, 1), :].rearrange("p a n -> p (a n)")
                    for br in range(3):
                        n = first + 3 * jj + br
                        par, hn = n % 2, i * 3 + n // 2
                        dve.wait_ge(unit_mm, i * 6 + (n + 1))
                        if br == 0:
                            dve.wait_ge(gates_in[jj], i * 48 + 48)
                        dst = mx if br == 0 else prod[:, br - 1, :]
                        V.tensor_tensor(dst, pair[par][:, :], gates[:, jj, br, :], ALU.mult) \
                         .then_inc(unit_out[par], 1)
                        dve.wait_ge(unit_out[par], hn + 1)
                        if br == 1:
                            V.tensor_tensor(mx, mx, prod[:, 0, :], ALU.add).then_inc(swapped_in, 1)
                        if br == 2:
                            dve.wait_ge(swapped_in, i * 2 + (jj + 1))
                            V.tensor_tensor(mx, mx, prod[:, 1, :], ALU.add).then_inc(mixed_ok, 1)
            base = NT + 12
            dve.wait_ge(mixed_ok, NT)
            for j in range(NT):
                low(base + j, actA[:, 1, j, :], mixed[:, j, :], actA[:, 0, j, :])
            dve.wait_ge(x_in[1], 16 * NT)

            def add_x(n, par, hn, rel):
                dve.wait_ge(unit_mm, n + 1)
                x = tile(xB, rel)
                V.tensor_tensor(x, pair[par][:, :], x, ALU.add).then_inc(unit_out[par], 1)
            units(dve, FIRST["out"], N_OUT, 2, add_x)
            base += NT
            for par in range(2):
                dve.wait_ge(unit_out[par], (FIRST["mlp"] + 1 - par) // 2)
            dve.wait_ge(rstd_ok, 11)
            norm_split(base, NT, [xB[:, j, :] for j in range(NT)], [SM("ln_mlp", j) for j in range(NT)],
                       tmpn, actA)
            base += NT
            dve.wait_ge(lo_ok, base)
            for g in range(N_GROUP):
                n0 = FIRST["mlp"] + 16 * g
                if g:
                    dve.wait_ge(unit_mm, n0)

                def split_u(n, par, hn, rel):
                    c = n - (FIRST["mlp"] + 8 * g)
                    dve.wait_ge(relu_ok, c + 1)
                    V.tensor_copy(tile(uB, rel, 0), mt[:, par, :]).then_inc(hfin, 1)
                    dve.wait_ge(hfin, c + (HG_HEADS + 1))
                    V.tensor_tensor(tile(uB, rel, 1), mt[:, par, :], tile(uB, rel, 0).bitcast(F32),
                                    ALU.subtract).then_inc(u_ok, 1)
                units(dve, n0, 8, 2, split_u)
                if g < N_GROUP - 1:
                    units(dve, n0 + 8, 8, 2, add_x)
                else:
                    def add_split(n, par, hn, rel):
                        add_x(n, par, hn, rel)
                        c = rel + base
                        dve.wait_ge(hi_ok, c + 1)
                        V.tensor_tensor(tile(actA, rel, 1), tile(xB, rel), tile(actA, rel, 0).bitcast(F32),
                                        ALU.subtract).then_inc(lo_ok, 1)
                    units(dve, n0 + 8, 8, 2, add_split)
            base += NT
            for g, win in enumerate(POOL_WINDOWS):
                n = FIRST["in2"] + g
                dve.wait_ge(unit_out[n % 2], n // 2 + 1)
                if g:
                    dve.wait_ge(pooled_ok, g)
                src = u2[:, g, :]
                for d in range(g + 1):
                    sh = 1 << d
                    dst = sq[:, d % 2, :]
                    step(V.tensor_copy(dst[:, 0:sh], src[:, 0:sh]))
                    step(V.tensor_tensor(dst[:, sh:S], src[:, sh:S], src[:, 0:S - sh], ALU.add))
                    src = dst
                other = sq[:, (g + 1) % 2, 0:16]
                a = CST["pool"][0] + 16 * g
                step(V.tensor_tensor(other, src[:, 0:16], cst[:, a:a + 16], ALU.mult))
                step(V.scalar_tensor_tensor(u2[:, g, 16:S], src[:, 16:S], 1.0 / win, u2[:, g, 16:S],
                                            ALU.mult, ALU.subtract))
                V.tensor_tensor(u2[:, g, 0:16], other, u2[:, g, 0:16], ALU.subtract).then_inc(pooled_ok, 1)
            for g in range(4):
                key = ("pool", g)
                wait_ready(dve, key)
                n = FIRST["in2"] + 4 + g
                dve.wait_ge(unit_out[n % 2], n // 2 + 1)
                V.scalar_tensor_tensor(gb[:, g, :], mpair(key)[:, :], SM("pool_scale", g), gb[:, g, :],
                                       ALU.mult, ALU.mult).then_inc(F(key), 1)
            dve.wait_ge(rstd_ok, 12)
            norm_split(base, 2 * NT, [xq[:, g, :] for g in range(4)], [SM("q_norm_2", g) for g in range(4)],
                       tmp2, xqS)
            dve.wait_ge(pos_in, 32)
            V.tensor_copy(posqf[:, :], posqi[:, :]).then_inc(rstd_used, 1)
            dve.wait_ge(rstd_ok, 13)
            dve.wait_ge(lo_ok, base + 4)
            norm_split(base + 4, 2 * NT + 4, [xkv[:, g, :] for g in range(2)],
                       [SM("kv_norm_2", g) for g in range(2)], tmp2, xkvS)
            step(V.tensor_copy(posb[:, :], posi[:, :]))
            a0, a1 = ang[:, 0, :], ang[:, 1, :]
            c1 = 6.28125
            c2 = float(np.float32(np.round((TWO_PI - c1) * 2 ** 22) / 2 ** 22))
            c3 = TWO_PI - c1 - c2
            step(V.tensor_scalar(a0, posb[:, :], C("rope")[:, 0:1], None, ALU.mult))
            step(V.tensor_scalar(a1, a0, 1.0 / TWO_PI, MAGIC, ALU.mult, ALU.add))
            step(V.tensor_scalar(a1, a1, -MAGIC, None, ALU.add))
            for cc in (c1, c2, c3):
                step(V.scalar_tensor_tensor(a0, a1, -cc, a0, ALU.mult, ALU.add))
            dve.wait_ge(lo_ok, base + 6)
            LIM = 3.1415925
            V.tensor_scalar(cs[:, 1, :], a0, -LIM, LIM, ALU.max, ALU.min).then_inc(trig_in, 1)
            step(V.tensor_scalar(a0, a0, float(np.pi / 2), None, ALU.add))
            step(V.tensor_scalar(a1, a0, float(np.pi), -TWO_PI, ALU.is_gt, ALU.mult))
            step(V.tensor_tensor(a0, a0, a1, ALU.add))
            V.tensor_scalar(cs[:, 0, :], a0, -LIM, LIM, ALU.max, ALU.min).then_inc(trig_in, 1)
            dve.wait_ge(trig, 2)
            for r in range(3):
                key = ("swap", r)
                x = qr[:, r, :] if r < 2 else kr[:, :]
                wait_ready(dve, key)
                V.tensor_tensor(rtmp[:, :], mpair(key)[:, :], cs[:, 1, :], ALU.mult).then_inc(F(key), 1)
                wait_done(dve, key)
                step(V.tensor_tensor(x, x, cs[:, 0, :], ALU.mult))
                V.tensor_tensor(x, x, rtmp[:, :], ALU.add).then_inc(roped, 1)
                dve.wait_ge(roped, r + 1)

            made = [0]

            def mask2(b, h):
                if h == 0:
                    made[0] += 1
                    V.tensor_scalar(pen2[:, b % 2, :], posb[:, :], posqf[:, b:b + 1], NEG,
                                    ALU.is_gt, ALU.mult).then_inc(pen2_ok, 1)
                    dve.wait_ge(pen2_ok, made[0])
                return pen2[:, b % 2, :]

            def gated(b, src):
                y = u2[:, :, b * P:(b + 1) * P]
                return V.tensor_tensor(y, src, y, ALU.mult)

            attention(1, MLA_HEADS, P, float(192) ** -0.5, at2, NB * HEADS, NB, mask2, gated)
            base += 6
            for b in (NB - 2, NB - 1):
                wait_done(dve, ("yT", 1, b))
            for j in range(NT):
                src = u2[:, j, :] if j < 4 else gb[:, j - 4, :]
                low(base + j, actA[:, 1, j, :], src, actA[:, 0, j, :])

            def add_scaled(n, par, hn, rel):
                dve.wait_ge(unit_mm, n + 1)
                x = tile(xB, rel)
                V.scalar_tensor_tensor(x, x, float(2.0 ** 0.25), pair[par][:, :], ALU.mult, ALU.add) \
                 .then_inc(unit_out[par], 1)
            units(dve, FIRST["out2"], N_OUT2, 2, add_scaled)
            for par in range(2):
                dve.wait_ge(unit_out[par], (N_UNITS + 1 - par) // 2)
            wait_ready(dve, "mu")
            V.tensor_copy(mu[:, :], mpair("mu")[:, :]).then_inc(F("mu"), 1)
            wait_done(dve, "mu")
            for j in range(NT):
                ins = V.tensor_tensor(xB[:, j, :], xB[:, j, :], mu[:, :], ALU.subtract)
                ins.then_inc(centred, 1)
            dve.wait_ge(centred, NT)
            dve.wait_ge(rstd_ok, 14)
            for j in range(NT):
                step(V.scalar_tensor_tensor(xB[:, j, :], xB[:, j, :], SM("ln_g", j), rstd[:, :],
                                            ALU.mult, ALU.mult))
                if j >= 2:
                    dve.wait_ge(fin_out[j % 2], 16 * (j // 2))
                V.tensor_scalar(fin[:, j % 2, :], xB[:, j, :], SM("ln_b", j), None, ALU.add).then_inc(fin_ok, 1)


def n_keys(st, b):
    return P * (b + 1) if st == 0 else S


def stat_key(key):
    return ("stat",) + (key if isinstance(key, tuple) else (key,))


def tile(tensor, rel, part=None):
    if part is None:
        return tensor[:, rel, :] if isinstance(rel, int) else \
            tensor[:, bass.ds(rel, 1), :].rearrange("p a n -> p (a n)")
    return tensor[:, part, rel, :] if isinstance(rel, int) else \
        tensor[:, part, bass.ds(rel, 1), :].rearrange("p a n -> p (a n)")


def by_unit(w):
    k, n = w.shape
    return np.ascontiguousarray(w.reshape(k // P, P, n // P, P).transpose(2, 1, 0, 3)
                                .reshape(n // P, P, k))


def by_tile(v):
    return np.ascontiguousarray(v.reshape(-1, P).T)


def kernel(**inputs):
    import concourse.bacc as bacc
    from concourse.bass_utils import run_bass_kernel_spmd

    a = {k: np.asarray(v) for k, v in inputs.items()}
    w = a["w_in"][0]
    cut = np.cumsum([0, 512, 128, 128, 256, 64, 4, 512, 512, 512, 512, 512, 512, 512, 3072])
    aq, ak, av, iq, ik, iw, hq, hf, hi, hg, cb, cc, ch, gt = (w[:, cut[i]:cut[i + 1]] for i in range(14))
    pad = np.zeros((D, 60), np.float32)
    q_cols = [np.concatenate([aq[:, j * 64:(j + 1) * 64], aq[:, (j + 4) * 64:(j + 5) * 64]], 1) for j in range(4)]
    cols = [ik, iw, pad, iq] + q_cols + [ak, av]
    for j in range(4):
        s = slice(j * P, (j + 1) * P)
        cols += [cc[:, s], ch[:, s], cb[:, s]]
    for j in range(4):
        s = slice(j * P, (j + 1) * P)
        cols += [hq[:, s], hf[:, s], hi[:, s], hg[:, s]]
    cols += [gt]
    w_in = np.concatenate(cols, 1)
    ups = [by_unit(a[n][0]) for n in ("w_up_attn", "w_up_hgrn", "w_up_conv")]
    w_up = np.ascontiguousarray(np.stack(ups, 1).reshape(N_UP, P, HALF))
    up, down = by_unit(a["w_mlp_up"][0]), a["w_mlp_down"][0]
    mlp = []
    for g in range(N_GROUP):
        mlp += [up[8 * g:8 * g + 8], by_unit(down[D * g:D * (g + 1)])]
    w = a["w_in_2"]
    cut = np.cumsum([0, 512, 256, 64, 512, 512, 512])
    xq, xkv, kr, ga, up2, gb = (w[:, cut[i]:cut[i + 1]] for i in range(6))
    w_in2 = np.concatenate([up2, gb, xq, xkv, ga, kr, kr], 1)
    uq = a["w_uq_2"].reshape(512, MLA_HEADS, 192)
    uq = np.concatenate([uq[:, :, :P].reshape(512, -1), uq[:, :, P:].reshape(512, -1)], 1)
    ukv = a["w_ukv_2"].reshape(256, MLA_HEADS, 2 * P)
    ukv = np.concatenate([ukv[:, :, :P].reshape(256, -1), ukv[:, :, P:].reshape(256, -1)], 1)
    pos = a["positions_2"][0]
    small = [by_tile(a["ln_mix_g"][0]), by_tile(a["ln_mlp_g"][0]), by_tile(a["hgrn_norm_g"][0]),
             np.tile(a["q_norm_g"][0], 2)[:, None], np.tile(a["k_norm_g"][0], 2)[:, None],
             by_tile(a["conv_w"][0].reshape(-1)), by_tile(a["pool_scale_2"]), by_tile(a["q_norm_g_2"]),
             by_tile(a["kv_norm_g_2"]), by_tile(a["ln_g_2"][0]), by_tile(a["ln_b_2"][0])]
    cst, masks = shape_constants()
    arrays = {
        "xT": a["x"][0].T, "cst": cst, "masks": masks, "small": np.concatenate(small, 1),
        "rel_bias": a["rel_bias"], "w_in": by_unit(w_in), "w_up": w_up, "w_out": by_unit(a["w_out"][0]),
        "w_mlp": np.concatenate(mlp, 0), "w_in2": by_unit(w_in2), "w_uq": by_unit(uq), "w_ukv": by_unit(ukv),
        "w_out2": by_unit(a["w_out_2"]), "pool_w": a["pool_w_2"].transpose(1, 0, 2),
        "pos_row": pos[None, :], "pos_q": pos.reshape(NB, P).T,
    }
    arrays = {k: np.ascontiguousarray(v) for k, v in arrays.items()}
    nc = bacc.Bacc("TRN2", target_bir_lowering=False, num_devices=1)
    t = {k: nc.dram_tensor(k, v.shape, mybir.dt.from_np(v.dtype), kind="ExternalInput").ap()
         for k, v in arrays.items()}
    t["outT"] = nc.dram_tensor("outT", (D, S), F32, kind="ExternalOutput").ap()
    build(nc, t)
    r = run_bass_kernel_spmd(nc, [arrays], core_ids=[0])
    return np.ascontiguousarray(r.results[0]["outT"].T)[None]
```

```python
from contextlib import ExitStack

import numpy as np
import concourse.bass as bass
from concourse import mybir

F32 = mybir.dt.float32
F32R = mybir.dt.float32r
I32 = mybir.dt.int32
ACT = mybir.ActivationFunctionType
ALU = mybir.AluOpType
AX = mybir.AxisListType

P = 128
S = 1024
D = 1024
NT = D // P
NB = S // P
HALF = 512
EPS = 1e-6
LN_EPS = 1e-5

HEADS, HD, TOPK = 8, 64, 256
IDX_HEADS = 4
BUCKETS, MAX_DIST = 32, 128
HG_HEADS = 4
LEVELS = 7
CONV_T = 4
D_FF = 4096
MLA_HEADS = 4
POOL_WINDOWS = (2, 4, 8, 16)
ROPE_HALF = 32

NEG = -1.0e30
FILL = -1.0e38
PICKED = -3.0e38
TWO_PI = 2.0 * np.pi
MAGIC = 1.5 * 2.0 ** 23

N_QK, N_CONV, N_HG, N_GATE = 9, 12, 16, 24
N_IN = N_QK + N_CONV + N_HG + N_GATE
N_UP = 24
N_OUT = 8
N_GROUP = 4
N_MLP = 16 * N_GROUP
N_IN2 = 19
N_UQ = 6
N_UKV = 8
N_OUT2 = 8
FIRST = {}
_n = 0
for _name, _count in (("in", N_IN), ("up", N_UP), ("out", N_OUT), ("mlp", N_MLP), ("in2", N_IN2),
                      ("uq", N_UQ), ("ukv", N_UKV), ("out2", N_OUT2)):
    FIRST[_name] = _n
    _n += _count
N_UNITS = _n

CST = {}
_c = 0
for _name, _w in (("ident", P), ("mean64", P), ("mean128", P), ("mean256", P), ("mean512", P),
                  ("mean1024", P), ("causal", P), ("causal_neg", P), ("reset", S), ("bucket", 384),
                  ("pool", 4 * 16), ("rope", 8), ("swap", P)):
    CST[_name] = (_c, _w)
    _c += _w
N_CST = _c


def shape_constants():
    c = np.zeros((P, N_CST), np.float32)

    def put(name, value):
        a, w = CST[name]
        c[:value.shape[0], a:a + w] = value

    i = np.arange(P)
    put("ident", np.eye(P, dtype=np.float32))
    put("mean64", ((i[:, None] // 64) == (i[None, :] // 64)) / np.float32(64))
    for n in (128, 256, 512, 1024):
        put(f"mean{n}", np.full((P, P), 1.0 / n, np.float32))
    put("causal", np.where(i[None, :] > i[:, None], FILL, 0.0).astype(np.float32))
    put("causal_neg", np.where(i[None, :] > i[:, None], NEG, 0.0).astype(np.float32))
    put("reset", np.broadcast_to((np.arange(S) % P != 0).astype(np.float32), (P, S)))
    j = np.arange(384)
    d = np.maximum(255 - j, 0)
    half = BUCKETS // 2
    far = half + (np.log(np.maximum(d, 1).astype(np.float32) / np.float32(half))
                  / np.float32(np.log(MAX_DIST / half)) * np.float32(BUCKETS - half)).astype(np.int32)
    b = np.where(d < half, d, np.minimum(far, BUCKETS - 1))
    hot = np.zeros((BUCKETS, 384), np.float32)
    hot[b, j] += 1.0
    hot[BUCKETS - 1, :] -= 1.0
    put("bucket", hot)
    pool = np.zeros((P, 4, 16), np.float32)
    for g, w in enumerate(POOL_WINDOWS):
        pool[:, g, :] = 1.0 / np.minimum(np.arange(16) + 1, w)
    put("pool", pool.reshape(P, 64))
    rope = np.zeros((P, 8), np.float32)
    rope[:, 0] = (np.float32(10000.0) ** (-(i % ROPE_HALF).astype(np.float32) / ROPE_HALF))
    rope[:, 1] = EPS
    rope[:, 2] = LN_EPS
    put("rope", rope)
    swap = np.zeros((P, P), np.float32)
    for o in range(P):
        swap[o ^ ROPE_HALF, o] = 1.0 if o & ROPE_HALF else -1.0
    put("swap", swap)
    masks = np.zeros((P, LEVELS + 1, P), np.int32)
    for lv in range(LEVELS):
        m = 64 >> lv
        same = (i[:, None] // (2 * m)) == (i[None, :] // (2 * m))
        masks[:, lv, :] = same & ((i[:, None] // m) % 2 == 0) & ((i[None, :] // m) % 2 == 1)
    masks[:, LEVELS, :] = np.eye(P, dtype=np.int32)
    return c, masks.reshape(P, -1)


SMALL = {}
_c = 0
for _name, _w in (("ln_mix", 8), ("ln_mlp", 8), ("hg_norm", 1), ("q_norm", 1), ("k_norm", 1), ("conv", 12),
                  ("pool_scale", 4), ("q_norm_2", 4), ("kv_norm_2", 2), ("ln_g", 8), ("ln_b", 8)):
    SMALL[_name] = (_c, _w)
    _c += _w
N_SMALL = _c



def attention_uses(st, heads):
    uses, n = [("qk", st, 0)], NB * heads
    for i in range(n + 3):
        uses += [("qk", st, i + 1)] * (i + 1 < n)
        uses += [("yT", st, (i - 2) // heads - 1)] * (i >= 3 and (i - 2) % heads == 0)
    return uses


def gate_phase():
    order = [("G",)] + [("stat", "qk", j) for j in range(5)] + [("G",)] * 6 + [("iT", 0)]
    for h in range(HG_HEADS):
        order += [("lv", h, 0), ("lv", h, 1), ("G",), ("lv", h, 2), ("lv", h, 3), ("G",)]
        order += [("lv", h, 4), ("lv", h, 5), ("G",), ("lv", h, 6), ("lv", h, 7), ("kT", h), ("G",)]
        order += [("dS", h), ("o", h)] + [("iT", h + 1)] * (h + 1 < HG_HEADS) + [("stat", "hg", h)]
    order += [("G",)]
    assert order.count(("G",)) == N_GATE
    return order


GATE_PHASE = gate_phase()


def misc_plan():
    uses = [("stat", "x"), "iwT"]
    uses += [("idx", b, h) for b in range(2, NB) for h in range(IDX_HEADS)]
    uses += ["vT"] + [("bias", h) for h in range(HEADS)]
    uses += [key for key in GATE_PHASE if key[0] != "G"]
    uses += attention_uses(0, HEADS)
    uses += ["ss1"]
    uses += [("pool", g) for g in range(4)]
    uses += [("stat", "xq"), ("stat", "xkv"), ("swap", 0), ("swap", 1), ("swap", 2)]
    uses += [("v2T", h) for h in range(MLA_HEADS)]
    uses += attention_uses(1, MLA_HEADS)
    uses += ["mu", ("stat", "var")]
    plan, ready, free = {}, [0, 0], [0, 0]
    for m, key in enumerate(uses):
        s = m % 2
        ready[s] += not (isinstance(key, tuple) and key[0] == "stat")
        plan[key] = (s, ready[s], free[s])
        free[s] += 1
    return plan


STATS = [("x", NT)] + [(("qk", j), 1) for j in range(5)] + [(("hg", h), 1) for h in range(HG_HEADS)]
STATS += [("xq", 4), ("xkv", 2), ("var", NT)]
STAT_BASE, STAT_NO = {}, {}
_c = 0
for _i, (_k, _w) in enumerate(STATS):
    STAT_BASE[_k], STAT_NO[_k] = _c, _i
    _c += _w


def build(nc, t):
    with ExitStack() as ctx:
        BASE = 16512
        MISC = misc_plan()

        def sem(name):
            return ctx.enter_context(nc.semaphore(name))

        def at(name, kb, shape, dt=F32):
            return nc.alloc_sbuf_tensor_at(name, shape, dt, offset=BASE + int(kb * 1024))

        raw = at("raw", 0, [P, 2, 1024])
        w_hi = at("w_hi", 8, [P, 2, 1024], F32R)
        w_lo = at("w_lo", 16, [P, 2, 1024], F32R)
        actA = at("actA", 24, [P, 2, NT, S], F32R)
        X0 = at("X0", 88, [P, NT, S])
        att = at("att", 88, [P, N_QK, S])
        pen = at("pen", 124, [P, 4608])
        toep = at("toep", 142, [P, HEADS, 256])
        V1 = at("V1", 152, [P, NB, P])
        ik_up = at("ik_up", 154, [P, S])
        stage = at("stage", 158, [P, 4, S])
        sq = at("sq", 176, [P, 2, S])
        cst = at("cst", 184, [P, N_CST])
        small = at("small", 194.5, [P, N_SMALL])
        iw = at("iw", 195, [P, NB, IDX_HEADS])
        tiny = at("tiny", 195.125, [P, 32])
        top8 = at("top8", 195.25, [P, 8])
        rb = at("rb", 195.3125, [BUCKETS, HEADS])
        hmask = at("hmask", 195.5, [P, LEVELS + 1, P], I32)
        rstd = at("rstd", 199.5, [P, S])
        assert 184 * 1024 + N_CST * 4 <= 194.5 * 1024 and N_SMALL * 4 <= 512
        hq = at("hq", 88, [P, 4, S])
        hG = at("hG", 104, [P, S])
        hk = at("hk", 108, [P, S])
        hE = at("hE", 112, [P, 2, S])
        hW = at("hW", 120, [P, 2, S])
        hattn = at("hattn", 128, [P, NB, P])
        hiT = at("hiT", 132, [P, NB, P])
        hkT = at("hkT", 136, [P, NB, P])
        hS = at("hS", 140, [P, NB, P])
        hqG = at("hqG", 144, [P, S])
        hy = at("hy", 148, [P, S])
        cin = at("cin", 88, [P, 3 * CONV_T, S])
        cu = at("cu", 136, [P, S])
        cy = at("cy", 140, [P, 2, S])
        at1 = dict(L=at("a_L", 24, [P, 2, S]), Pm=at("a_P", 32, [P, 2, S]), PT=at("a_PT", 40, [P, 2, S]),
                   O=at("a_O", 48, [P, 2, HALF]))
        yT = at("yT", 158, [P, 4, S])
        ysp = at("ysp", 24, [P, 12, 2, S], F32R)
        gates = at("gates", 120, [P, 2, 3, S])
        prod = at("prod", 144, [P, 2, S])
        mixed = at("mixed", 152, [P, NT, S])
        xB = at("xB", 88, [P, NT, S])
        tmpn = at("tmpn", 158, [P, 2, S])
        uB = at("uB", 120, [P, 2, NT, S], F32R)
        mt = at("mt", 199.5, [P, 2, S])
        u2 = at("u2", 120, [P, 4, S])
        gb = at("gb", 136, [P, 4, S])
        xq = at("xq", 152, [P, 4, S])
        xkv = at("xkv", 168, [P, 2, S])
        poolw = at("poolw", 195.5, [P, 4, P])
        kr = at("kr", 195.5, [P, S])
        posb = at("posb", 203.5, [P, S])
        posi = at("posi", 203.5, [P, S], I32)
        xqS = at("xqS", 24, [P, 2, 4, S], F32R)
        xkvS = at("xkvS", 56, [P, 2, 2, S], F32R)
        tmp2 = at("tmp2", 72, [P, 2, S])
        kn = at("kn", 72, [P, 4, S])
        v4 = at("v4", 24, [P, 4, S])
        V2 = at("V2", 40, [P, NB, HALF])
        qr = at("qr", 176, [P, 2, S])
        cs = at("cs", 168, [P, 2, S])
        pen2 = at("pen2", 168, [P, 2, S])
        ang = at("ang", 80, [P, 2, S])
        at2 = dict(L=at("b_L", 56, [P, 2, S]), Pm=at("b_P", 64, [P, 2, S]), PT=at("b_PT", 24, [P, 2, S]),
                   O=at("b_O", 32, [P, 2, HALF]))
        fin = at("fin", 24, [P, 2, S])
        rtmp = at("rtmp", 40, [P, S])
        mu = at("mu", 120, [P, S])
        pad = at("pad", 195.46875, [P, 2])
        posqi = at("posqi", 195.375, [P, NB], I32)
        posqf = at("posqf", 195.4375, [P, NB])
        pair = [ctx.enter_context(nc.psum_tensor(f"pair{i}", [P, 2 * HALF], F32)) for i in range(4)]

        proj = nc.dram_tensor("proj", (N_CONV + N_HG + N_GATE, P, S), F32, kind="Internal").ap()
        ydram = nc.dram_tensor("ydram", (8, P, S), F32, kind="Internal").ap()
        att_dram = nc.dram_tensor("att_dram", (P, 5 * S), F32, kind="Internal").ap()
        pen_dram = nc.dram_tensor("pen_dram", (P, 4608), F32, kind="Internal").ap()
        skew = nc.dram_tensor("skew", (HEADS, P, 384), F32, kind="Internal")

        consts_in = sem("consts_in")
        x_in = [sem(f"x_in{i}") for i in range(2)]
        w_in = [sem("w_in0"), sem("w_in1")]
        w_split = sem("w_split")
        w_hi_ok = sem("w_hi_ok")
        unit_mm = sem("unit_mm")
        unit_out = [sem("unit_out0"), sem("unit_out1")]
        ready = [sem("ready0"), sem("ready1")]
        free = [sem("free0"), sem("free1")]
        spilled = [sem(f"spilled{i}") for i in range(4)]
        squares = sem("squares")
        squares_used = sem("squares_used")
        rstd_ok = sem("rstd_ok")
        rstd_used = sem("rstd_used")
        dve_step = sem("dve_step")
        act_step = sem("act_step")
        pool_step = sem("pool_step")
        nrm = sem("nrm")
        hi_ok = sem("hi_ok")
        lo_ok = sem("lo_ok")
        ik_copied = sem("ik_copied")
        idx_used = sem("idx_used")
        topk = sem("topk")
        pen_ok = sem("pen_ok")
        skew_out = sem("skew_out")
        toep_in = sem("toep_in")
        parked = sem("parked")
        att_in = sem("att_in")
        pen_in = sem("pen_in")
        gate_ok = sem("gate_ok")
        ss_sq = sem("ss_sq")
        ss_sum = sem("ss_sum")
        mu_sum = sem("mu_sum")
        mix_step = sem("mix_step")
        conv_in = [sem(f"conv_in{i}") for i in range(CONV_T)]
        zi_in = sem("zi_in")
        q_in = sem("q_in")
        g_in = sem("g_in")
        y_out = [sem("y_out0"), sem("y_out1")]
        y_made = sem("y_made")
        lsg = sem("lsg")
        hk_raw = sem("hk_raw")
        hk_ok = sem("hk_ok")
        expo = sem("expo")
        decay = sem("decay")
        weighted = sem("weighted")
        hfin = sem("hfin")
        l_ok = sem("l_ok")
        nm_ok = sem("nm_ok")
        p_ok = sem("p_ok")
        pT_ps = sem("pT_ps")
        pT_ok = sem("pT_ok")
        pv_ok = sem("pv_ok")
        o_ok = sem("o_ok")
        yin_in = [sem("yin_in0"), sem("yin_in1")]
        gates_in = [sem("gates_in0"), sem("gates_in1")]
        mixed_ok = sem("mixed_ok")
        relu_ok = sem("relu_ok")
        u_ok = sem("u_ok")
        pooled_ok = sem("pooled_ok")
        poolw_in = sem("poolw_in")
        pos_in = sem("pos_in")
        trig = sem("trig")
        trig_in = sem("trig_in")
        roped = sem("roped")
        pen2_ok = sem("pen2_ok")
        centred = sem("centred")
        fin_ok = sem("fin_ok")
        fin_out = [sem("fin_out0"), sem("fin_out1")]

        def C(name, rows=P):
            a, w = CST[name]
            return cst[0:rows, a:a + w]

        def SM(name, j=0):
            a = SMALL[name][0]
            return small[:, a + j:a + j + 1]

        EPSV = C("rope")[:, 1:2]
        LNEPSV = C("rope")[:, 2:3]

        def mpair(key):
            return pair[2 + MISC[key][0]]

        def wait_ready(eng, key):
            s, r, _ = MISC[key]
            eng.wait_ge(ready[s], r)

        def wait_done(eng, key):
            s, _, f = MISC[key]
            eng.wait_ge(free[s], f + 1)

        def wait_room(pe, key):
            s, _, f = MISC[key]
            if f > 0:
                pe.wait_ge(free[s], f)

        def R(key):
            return ready[MISC[key][0]]

        def F(key):
            return free[MISC[key][0]]

        def units(eng, first, count, width, body):
            k = count % width
            for n in range(first, first + k):
                body(n, n % 2, n // 2, n - first)
            start = first + k
            with eng.Fori(0, (count - k) // width) as i:
                for u in range(width):
                    n = start + u
                    if width % 2 == 0:
                        body(i * width + n, n % 2, i * (width // 2) + n // 2, i * width + (k + u))

        block = ctx.enter_context(nc.Block())

        @block.sync
        def _(sp):
            def load_units(name, first, count, kt):
                src = t[name]

                def body(n, par, hn, rel):
                    if isinstance(n, int) and n < 2:
                        pass
                    else:
                        sp.wait_ge(w_split, n - 1)
                    row = src[rel, :, :] if isinstance(rel, int) else \
                        src[bass.ds(rel, 1), :, :].rearrange("a p n -> p (a n)")
                    sp.dma_start(raw[:, par, 0:kt * P], row).then_inc(w_in[par], 16)
                units(sp, first, count, 2, body)

            sp.dma_start(cst[:, :], t["cst"]).then_inc(consts_in, 16)
            sp.dma_start(small[:, :], t["small"]).then_inc(consts_in, 16)
            sp.dma_start(rb[:, :], t["rel_bias"]).then_inc(consts_in, 16)
            sp.dma_start(hmask[:, :, :].rearrange("p a b -> p (a b)"), t["masks"]).then_inc(consts_in, 16)
            for j in range(NT):
                sp.dma_start(X0[:, j, :], t["xT"][j * P:(j + 1) * P, :]).then_inc(x_in[0], 16)
            load_units("w_in", 0, N_IN, 8)
            sp.wait_ge(skew_out, 16 * HEADS)
            sp.wait_ge(y_made, CONV_T + HG_HEADS)
            for par in range(2):
                sp.wait_ge(y_out[par], 16 * ((CONV_T + HG_HEADS) // 2))
            sp.dma_start(att[:, 3:8, :].rearrange("p a b -> p (a b)"), att_dram).then_inc(att_in, 16)
            sp.dma_start(pen[:, :], pen_dram).then_inc(pen_in, 16)
            for h in range(HEADS):
                src = bass.AP(skew, h * P * 384 + 127, [[383, P], [1, 256]])
                sp.dma_start(toep[:, h, :], src).then_inc(toep_in, 16)
            for k in range(8):
                if k >= 2:
                    sp.wait_ge(lo_ok, NT + 4 + k - 1)
                sp.dma_start(sq[:, k % 2, :], ydram[k]).then_inc(yin_in[k % 2], 16)
            load_units("w_up", FIRST["up"], N_UP, 4)
            sp.wait_ge(mixed_ok, NT)
            for j in range(NT):
                sp.dma_start(xB[:, j, :], t["xT"][j * P:(j + 1) * P, :]).then_inc(x_in[1], 16)
            load_units("w_out", FIRST["out"], N_OUT, 8)
            load_units("w_mlp", FIRST["mlp"], N_MLP, 8)
            load_units("w_in2", FIRST["in2"], N_IN2, 8)
            load_units("w_uq", FIRST["uq"], N_UQ, 4)
            load_units("w_ukv", FIRST["ukv"], N_UKV, 2)
            load_units("w_out2", FIRST["out2"], N_OUT2, 8)
            for k in range(NT):
                sp.wait_ge(fin_ok, k + 1)
                sp.dma_start(t["outT"][k * P:(k + 1) * P, :], fin[:, k % 2, :]).then_inc(fin_out[k % 2], 16)
            for k in range(2):
                sp.wait_ge(fin_out[k], 16 * (NT // 2))

        @block.gpsimd
        def _(pool):
            def split_units(first, count, kt):
                def body(n, par, hn, rel):
                    pool.wait_ge(w_in[par], (hn + 1) * 16)
                    if not isinstance(n, int) or n >= 2:
                        pool.wait_ge(unit_mm, n - 1)
                    nc.gpsimd.tensor_tensor(pad[:, 0:1], pad[:, 1:2], pad[:, 1:2], ALU.add)
                    w = kt * P
                    nc.gpsimd.tensor_copy(w_hi[:, par, 0:w], raw[:, par, 0:w]).then_inc(w_hi_ok, 1)
                    pool.wait_ge(w_hi_ok, n + 1)
                    nc.gpsimd.tensor_tensor(w_lo[:, par, 0:w], raw[:, par, 0:w],
                                            w_hi[:, par, 0:w].bitcast(F32), ALU.subtract).then_inc(w_split, 1)
                units(pool, first, count, 2, body)

            nc.gpsimd.memset(pad[:, :], 0.0).then_inc(pool_step, 1)
            pool.wait_ge(pool_step, 1)
            split_units(0, N_IN, 8)
            split_units(FIRST["up"], N_UP, 4)
            split_units(FIRST["out"], N_OUT + N_MLP + N_IN2, 8)
            split_units(FIRST["uq"], N_UQ, 4)
            split_units(FIRST["ukv"], N_UKV, 2)
            split_units(FIRST["out2"], N_OUT2, 8)

        @block.tensor
        def _(pe):
            def product(n, par, hn, kt, hi, lo):
                pe.wait_ge(w_split, n + 1)
                if not isinstance(n, int) or n >= 2:
                    pe.wait_ge(unit_out[par], hn)
                last = None
                for half in range(2):
                    cols = slice(half * HALF, (half + 1) * HALF)
                    for k in range(kt):
                        wk = slice(k * P, (k + 1) * P)
                        for i, (w, x) in enumerate(((w_hi, hi(k)), (w_hi, lo(k)), (w_lo, hi(k)))):
                            last = nc.tensor.matmul(pair[par][:, cols], w[:, par, wk], x[:, cols],
                                                    start=(k == 0 and i == 0), stop=(k == kt - 1 and i == 2))
                last.then_inc(unit_mm, 1)

            def product_first(n, kt, hi, lo, ok, base):
                par = n % 2
                pe.wait_ge(w_split, n + 1)
                if n >= 2:
                    pe.wait_ge(unit_out[par], n // 2)
                last = None
                for k in range(kt):
                    pe.wait_ge(ok, base + k + 1)
                    wk = slice(k * P, (k + 1) * P)
                    for half in range(2):
                        cols = slice(half * HALF, (half + 1) * HALF)
                        for i, (w, x) in enumerate(((w_hi, hi(k)), (w_hi, lo(k)), (w_lo, hi(k)))):
                            last = nc.tensor.matmul(pair[par][:, cols], w[:, par, wk], x[:, cols],
                                                    start=(k == 0 and i == 0), stop=(k == kt - 1 and i == 2))
                last.then_inc(unit_mm, 1)

            def products(first, count, kt, hi, lo, width=2):
                units(pe, first, count, width, lambda n, par, hn, rel: product(n, par, hn, kt, hi, lo))

            def stat(key, name, srcs_n):
                base = STAT_BASE[key]
                wait_room(pe, stat_key(key))
                for k in range(srcs_n):
                    c = base + k
                    pe.wait_ge(squares, c + 1)
                    for half in range(2):
                        cols = slice(half * HALF, (half + 1) * HALF)
                        mm = nc.tensor.matmul(mpair(stat_key(key))[:, cols], C(name), sq[:, c % 2, cols],
                                              start=(k == 0), stop=(k == srcs_n - 1))
                    mm.then_inc(squares_used, 1)

            def transposes(key, src, count):
                wait_room(pe, key)
                for c in range(count):
                    mm = nc.tensor.transpose(mpair(key)[:, c * P:(c + 1) * P], src(c), C("ident"))
                mm.then_inc(R(key), 1)

            hA = lambda k: actA[:, 0, k, :]
            lA = lambda k: actA[:, 1, k, :]
            pe.wait_ge(consts_in, 64)
            stat("x", "mean1024", NT)
            product_first(0, 8, hA, lA, lo_ok, 0)
            for n in range(1, 3):
                product(n, n % 2, n // 2, 8, hA, lA)
            pe.wait_ge(unit_out[0], 2)
            pe.wait_ge(unit_out[1], 1)
            transposes("iwT", lambda c: att[:, 0, c * P:(c + 1) * P], NB)
            pe.wait_ge(ik_copied, 16)
            for b in range(2, NB):
                for h in range(IDX_HEADS):
                    key = ("idx", b, h)
                    wait_room(pe, key)
                    lo_p = (h % 2) * 64
                    ks = att[0:64, 0, :] if h % 2 == 0 else ik_up[64:128, :]
                    for c0 in range(0, P * (b + 1), HALF):
                        c1 = min(c0 + HALF, P * (b + 1))
                        mm = nc.tensor.matmul(mpair(key)[:, c0:c1],
                                              att[lo_p:lo_p + 64, 1 + h // 2, b * P:(b + 1) * P],
                                              ks[:, c0:c1], start=True, stop=True)
                    mm.then_inc(R(key), 1)
            for n in range(3, N_QK):
                product(n, n % 2, n // 2, 8, hA, lA)
            pe.wait_ge(unit_out[0], 5)
            transposes("vT", lambda c: att[:, 8, c * P:(c + 1) * P], NB)
            for h in range(HEADS):
                key = ("bias", h)
                wait_room(pe, key)
                nc.tensor.matmul(mpair(key)[:, 0:384], rb[:, h:h + 1].broadcast_to([BUCKETS, P]),
                                 C("bucket", BUCKETS), start=True, stop=True).then_inc(R(key), 1)
            products(N_QK, N_CONV + N_HG, 8, hA, lA, 4)
            n = N_IN - N_GATE
            for key in GATE_PHASE:
                h = key[1] if len(key) > 1 else None
                if key[0] == "G":
                    product(n, n % 2, n // 2, 8, hA, lA)
                    n += 1
                elif key[:2] == ("stat", "qk"):
                    stat(("qk", key[2]), "mean64", 1)
                elif key[0] == "stat":
                    stat(("hg", key[2]), "mean128", 1)
                elif key[0] == "iT":
                    pe.wait_ge(zi_in, 16 * (h + 1))
                    transposes(key, lambda c: hq[:, 2, c * P:(c + 1) * P], NB)
                elif key[0] == "lv":
                    lv = key[2]
                    if lv < LEVELS:
                        pe.wait_ge(weighted, h * (LEVELS + 1) + lv + 1)
                        ks, qs = hW[:, lv % 2, :], hW[:, lv % 2, :]
                    else:
                        pe.wait_ge(hk_ok, h + 1)
                        ks, qs = hk[:, :], hq[:, 0, :]
                    wait_room(pe, key)
                    for c in range(NB):
                        cc = slice(c * P, (c + 1) * P)
                        mm = nc.tensor.matmul(mpair(key)[:, cc], ks[:, cc], qs[:, cc], start=True, stop=True)
                    mm.then_inc(R(key), 1)
                elif key[0] == "kT":
                    pe.wait_ge(weighted, (h + 1) * (LEVELS + 1))
                    transposes(key, lambda c: hW[:, 1, c * P:(c + 1) * P], NB)
                elif key[0] == "dS":
                    wait_done(pe, ("kT", h))
                    wait_done(pe, ("iT", h))
                    wait_room(pe, key)
                    for c in range(NB - 1):
                        mm = nc.tensor.matmul(mpair(key)[:, c * P:(c + 1) * P], hkT[:, c, :], hiT[:, c, :],
                                              start=True, stop=True)
                    mm.then_inc(R(key), 1)
                elif key[0] == "o":
                    wait_done(pe, ("dS", h))
                    wait_done(pe, ("lv", h, LEVELS))
                    wait_done(pe, ("lv", h, LEVELS - 1))
                    pe.wait_ge(hfin, h + 1)
                    wait_room(pe, key)
                    for c in range(NB):
                        out = mpair(key)[:, c * P:(c + 1) * P]
                        mm = nc.tensor.matmul(out, hiT[:, c, :], hattn[:, c, :], start=True, stop=(c == 0))
                        if c:
                            mm = nc.tensor.matmul(out, hS[:, c, :], hqG[:, c * P:(c + 1) * P],
                                                  start=False, stop=True)
                    mm.then_inc(R(key), 1)

            def attention(st, heads, dv, buf, logits, values, i0, b0):
                N = NB * heads

                def qk(i):
                    key = ("qk", st, i)
                    wait_room(pe, key)
                    logits(i // heads, i % heads, mpair(key)).then_inc(R(key), 1)

                def turn(i):
                    pe.wait_ge(p_ok, i0 + i + 1)
                    if i0 + i > 0:
                        pe.wait_ge(pT_ok, i0 + i)
                    for kb in range(n_keys(st, i // heads) // P):
                        mm = nc.tensor.transpose(pair[0][:, kb * P:(kb + 1) * P],
                                                 buf["Pm"][:, i % 2, kb * P:(kb + 1) * P], C("ident"))
                    mm.then_inc(pT_ps, 1)

                def pv(i):
                    b, h = i // heads, i % heads
                    pe.wait_ge(pT_ok, i0 + i + 1)
                    if i0 + i >= 2:
                        pe.wait_ge(o_ok, i0 + i - 1)
                    nk = n_keys(st, b) // P
                    for kb in range(nk):
                        a = (i % 2) * HALF
                        mm = nc.tensor.matmul(pair[1][:, a:a + dv], buf["PT"][:, i % 2, kb * P:(kb + 1) * P],
                                              values(kb, h), start=(kb == 0), stop=(kb == nk - 1))
                    mm.then_inc(pv_ok, 1)

                def turn_out(b):
                    pe.wait_ge(o_ok, i0 + (b + 1) * heads)
                    transposes(("yT", st, b), lambda c: buf["O"][:, b % 2, c * P:(c + 1) * P], 4)

                qk(0)
                for i in range(N + 3):
                    if i + 1 < N:
                        qk(i + 1)
                    if i < N:
                        turn(i)
                    if 1 <= i <= N:
                        pv(i - 1)
                    if 3 <= i and (i - 2) % heads == 0:
                        turn_out((i - 2) // heads - 1)

            def logits1(b, h, out):
                n, lo_p = P * (b + 1), (h // 4) * 64
                w = min(n, 2 * P)
                for c0 in range(0, n, HALF):
                    c1 = min(c0 + HALF, n)
                    near = max(c0, n - w)
                    mm = nc.tensor.matmul(out[:, c0:c1], att[lo_p:lo_p + 64, 3 + h % 4, b * P:(b + 1) * P],
                                          att[lo_p:lo_p + 64, 7, c0:c1], start=True, stop=(near >= c1))
                    if near < c1:
                        a = near - n + 2 * P
                        mm = nc.tensor.matmul(out[:, near:c1], C("ident"), toep[:, h, a:a + c1 - near],
                                              start=False, stop=True)
                return mm

            pe.wait_ge(att_in, 16)
            pe.wait_ge(toep_in, 16 * HEADS)
            wait_done(pe, "vT")
            pe.wait_ge(unit_out[0], (N_IN + 1) // 2)
            pe.wait_ge(unit_out[1], N_IN // 2)
            attention(0, HEADS, HD, at1, logits1, lambda kb, h: V1[:, kb, (h // 4) * 64:(h // 4) * 64 + 64], 0, 0)

            base = NT + 12
            yh = lambda br: lambda k: ysp[:, 4 * br + k, 0, :]
            yl = lambda br: lambda k: ysp[:, 4 * br + k, 1, :]
            for u in range(3):
                product_first(FIRST["up"] + u, 4, yh(u), yl(u), lo_ok, NT + 4 * u)
            for u in range(3, 6):
                n = FIRST["up"] + u
                product(n, n % 2, n // 2, 4, yh(u % 3), yl(u % 3))
            with pe.Fori(1, N_UP // 6) as i:
                for u in range(6):
                    n = FIRST["up"] + u
                    product(i * 6 + n, n % 2, i * 3 + n // 2, 4, yh(u % 3), yl(u % 3))
            product_first(FIRST["out"], 8, hA, lA, lo_ok, base)
            products(FIRST["out"] + 1, N_OUT - 1, 8, hA, lA)
            pe.wait_ge(ss_sum, NT + 1)
            wait_room(pe, "ss1")
            for half in range(2):
                cols = slice(half * HALF, (half + 1) * HALF)
                mm = nc.tensor.matmul(mpair("ss1")[:, cols], C("mean1024"), prod[:, 1, cols],
                                      start=True, stop=True)
            mm.then_inc(R("ss1"), 1)
            hU = lambda k: uB[:, 0, k, :]
            lU = lambda k: uB[:, 1, k, :]
            for g in range(N_GROUP):
                n0 = FIRST["mlp"] + 16 * g
                if g == 0:
                    product_first(n0, 8, hA, lA, lo_ok, base + NT)
                    products(n0 + 1, 7, 8, hA, lA)
                else:
                    products(n0, 8, 8, hA, lA)
                product_first(n0 + 8, 8, hU, lU, u_ok, 8 * g)
                products(n0 + 9, 7, 8, hU, lU)
            base += 3 * NT
            product_first(FIRST["in2"], 8, hA, lA, lo_ok, base - NT)
            products(FIRST["in2"] + 1, 13, 8, hA, lA)
            pe.wait_ge(poolw_in, 16)
            for g in range(4):
                key = ("pool", g)
                pe.wait_ge(pooled_ok, g + 1)
                wait_room(pe, key)
                for half in range(2):
                    cols = slice(half * HALF, (half + 1) * HALF)
                    mm = nc.tensor.matmul(mpair(key)[:, cols], poolw[:, g, :], u2[:, g, cols],
                                          start=True, stop=True)
                mm.then_inc(R(key), 1)
            products(FIRST["in2"] + 14, 5, 8, hA, lA)
            stat("xq", "mean512", 4)
            stat("xkv", "mean256", 2)
            qh, ql = (lambda k: xqS[:, 0, k, :]), (lambda k: xqS[:, 1, k, :])
            product_first(FIRST["uq"], 4, qh, ql, lo_ok, base)
            products(FIRST["uq"] + 1, N_UQ - 1, 4, qh, ql)
            pe.wait_ge(lo_ok, base + 6)
            products(FIRST["ukv"], N_UKV, 2, lambda k: xkvS[:, 0, k, :], lambda k: xkvS[:, 1, k, :])
            for par in range(2):
                pe.wait_ge(unit_out[par], (FIRST["ukv"] + 1 - par) // 2)
            for r in range(3):
                key = ("swap", r)
                src = qr[:, r, :] if r < 2 else kr[:, :]
                wait_room(pe, key)
                for half in range(2):
                    cols = slice(half * HALF, (half + 1) * HALF)
                    mm = nc.tensor.matmul(mpair(key)[:, cols], C("swap"), src[:, cols], start=True, stop=True)
                mm.then_inc(R(key), 1)
            for par in range(2):
                pe.wait_ge(unit_out[par], (FIRST["out2"] + 1 - par) // 2)
            for h in range(MLA_HEADS):
                transposes(("v2T", h), lambda c: v4[:, h, c * P:(c + 1) * P], NB)

            def logits2(b, h, out):
                lo_p = (h % 2) * 64
                q = slice(b * P, (b + 1) * P)
                for half in range(2):
                    cols = slice(half * HALF, (half + 1) * HALF)
                    nc.tensor.matmul(out[:, cols], xq[:, h, q], kn[:, h, cols], start=True, stop=False)
                    mm = nc.tensor.matmul(out[:, cols], qr[lo_p:lo_p + 64, h // 2, q],
                                          kr[lo_p:lo_p + 64, cols], start=False, stop=True)
                return mm

            pe.wait_ge(roped, 3)
            for h in range(2, 4):
                wait_done(pe, ("v2T", h))
            attention(1, MLA_HEADS, P, at2, logits2, lambda kb, h: V2[:, kb, h * P:(h + 1) * P],
                      NB * HEADS, NB)
            product_first(FIRST["out2"], 8, hA, lA, lo_ok, base + 6)
            products(FIRST["out2"] + 1, N_OUT2 - 1, 8, hA, lA)
            pe.wait_ge(mu_sum, NT)
            wait_room(pe, "mu")
            for half in range(2):
                cols = slice(half * HALF, (half + 1) * HALF)
                mm = nc.tensor.matmul(mpair("mu")[:, cols], C("mean1024"), mu[:, cols], start=True, stop=True)
            mm.then_inc(R("mu"), 1)
            stat("var", "mean1024", NT)

        @block.scalar
        def _(act):
            steps = [0]

            def step(ins):
                steps[0] += 1
                ins.then_inc(act_step, 1)
                act.wait_ge(act_step, steps[0])

            def stat(key, srcs, room, eps=EPSV, src_ok=None):
                base = STAT_BASE[key]
                mk = stat_key(key)
                for k, src in enumerate(srcs):
                    c = base + k
                    if c >= 2:
                        act.wait_ge(squares_used, c - 1)
                    if src_ok:
                        act.wait_ge(src_ok[0], src_ok[1] + k)
                    nc.scalar.activation(sq[:, c % 2, :], src, ACT.Square).then_inc(squares, 1)
                act.wait_ge(squares_used, base + len(srcs))
                root(mk, room, eps)

            def root(mk, room, eps):
                if room:
                    act.wait_ge(*room)
                nc.scalar.activation(rstd[:, :], mpair(mk)[:, :], ACT.Ln, bias=eps).then_inc(F(mk), 1)
                wait_done(act, mk)
                nc.scalar.activation(rstd[:, :], rstd[:, :], ACT.Exp, scale=-0.5).then_inc(rstd_ok, 1)

            def his(c0, dsts, srcs, src_ok):
                for k, (d, s) in enumerate(zip(dsts, srcs)):
                    if src_ok:
                        act.wait_ge(src_ok[0], src_ok[1] + k)
                    nc.scalar.copy(d, s).then_inc(hi_ok, 1)

            act.wait_ge(consts_in, 64)
            act.wait_ge(x_in[0], 16 * NT)
            stat("x", [X0[:, j, :] for j in range(NT)], None)
            his(0, [actA[:, 0, j, :] for j in range(NT)], [tmpn[:, j % 2, :] for j in range(NT)], (nrm, 1))

            def read_unit(n, par, hn, dst, func):
                act.wait_ge(unit_mm, n + 1)
                nc.scalar.activation(dst, pair[par][:, :], func).then_inc(unit_out[par], 1)

            for n in range(N_QK):
                if n == 0:
                    act.wait_ge(lo_ok, NT)
                read_unit(n, n % 2, n // 2, att[:, n, :], ACT.Copy)
                if n == 0:
                    act.wait_ge(unit_out[0], 1)
                    act.dma_start(ik_up[64:128, :], att[0:64, 0, :]).then_inc(ik_copied, 16)
                if n == 2:
                    c = 0
                    for b in range(2, NB):
                        for h in range(IDX_HEADS):
                            wait_ready(act, ("idx", b, h))
                            if c >= 2:
                                act.wait_ge(idx_used, c - 1)
                            w = P * (b + 1)
                            nc.scalar.activation(sq[:, c % 2, 0:w], mpair(("idx", b, h))[:, 0:w], ACT.Relu) \
                              .then_inc(F(("idx", b, h)), 1)
                            c += 1
            wait_ready(act, "vT")
            nc.scalar.copy(V1[:, :, :].rearrange("p a b -> p (a b)"), mpair("vT")[:, :]).then_inc(F("vT"), 1)
            act.wait_ge(idx_used, 6 * IDX_HEADS)
            for h in range(HEADS):
                key = ("bias", h)
                wait_ready(act, key)
                if h >= 2:
                    act.wait_ge(skew_out, 16 * h)
                nc.scalar.mul(sq[:, h % 2, 0:384], mpair(key)[:, 0:384], float(HD) ** 0.5).then_inc(F(key), 1)
                wait_done(act, key)
                act.dma_start(skew.ap()[h], sq[:, h % 2, 0:384]).then_inc(skew_out, 16)

            def spill(first, quads, funcs, peel):
                def quad(i, q):
                    for s in range(4):
                        n = first + s
                        a = i * 4 + n
                        rel = i * 4 + (n - N_QK)
                        if q != 0:
                            act.wait_ge(spilled[s], (i + (first - N_QK) // 4) * 16)
                        par, hn = n % 2, i * 2 + n // 2
                        read_unit(a, par, hn, stage[:, s, :], funcs[s])
                        act.wait_ge(unit_out[par], hn + 1)
                        dst = proj[rel, :, :] if isinstance(rel, int) else \
                            proj[bass.ds(rel, 1), :, :].rearrange("a p n -> p (a n)")
                        act.dma_start(dst, stage[:, s, :]).then_inc(spilled[s], 16)
                if peel:
                    quad(0, 0)
                with act.Fori(int(peel), quads) as i:
                    quad(i, None)

            spill(N_QK, N_CONV // 4, [ACT.Copy] * 4, True)
            spill(N_QK + N_CONV, N_HG // 4, [ACT.Copy] * 3 + [ACT.Silu], False)
            act.wait_ge(skew_out, 16 * HEADS)

            def load_head(h, first, count, landed):
                a = N_CONV + 4 * h + first
                act.dma_start(hq[:, first:first + count, :], proj[a:a + count].rearrange("a p n -> p a n")) \
                   .then_inc(landed, 16)

            def store_y(j):
                act.wait_ge(y_made, j + 1)
                if j < CONV_T:
                    act.dma_start(ydram[4 + j], cy[:, j % 2, :]).then_inc(y_out[j % 2], 16)
                else:
                    act.dma_start(ydram[j - CONV_T], hy[:, :]).then_inc(y_out[j % 2], 16)

            def before_levels(h):
                act.wait_ge(zi_in, 16 * (h + 1))
                step(nc.scalar.activation(hE[:, 1, :], hq[:, 1, :], ACT.Abs))
                step(nc.scalar.activation(hE[:, 1, :], hE[:, 1, :], ACT.Exp, scale=-1.0))
                nc.scalar.activation(hE[:, 1, :], hE[:, 1, :], ACT.Ln, bias=1.0).then_inc(lsg, 1)
                act.wait_ge(hk_raw, h + 1)
                nc.scalar.activation(hk[:, :], hk[:, :], ACT.Exp, scale=-1.0).then_inc(hk_ok, 1)
                for lv in range(2):
                    act.wait_ge(expo, h * (LEVELS + 1) + lv + 1)
                    nc.scalar.activation(hE[:, lv % 2, :], hE[:, lv % 2, :], ACT.Exp).then_inc(decay, 1)

            n, quads, gates_read = N_IN - N_GATE, (N_CONV + N_HG) // 4, 0
            for key in GATE_PHASE:
                h = key[1] if len(key) > 1 else None
                if key[0] == "G":
                    s = (n - N_QK) % 4
                    act.wait_ge(spilled[s], 16 * ((n - N_QK) // 4))
                    read_unit(n, n % 2, n // 2, stage[:, s, :], ACT.Copy)
                    act.wait_ge(unit_out[n % 2], n // 2 + 1)
                    act.dma_start(proj[n - N_QK], stage[:, s, :]).then_inc(spilled[s], 16)
                    n += 1
                    gates_read += 1
                    if gates_read == 2:
                        act.wait_ge(rstd_used, 5)
                        act.dma_start(att_dram, att[:, 3:8, :].rearrange("p a b -> p (a b)")) \
                           .then_inc(parked, 16)
                        act.dma_start(pen_dram, pen[:, :]).then_inc(parked, 16)
                        for s in range(4):
                            act.wait_ge(spilled[s], 16 * quads)
                    if gates_read == 3:
                        act.wait_ge(parked, 32)
                        for j in range(CONV_T):
                            act.dma_start(cin[:, 3 * j:3 * j + 3, :],
                                          proj[3 * j:3 * j + 3].rearrange("a p n -> p a n")).then_inc(conv_in[j], 16)
                    if gates_read in (4, 5, 6):
                        store_y(gates_read - 4)
                    if gates_read == 5:
                        load_head(0, 1, 2, zi_in)
                        load_head(0, 0, 1, q_in)
                        load_head(0, 3, 1, g_in)
                    if gates_read == 7:
                        store_y(CONV_T - 1)
                        before_levels(0)
                elif key[:2] == ("stat", "qk"):
                    j = key[2]
                    stat(("qk", j), [att[:, 3 + j, :]], (rstd_used, j) if j else None)
                elif key[0] == "stat":
                    h = key[2]
                    stat(("hg", h), [mpair(("o", h))[:, :]], (rstd_used, 5) if h == 0 else (y_made, CONV_T + h))
                    store_y(CONV_T + h)
                    if h < HG_HEADS - 1:
                        load_head(h + 1, 3, 1, g_in)
                elif key[0] == "iT":
                    wait_ready(act, key)
                    if h:
                        wait_ready(act, ("o", h - 1))
                    nc.scalar.copy(hiT[:, :, :].rearrange("p a b -> p (a b)"), mpair(key)[:, :]) \
                      .then_inc(F(key), 1)
                elif key[0] == "lv":
                    lv = key[2]
                    if lv == 2 and h < HG_HEADS - 1:
                        act.wait_ge(expo, h * (LEVELS + 1) + 1)
                        wait_ready(act, ("iT", h))
                        load_head(h + 1, 1, 2, zi_in)
                    if 2 <= lv < LEVELS:
                        act.wait_ge(expo, h * (LEVELS + 1) + lv + 1)
                        nc.scalar.activation(hE[:, lv % 2, :], hE[:, lv % 2, :], ACT.Exp).then_inc(decay, 1)
                    elif lv == LEVELS:
                        if h == 0:
                            for par in range(2):
                                act.wait_ge(y_out[par], 16 * (CONV_T // 2))
                        nc.scalar.activation(hqG[:, :], hG[:, :], ACT.Exp).then_inc(decay, 1)
                        act.wait_ge(expo, (h + 1) * (LEVELS + 1))
                        nc.scalar.activation(hE[:, 1, :], hE[:, 1, :], ACT.Exp).then_inc(decay, 1)
                elif key[0] == "kT":
                    wait_ready(act, key)
                    nc.scalar.copy(hkT[:, :, :].rearrange("p a b -> p (a b)"), mpair(key)[:, :]) \
                      .then_inc(F(key), 1)
                    if h < HG_HEADS - 1:
                        act.wait_ge(hfin, h + 1)
                        wait_ready(act, ("lv", h, LEVELS))
                        load_head(h + 1, 0, 1, q_in)
                        before_levels(h + 1)
                elif key[0] == "o":
                    wait_ready(act, key)

            def attention(st, heads, buf, i0):
                N = NB * heads
                for i in range(N + 1):
                    if i < N:
                        w = n_keys(st, i // heads)
                        act.wait_ge(nm_ok, i0 + i + 1)
                        if i >= 2:
                            act.wait_ge(pT_ps, i0 + i - 1)
                        nc.scalar.activation(buf["Pm"][:, i % 2, 0:w], buf["L"][:, i % 2, 0:w], ACT.Exp,
                                             bias=tiny[:, 12 + i % 4:13 + i % 4],
                                             accum_out=tiny[:, 16 + i % 4:17 + i % 4]).then_inc(p_ok, 1)
                    if i >= 1:
                        w = n_keys(st, (i - 1) // heads)
                        act.wait_ge(pT_ps, i0 + i)
                        if i >= 3:
                            act.wait_ge(pv_ok, i0 + i - 2)
                        nc.scalar.copy(buf["PT"][:, (i - 1) % 2, 0:w], pair[0][:, 0:w]).then_inc(pT_ok, 1)

            attention(0, HEADS, at1, 0)
            for b in (NB - 2, NB - 1):
                wait_done(act, ("yT", 0, b))
            base = NT
            his(base, [ysp[:, k, 0, :] for k in range(4)], [yT[:, k, :] for k in range(4)], None)
            for k in range(8):
                act.wait_ge(yin_in[k % 2], 16 * (k // 2 + 1))
                nc.scalar.copy(ysp[:, 4 + k, 0, :], sq[:, k % 2, :]).then_inc(hi_ok, 1)

            def load_gates(j):
                for b in range(3):
                    act.dma_start(gates[:, j % 2, b, :], proj[N_CONV + N_HG + 8 * b + j]) \
                       .then_inc(gates_in[j % 2], 16)

            load_gates(0)
            load_gates(1)
            for j in range(NT):
                act.wait_ge(gates_in[j % 2], 48 * (j // 2 + 1))
                nc.scalar.activation(gates[:, j % 2, :, :], gates[:, j % 2, :, :], ACT.Sigmoid).then_inc(gate_ok, 1)
                act.wait_ge(mixed_ok, j + 1)
                if j + 2 < NT:
                    load_gates(j + 2)
            his(0, [actA[:, 0, j, :] for j in range(NT)], [mixed[:, j, :] for j in range(NT)],
                None)
            act.dma_start(poolw[:, :, :], t["pool_w"]).then_inc(poolw_in, 16)
            wait_ready(act, "ss1")
            root("ss1", None, EPSV)
            his(0, [actA[:, 0, j, :] for j in range(NT)], [tmpn[:, j % 2, :] for j in range(NT)], (nrm, NT + 1))
            for g in range(N_GROUP):
                n0 = FIRST["mlp"] + 16 * g

                def relu(n, par, hn, rel):
                    act.wait_ge(unit_mm, n + 1)
                    c = n - FIRST["mlp"] - 8 * g
                    if not isinstance(n, int) or c >= 2:
                        act.wait_ge(u_ok, c - 1)
                    nc.scalar.activation(mt[:, par, :], pair[par][:, :], ACT.Relu).then_inc(unit_out[par], 1)
                    act.wait_ge(unit_out[par], hn + 1)
                    nc.scalar.activation(mt[:, par, :], mt[:, par, :], ACT.Square).then_inc(relu_ok, 1)
                if g == 0:
                    act.wait_ge(lo_ok, 3 * NT + 12)
                    for n in range(n0, n0 + 8):
                        relu(n, n % 2, n // 2, n - n0)
                else:
                    units(act, n0, 8, 2, relu)
            base = 3 * NT + 12

            def high_x(n, par, hn, rel):
                act.wait_ge(unit_out[par], hn + 1)
                dst, src = tile(actA, rel, 0), tile(xB, rel)
                nc.scalar.copy(dst, src).then_inc(hi_ok, 1)
            units(act, FIRST["mlp"] + N_MLP - 8, 8, 2, high_x)
            act.dma_start(posqi[:, :], t["pos_q"]).then_inc(pos_in, 16)
            base += NT
            n = FIRST["in2"]
            outs = [(u2[:, g, :], ACT.Copy) for g in range(4)] + [(gb[:, g, :], ACT.Silu) for g in range(4)]
            outs += [(xq[:, g, :], ACT.Copy) for g in range(4)] + [(xkv[:, g, :], ACT.Copy) for g in range(2)]
            outs += [(u2[:, g, :], ACT.Silu) for g in range(4)] + [(kr[:, :], ACT.Copy)]
            for dst, func in outs:
                if n == FIRST["in2"] + 14:
                    for g in range(4):
                        wait_ready(act, ("pool", g))
                read_unit(n, n % 2, n // 2, dst, func)
                n += 1
            act.dma_start(posi[:, :], t["pos_row"].partition_broadcast(P)).then_inc(pos_in, 16)
            stat("xq", [xq[:, g, :] for g in range(4)], (lo_ok, 3 * NT + 12))
            his(0, [xqS[:, 0, g, :] for g in range(4)], [tmp2[:, g % 2, :] for g in range(4)], (nrm, 2 * NT + 1))
            stat("xkv", [xkv[:, g, :] for g in range(2)], (rstd_used, 6))
            his(0, [xkvS[:, 0, g, :] for g in range(2)], [tmp2[:, g % 2, :] for g in range(2)], (nrm, 2 * NT + 5))
            n = FIRST["uq"]
            act.wait_ge(lo_ok, base + 6)
            for dst in [xq[:, h, :] for h in range(4)] + [qr[:, r, :] for r in range(2)]:
                read_unit(n, n % 2, n // 2, dst, ACT.Copy)
                n += 1
            act.wait_ge(trig_in, 2)
            nc.scalar.activation(cs[:, 0, :], cs[:, 0, :], ACT.Sin).then_inc(trig, 1)
            nc.scalar.activation(cs[:, 1, :], cs[:, 1, :], ACT.Sin).then_inc(trig, 1)
            for dst in [kn[:, h, :] for h in range(4)] + [v4[:, h, :] for h in range(4)]:
                read_unit(n, n % 2, n // 2, dst, ACT.Copy)
                n += 1
            for h in range(MLA_HEADS):
                key = ("v2T", h)
                wait_ready(act, key)
                if h == 0:
                    act.wait_ge(roped, 3)
                nc.scalar.copy(V2[:, :, h * P:(h + 1) * P],
                               mpair(key)[:, :].rearrange("p (a b) -> p a b", b=P)).then_inc(F(key), 1)
            attention(1, MLA_HEADS, at2, NB * HEADS)
            for b in (NB - 2, NB - 1):
                wait_done(act, ("yT", 1, b))
            his(0, [actA[:, 0, j, :] for j in range(NT)],
                [u2[:, j, :] for j in range(4)] + [gb[:, j, :] for j in range(4)], None)
            stat("var", [xB[:, j, :] for j in range(NT)], (roped, 3), LNEPSV, (centred, 1))

        @block.vector
        def _(dve):
            steps = [0]

            def step(ins):
                steps[0] += 1
                ins.then_inc(dve_step, 1)
                dve.wait_ge(dve_step, steps[0])

            V = nc.vector

            def low(c, dst, src, hi):
                dve.wait_ge(hi_ok, c + 1)
                V.tensor_tensor(dst, src, hi.bitcast(F32), ALU.subtract).then_inc(lo_ok, 1)

            def norm_split(c0, q0, tiles, gains, tmp, dst):
                for k in range(len(tiles) + 1):
                    if k < len(tiles):
                        if k >= 2:
                            dve.wait_ge(lo_ok, c0 + k - 1)
                        V.scalar_tensor_tensor(tmp[:, k % 2, :], tiles[k], gains[k], rstd[:, :],
                                               ALU.mult, ALU.mult).then_inc(nrm, 1)
                    if k >= 1:
                        dve.wait_ge(nrm, q0 + k)
                        low(c0 + k - 1, dst[:, 1, k - 1, :], tmp[:, (k - 1) % 2, :], dst[:, 0, k - 1, :])

            dve.wait_ge(consts_in, 64)
            dve.wait_ge(x_in[0], 16 * NT)
            dve.wait_ge(rstd_ok, 1)
            norm_split(0, 0, [X0[:, j, :] for j in range(NT)], [SM("ln_mix", j) for j in range(NT)], tmpn, actA)
            wait_ready(dve, "iwT")
            V.tensor_scalar(iw[:, :, :], mpair("iwT")[:, :].rearrange("p (a b) -> p a b", b=P)[:, :, 64:68],
                            float(IDX_HEADS) ** -0.5 * float(HD) ** -0.5, None, ALU.mult).then_inc(F("iwT"), 1)
            wait_done(dve, "iwT")
            c = 0
            off = lambda b: P * b * (b + 1) // 2
            for b in range(2, NB):
                w = P * (b + 1)
                sc = pen[:, off(b):off(b) + w]
                for h in range(IDX_HEADS):
                    wait_done(dve, ("idx", b, h))
                    src = sq[:, c % 2, 0:w]
                    if h == 0:
                        V.tensor_scalar(sc, src, iw[:, b, h:h + 1], None, ALU.mult).then_inc(idx_used, 1)
                    else:
                        dve.wait_ge(idx_used, c)
                        V.scalar_tensor_tensor(sc, src, iw[:, b, h:h + 1], sc, ALU.mult, ALU.add) \
                         .then_inc(idx_used, 1)
                    c += 1
                dve.wait_ge(idx_used, c)
                step(V.tensor_tensor(sc[:, w - P:w], sc[:, w - P:w], C("causal"), ALU.add))
            V.tensor_copy(pen[:, 0:P], C("causal_neg")).then_inc(pen_ok, 1)
            V.memset(pen[:, P:2 * P], 0.0).then_inc(pen_ok, 1)
            V.tensor_copy(pen[:, 2 * P:3 * P], C("causal_neg")).then_inc(pen_ok, 1)
            rounds = TOPK // 8
            for b in range(2, NB):
                w = P * (b + 1)
                sc = pen[:, off(b):off(b) + w]
                done = (b - 2) * 2 * rounds
                for u in range(rounds):
                    V.max(top8[:, :], sc).then_inc(topk, 1)
                    dve.wait_ge(topk, done + 2 * u + 1)
                    V.match_replace(sc, top8[:, :], sc, PICKED).then_inc(topk, 1)
                    dve.wait_ge(topk, done + 2 * u + 2)
                V.tensor_scalar(sc, sc, 2 * FILL, NEG, ALU.is_gt, ALU.mult).then_inc(pen_ok, 1)
            for j in range(5):
                dve.wait_ge(rstd_ok, 2 + j)
                g = SM("q_norm") if j < 4 else SM("k_norm")
                if j == 0:
                    dve.wait_ge(unit_out[0], 5)
                V.scalar_tensor_tensor(att[:, 3 + j, :], att[:, 3 + j, :], g, rstd[:, :],
                                       ALU.mult, ALU.mult).then_inc(rstd_used, 1)
            dve.wait_ge(pen_ok, 9)
            dve.wait_ge(parked, 32)
            for j in range(CONV_T):
                dve.wait_ge(conv_in[j], 16)
                y = cy[:, j % 2, :]
                step(V.tensor_tensor(cu[:, :], cin[:, 3 * j, :], cin[:, 3 * j + 1, :], ALU.mult))
                if j >= 2:
                    dve.wait_ge(y_out[j % 2], 16 * (j // 2))
                step(V.tensor_scalar(y, cu[:, :], SM("conv", 2 * 4 + j), None, ALU.mult))
                for d in (1, 2):
                    step(V.scalar_tensor_tensor(y[:, d:S], cu[:, 0:S - d], SM("conv", (2 - d) * 4 + j),
                                                y[:, d:S], ALU.mult, ALU.add))
                V.tensor_tensor(y, y, cin[:, 3 * j + 2, :], ALU.mult).then_inc(y_made, 1)
                dve.wait_ge(y_made, j + 1)
            step(V.memset(hattn[:, :, :], 0.0))
            def exponents(lv):
                dst = hE[:, lv % 2, :]
                if lv < LEVELS:
                    m = 64 >> lv
                    gv = hG[:, :].rearrange("p (n x m) -> p n x m", x=2, m=m)
                    dv = dst.rearrange("p (n x m) -> p n x m", x=2, m=m)
                    mid = gv[:, :, 0, m - 1:m].broadcast_to([P, S // (2 * m), m])
                    V.tensor_tensor(dv[:, :, 1, :], gv[:, :, 1, :], mid, ALU.subtract)
                    V.tensor_tensor(dv[:, :, 0, :], mid, gv[:, :, 0, :], ALU.subtract).then_inc(expo, 1)
                else:
                    gv = hG[:, :].rearrange("p (n m) -> p n m", m=P)
                    V.tensor_tensor(dst.rearrange("p (n m) -> p n m", m=P),
                                    gv[:, :, P - 1:P].broadcast_to([P, NB, P]), gv,
                                    ALU.subtract).then_inc(expo, 1)

            def keep(h, lv):
                key = ("lv", h, lv)
                wait_ready(dve, key)
                if lv:
                    wait_done(dve, ("lv", h, lv - 1))
                V.copy_predicated(hattn[:, :, :], hmask[:, lv:lv + 1, :].broadcast_to([P, NB, P]),
                                  mpair(key)[:, :].rearrange("p (a b) -> p a b", b=P)).then_inc(F(key), 1)

            def before_levels(h):
                dve.wait_ge(lsg, h + 1)
                dve.wait_ge(zi_in, 16 * (h + 1))
                V.scalar_tensor_tensor(hk[:, :], hq[:, 1, :], 0.0, hE[:, 1, :], ALU.max, ALU.add) \
                 .then_inc(hk_raw, 1)
                step(V.scalar_tensor_tensor(hE[:, 0, :], hq[:, 1, :], 0.0, hE[:, 1, :],
                                            ALU.min, ALU.subtract))
                dve.wait_ge(hk_raw, h + 1)
                step(V.tensor_tensor_scan(hG[:, :], C("reset"), hE[:, 0, :], 0.0, ALU.mult, ALU.add))
                exponents(0)
                exponents(1)

            def finish(h):
                key = ("o", h)
                wait_ready(dve, key)
                dve.wait_ge(squares, STAT_BASE[("hg", h)] + 1)
                if h:
                    j = CONV_T + h - 1
                    dve.wait_ge(y_out[j % 2], 16 * (j // 2 + 1))
                dve.wait_ge(g_in, 16 * (h + 1))
                V.scalar_tensor_tensor(hy[:, :], mpair(key)[:, :], SM("hg_norm"), hq[:, 3, :],
                                       ALU.mult, ALU.mult).then_inc(F(key), 1)
                wait_done(dve, key)
                dve.wait_ge(rstd_ok, 7 + h)
                V.tensor_tensor(hy[:, :], hy[:, :], rstd[:, :], ALU.mult).then_inc(y_made, 1)

            before_levels(0)
            for h in range(HG_HEADS):
                e0 = h * (LEVELS + 1)
                dve.wait_ge(hk_ok, h + 1)
                dve.wait_ge(q_in, 16 * (h + 1))
                for lv in range(LEVELS):
                    dve.wait_ge(decay, h * (LEVELS + 2) + lv + 1)
                    if lv >= 2:
                        wait_ready(dve, ("lv", h, lv - 2))
                    elif h:
                        wait_ready(dve, ("lv", h - 1, LEVELS - 1) if lv == 0 else ("kT", h - 1))
                    m = 64 >> lv
                    v = lambda a: a.rearrange("p (n x m) -> p n x m", x=2, m=m)
                    wv, ev = v(hW[:, lv % 2, :]), v(hE[:, lv % 2, :])
                    V.tensor_tensor(wv[:, :, 1, :], v(hq[:, 0, :])[:, :, 1, :], ev[:, :, 1, :], ALU.mult)
                    V.tensor_tensor(wv[:, :, 0, :], v(hk[:, :])[:, :, 0, :], ev[:, :, 0, :],
                                    ALU.mult).then_inc(weighted, 1)
                    if lv + 2 <= LEVELS:
                        dve.wait_ge(weighted, e0 + lv + 1)
                        exponents(lv + 2)
                    if lv == 1 and h:
                        finish(h - 1)
                    if lv >= 1:
                        keep(h, lv - 1)
                dve.wait_ge(decay, h * (LEVELS + 2) + LEVELS + 1)
                step(V.tensor_copy(tiny[:, 0:8], hqG[:, P - 1:S:P]))
                V.tensor_tensor(hqG[:, :], hqG[:, :], hq[:, 0, :], ALU.mult).then_inc(hfin, 1)
                dve.wait_ge(decay, (h + 1) * (LEVELS + 2))
                wait_ready(dve, ("lv", h, LEVELS - 2))
                V.tensor_tensor(hW[:, 1, :], hk[:, :], hE[:, 1, :], ALU.mult).then_inc(weighted, 1)
                keep(h, LEVELS - 1)
                keep(h, LEVELS)
                if h + 1 < HG_HEADS:
                    dve.wait_ge(weighted, e0 + LEVELS + 1)
                    before_levels(h + 1)
                wait_ready(dve, ("dS", h))
                dS = mpair(("dS", h))
                step(V.tensor_copy(hS[:, 1, :], dS[:, 0:P]))
                for c in range(1, NB - 1):
                    ins = V.scalar_tensor_tensor(hS[:, c + 1, :], hS[:, c, :], tiny[:, c:c + 1],
                                                 dS[:, c * P:(c + 1) * P], ALU.mult, ALU.add)
                    if c < NB - 2:
                        step(ins)
                    else:
                        ins.then_inc(F(("dS", h)), 1)
            finish(HG_HEADS - 1)

            def attention(st, heads, dv, scale, buf, i0, b0, mask, write):
                N = NB * heads
                for i in range(N + 4):
                    if i < N:
                        b, h = i // heads, i % heads
                        w, key = n_keys(st, b), ("qk", st, i)
                        m = mask(b, h)
                        wait_ready(dve, key)
                        if i >= 2:
                            dve.wait_ge(p_ok, i0 + i - 1)
                        V.tensor_tensor_reduce(buf["L"][:, i % 2, 0:w], mpair(key)[:, 0:w], m, scale, -3.0e38,
                                               ALU.add, ALU.max, tiny[:, 8 + i % 4:9 + i % 4]) \
                         .then_inc(F(key), 1)
                        wait_done(dve, key)
                        V.tensor_scalar(tiny[:, 12 + i % 4:13 + i % 4], tiny[:, 8 + i % 4:9 + i % 4], -1.0,
                                        None, ALU.mult).then_inc(nm_ok, 1)
                    if 2 <= i < N + 2:
                        j = i - 2
                        b, h = j // heads, j % heads
                        dve.wait_ge(p_ok, i0 + j + 1)
                        step(V.reciprocal(tiny[:, 20 + j % 4:21 + j % 4], tiny[:, 16 + j % 4:17 + j % 4]))
                        dve.wait_ge(pv_ok, i0 + j + 1)
                        if h == 0 and b >= 2:
                            wait_ready(dve, ("yT", st, b - 2))
                        a = (j % 2) * HALF
                        V.tensor_scalar(buf["O"][:, b % 2, h * dv:(h + 1) * dv], pair[1][:, a:a + dv],
                                        tiny[:, 20 + j % 4:21 + j % 4], None, ALU.mult).then_inc(o_ok, 1)
                    if i >= 4 and (i - 3) % heads == 0:
                        b = (i - 3) // heads - 1
                        key = ("yT", st, b)
                        wait_ready(dve, key)
                        src = mpair(key)[:, 0:HALF].rearrange("p (a b) -> p a b", b=P)
                        write(b, src).then_inc(F(key), 1)

            dve.wait_ge(pen_in, 16)
            for s in range(4):
                dve.wait_ge(spilled[s], 16 * (N_CONV + N_HG + N_GATE) // 4)
            attention(0, HEADS, HD, float(HD) ** -0.5, at1, 0, 0,
                      lambda b, h: pen[:, off(b):off(b) + P * (b + 1)],
                      lambda b, src: V.tensor_copy(yT[:, :, b * P:(b + 1) * P], src))
            for b in (NB - 2, NB - 1):
                wait_done(dve, ("yT", 0, b))
            for k in range(12):
                low(NT + k, ysp[:, k, 1, :], yT[:, k, :] if k < 4 else sq[:, k % 2, :], ysp[:, k, 0, :])
            first = FIRST["up"]
            with dve.Fori(0, 4) as i:
                for jj in range(2):
                    mx = mixed[:, bass.ds(i * 2 + jj, 1), :].rearrange("p a n -> p (a n)")
                    for br in range(3):
                        n = first + 3 * jj + br
                        par, hn = n % 2, i * 3 + n // 2
                        dve.wait_ge(unit_mm, i * 6 + (n + 1))
                        if br == 0:
                            dve.wait_ge(gate_ok, i * 2 + (jj + 1))
                        dst = mx if br == 0 else prod[:, br - 1, :]
                        V.tensor_tensor(dst, pair[par][:, :], gates[:, jj, br, :], ALU.mult) \
                         .then_inc(unit_out[par], 1)
                        dve.wait_ge(unit_out[par], hn + 1)
                        if br == 1:
                            V.tensor_tensor(mx, mx, prod[:, 0, :], ALU.add).then_inc(mix_step, 1)
                        if br == 2:
                            dve.wait_ge(mix_step, i * 2 + (jj + 1))
                            V.tensor_tensor(mx, mx, prod[:, 1, :], ALU.add).then_inc(mixed_ok, 1)
            base = NT + 12
            dve.wait_ge(mixed_ok, NT)
            for j in range(NT):
                low(base + j, actA[:, 1, j, :], mixed[:, j, :], actA[:, 0, j, :])
            dve.wait_ge(x_in[1], 16 * NT)

            def add_x(n, par, hn, rel):
                dve.wait_ge(unit_mm, n + 1)
                x = tile(xB, rel)
                V.tensor_tensor(x, pair[par][:, :], x, ALU.add).then_inc(unit_out[par], 1)
            V.memset(prod[:, 1, :], 0.0).then_inc(ss_sum, 1)

            def add_x_square(n, par, hn, rel):
                add_x(n, par, hn, rel)
                dve.wait_ge(unit_out[par], hn + 1)
                x = tile(xB, rel)
                V.tensor_tensor(prod[:, 0, :], x, x, ALU.mult).then_inc(ss_sq, 1)
                dve.wait_ge(ss_sq, rel + 1)
                dve.wait_ge(ss_sum, rel + 1)
                V.tensor_tensor(prod[:, 1, :], prod[:, 1, :], prod[:, 0, :], ALU.add).then_inc(ss_sum, 1)
            units(dve, FIRST["out"], N_OUT, 2, add_x_square)
            base += NT
            for par in range(2):
                dve.wait_ge(unit_out[par], (FIRST["mlp"] + 1 - par) // 2)
            dve.wait_ge(rstd_ok, 11)
            norm_split(base, NT, [xB[:, j, :] for j in range(NT)], [SM("ln_mlp", j) for j in range(NT)],
                       tmpn, actA)
            base += NT
            dve.wait_ge(lo_ok, base)
            for g in range(N_GROUP):
                n0 = FIRST["mlp"] + 16 * g
                if g:
                    dve.wait_ge(unit_mm, n0)

                def split_u(n, par, hn, rel):
                    c = n - (FIRST["mlp"] + 8 * g)
                    dve.wait_ge(relu_ok, c + 1)
                    V.tensor_copy(tile(uB, rel, 0), mt[:, par, :]).then_inc(hfin, 1)
                    dve.wait_ge(hfin, c + (HG_HEADS + 1))
                    V.tensor_tensor(tile(uB, rel, 1), mt[:, par, :], tile(uB, rel, 0).bitcast(F32),
                                    ALU.subtract).then_inc(u_ok, 1)
                units(dve, n0, 8, 2, split_u)
                if g < N_GROUP - 1:
                    units(dve, n0 + 8, 8, 2, add_x)
                else:
                    def add_split(n, par, hn, rel):
                        add_x(n, par, hn, rel)
                        c = rel + base
                        dve.wait_ge(hi_ok, c + 1)
                        V.tensor_tensor(tile(actA, rel, 1), tile(xB, rel), tile(actA, rel, 0).bitcast(F32),
                                        ALU.subtract).then_inc(lo_ok, 1)
                    units(dve, n0 + 8, 8, 2, add_split)
            base += NT
            for g, win in enumerate(POOL_WINDOWS):
                n = FIRST["in2"] + g
                dve.wait_ge(unit_out[n % 2], n // 2 + 1)
                if g:
                    dve.wait_ge(pooled_ok, g)
                src = u2[:, g, :]
                for d in range(g + 1):
                    sh = 1 << d
                    dst = sq[:, d % 2, :]
                    step(V.tensor_copy(dst[:, 0:sh], src[:, 0:sh]))
                    step(V.tensor_tensor(dst[:, sh:S], src[:, sh:S], src[:, 0:S - sh], ALU.add))
                    src = dst
                other = sq[:, (g + 1) % 2, 0:16]
                a = CST["pool"][0] + 16 * g
                step(V.tensor_tensor(other, src[:, 0:16], cst[:, a:a + 16], ALU.mult))
                step(V.scalar_tensor_tensor(u2[:, g, 16:S], src[:, 16:S], 1.0 / win, u2[:, g, 16:S],
                                            ALU.mult, ALU.subtract))
                V.tensor_tensor(u2[:, g, 0:16], other, u2[:, g, 0:16], ALU.subtract).then_inc(pooled_ok, 1)
            for g in range(4):
                key = ("pool", g)
                wait_ready(dve, key)
                n = FIRST["in2"] + 4 + g
                dve.wait_ge(unit_out[n % 2], n // 2 + 1)
                V.scalar_tensor_tensor(gb[:, g, :], mpair(key)[:, :], SM("pool_scale", g), gb[:, g, :],
                                       ALU.mult, ALU.mult).then_inc(F(key), 1)
            dve.wait_ge(rstd_ok, 12)
            norm_split(base, 2 * NT, [xq[:, g, :] for g in range(4)], [SM("q_norm_2", g) for g in range(4)],
                       tmp2, xqS)
            dve.wait_ge(pos_in, 32)
            V.tensor_copy(posqf[:, :], posqi[:, :]).then_inc(rstd_used, 1)
            dve.wait_ge(rstd_ok, 13)
            dve.wait_ge(lo_ok, base + 4)
            norm_split(base + 4, 2 * NT + 4, [xkv[:, g, :] for g in range(2)],
                       [SM("kv_norm_2", g) for g in range(2)], tmp2, xkvS)
            step(V.tensor_copy(posb[:, :], posi[:, :]))
            a0, a1 = ang[:, 0, :], ang[:, 1, :]
            c1 = 6.28125
            c2 = float(np.float32(np.round((TWO_PI - c1) * 2 ** 22) / 2 ** 22))
            c3 = TWO_PI - c1 - c2
            step(V.tensor_scalar(a0, posb[:, :], C("rope")[:, 0:1], None, ALU.mult))
            step(V.tensor_scalar(a1, a0, 1.0 / TWO_PI, MAGIC, ALU.mult, ALU.add))
            step(V.tensor_scalar(a1, a1, -MAGIC, None, ALU.add))
            for cc in (c1, c2, c3):
                step(V.scalar_tensor_tensor(a0, a1, -cc, a0, ALU.mult, ALU.add))
            dve.wait_ge(lo_ok, base + 6)
            LIM = 3.1415925
            V.tensor_scalar(cs[:, 1, :], a0, -LIM, LIM, ALU.max, ALU.min).then_inc(trig_in, 1)
            step(V.tensor_scalar(a0, a0, float(np.pi / 2), None, ALU.add))
            step(V.tensor_scalar(a1, a0, float(np.pi), -TWO_PI, ALU.is_gt, ALU.mult))
            step(V.tensor_tensor(a0, a0, a1, ALU.add))
            V.tensor_scalar(cs[:, 0, :], a0, -LIM, LIM, ALU.max, ALU.min).then_inc(trig_in, 1)
            dve.wait_ge(trig, 2)
            for r in range(3):
                key = ("swap", r)
                x = qr[:, r, :] if r < 2 else kr[:, :]
                wait_ready(dve, key)
                V.tensor_tensor(rtmp[:, :], mpair(key)[:, :], cs[:, 1, :], ALU.mult).then_inc(F(key), 1)
                wait_done(dve, key)
                step(V.tensor_tensor(x, x, cs[:, 0, :], ALU.mult))
                V.tensor_tensor(x, x, rtmp[:, :], ALU.add).then_inc(roped, 1)
                dve.wait_ge(roped, r + 1)

            made = [0]

            def mask2(b, h):
                if h == 0:
                    made[0] += 1
                    V.tensor_scalar(pen2[:, b % 2, :], posb[:, :], posqf[:, b:b + 1], NEG,
                                    ALU.is_gt, ALU.mult).then_inc(pen2_ok, 1)
                    dve.wait_ge(pen2_ok, made[0])
                return pen2[:, b % 2, :]

            def gated(b, src):
                y = u2[:, :, b * P:(b + 1) * P]
                return V.tensor_tensor(y, src, y, ALU.mult)

            attention(1, MLA_HEADS, P, float(192) ** -0.5, at2, NB * HEADS, NB, mask2, gated)
            base += 6
            for b in (NB - 2, NB - 1):
                wait_done(dve, ("yT", 1, b))
            for j in range(NT):
                src = u2[:, j, :] if j < 4 else gb[:, j - 4, :]
                low(base + j, actA[:, 1, j, :], src, actA[:, 0, j, :])

            def add_scaled(n, par, hn, rel):
                dve.wait_ge(unit_mm, n + 1)
                x = tile(xB, rel)
                V.scalar_tensor_tensor(x, x, float(2.0 ** 0.25), pair[par][:, :], ALU.mult, ALU.add) \
                 .then_inc(unit_out[par], 1)
                dve.wait_ge(unit_out[par], hn + 1)
                if isinstance(rel, int) and rel == 0:
                    V.tensor_copy(mu[:, :], x).then_inc(mu_sum, 1)
                else:
                    dve.wait_ge(mu_sum, rel)
                    V.tensor_tensor(mu[:, :], mu[:, :], x, ALU.add).then_inc(mu_sum, 1)
            add_scaled(FIRST["out2"], FIRST["out2"] % 2, FIRST["out2"] // 2, 0)
            dve.wait_ge(lo_ok, base + NT)

            def add_rest(n, par, hn, rel):
                add_scaled(n, par, hn, rel + 1)
            units(dve, FIRST["out2"] + 1, N_OUT2 - 1, 2, add_rest)
            wait_ready(dve, "mu")
            V.tensor_copy(mu[:, :], mpair("mu")[:, :]).then_inc(F("mu"), 1)
            wait_done(dve, "mu")
            for j in range(NT):
                ins = V.tensor_tensor(xB[:, j, :], xB[:, j, :], mu[:, :], ALU.subtract)
                ins.then_inc(centred, 1)
            dve.wait_ge(centred, NT)
            dve.wait_ge(rstd_ok, 14)
            for j in range(NT):
                step(V.scalar_tensor_tensor(xB[:, j, :], xB[:, j, :], SM("ln_g", j), rstd[:, :],
                                            ALU.mult, ALU.mult))
                if j >= 2:
                    dve.wait_ge(fin_out[j % 2], 16 * (j // 2))
                V.tensor_scalar(fin[:, j % 2, :], xB[:, j, :], SM("ln_b", j), None, ALU.add).then_inc(fin_ok, 1)


def n_keys(st, b):
    return P * (b + 1) if st == 0 else S


def stat_key(key):
    return ("stat",) + (key if isinstance(key, tuple) else (key,))


def tile(tensor, rel, part=None):
    if part is None:
        return tensor[:, rel, :] if isinstance(rel, int) else \
            tensor[:, bass.ds(rel, 1), :].rearrange("p a n -> p (a n)")
    return tensor[:, part, rel, :] if isinstance(rel, int) else \
        tensor[:, part, bass.ds(rel, 1), :].rearrange("p a n -> p (a n)")


def by_unit(w):
    k, n = w.shape
    return np.ascontiguousarray(w.reshape(k // P, P, n // P, P).transpose(2, 1, 0, 3)
                                .reshape(n // P, P, k))


def by_tile(v):
    return np.ascontiguousarray(v.reshape(-1, P).T)


def kernel(**inputs):
    import concourse.bacc as bacc
    from concourse.bass_utils import run_bass_kernel_spmd

    a = {k: np.asarray(v) for k, v in inputs.items()}
    w = a["w_in"][0]
    cut = np.cumsum([0, 512, 128, 128, 256, 64, 4, 512, 512, 512, 512, 512, 512, 512, 3072])
    aq, ak, av, iq, ik, iw, hq, hf, hi, hg, cb, cc, ch, gt = (w[:, cut[i]:cut[i + 1]] for i in range(14))
    pad = np.zeros((D, 60), np.float32)
    q_cols = [np.concatenate([aq[:, j * 64:(j + 1) * 64], aq[:, (j + 4) * 64:(j + 5) * 64]], 1) for j in range(4)]
    cols = [ik, iw, pad, iq] + q_cols + [ak, av]
    for j in range(4):
        s = slice(j * P, (j + 1) * P)
        cols += [cc[:, s], ch[:, s], cb[:, s]]
    for j in range(4):
        s = slice(j * P, (j + 1) * P)
        cols += [hq[:, s], hf[:, s], hi[:, s], hg[:, s]]
    cols += [gt]
    w_in = np.concatenate(cols, 1)
    ups = [by_unit(a[n][0]) for n in ("w_up_attn", "w_up_hgrn", "w_up_conv")]
    w_up = np.ascontiguousarray(np.stack(ups, 1).reshape(N_UP, P, HALF))
    up, down = by_unit(a["w_mlp_up"][0]), a["w_mlp_down"][0]
    mlp = []
    for g in range(N_GROUP):
        mlp += [up[8 * g:8 * g + 8], by_unit(down[D * g:D * (g + 1)])]
    w = a["w_in_2"]
    cut = np.cumsum([0, 512, 256, 64, 512, 512, 512])
    xq, xkv, kr, ga, up2, gb = (w[:, cut[i]:cut[i + 1]] for i in range(6))
    w_in2 = np.concatenate([up2, gb, xq, xkv, ga, kr, kr], 1)
    uq = a["w_uq_2"].reshape(512, MLA_HEADS, 192)
    uq = np.concatenate([uq[:, :, :P].reshape(512, -1), uq[:, :, P:].reshape(512, -1)], 1)
    ukv = a["w_ukv_2"].reshape(256, MLA_HEADS, 2 * P)
    ukv = np.concatenate([ukv[:, :, :P].reshape(256, -1), ukv[:, :, P:].reshape(256, -1)], 1)
    pos = a["positions_2"][0]
    small = [by_tile(a["ln_mix_g"][0]), by_tile(a["ln_mlp_g"][0]), by_tile(a["hgrn_norm_g"][0]),
             np.tile(a["q_norm_g"][0], 2)[:, None], np.tile(a["k_norm_g"][0], 2)[:, None],
             by_tile(a["conv_w"][0].reshape(-1)), by_tile(a["pool_scale_2"]), by_tile(a["q_norm_g_2"]),
             by_tile(a["kv_norm_g_2"]), by_tile(a["ln_g_2"][0]), by_tile(a["ln_b_2"][0])]
    cst, masks = shape_constants()
    arrays = {
        "xT": a["x"][0].T, "cst": cst, "masks": masks, "small": np.concatenate(small, 1),
        "rel_bias": a["rel_bias"], "w_in": by_unit(w_in), "w_up": w_up, "w_out": by_unit(a["w_out"][0]),
        "w_mlp": np.concatenate(mlp, 0), "w_in2": by_unit(w_in2), "w_uq": by_unit(uq), "w_ukv": by_unit(ukv),
        "w_out2": by_unit(a["w_out_2"]), "pool_w": a["pool_w_2"].transpose(1, 0, 2),
        "pos_row": pos[None, :], "pos_q": pos.reshape(NB, P).T,
    }
    arrays = {k: np.ascontiguousarray(v) for k, v in arrays.items()}
    nc = bacc.Bacc("TRN2", target_bir_lowering=False, num_devices=1)
    t = {k: nc.dram_tensor(k, v.shape, mybir.dt.from_np(v.dtype), kind="ExternalInput").ap()
         for k, v in arrays.items()}
    t["outT"] = nc.dram_tensor("outT", (D, S), F32, kind="ExternalOutput").ap()
    build(nc, t)
    r = run_bass_kernel_spmd(nc, [arrays], core_ids=[0])
    return np.ascontiguousarray(r.results[0]["outT"].T)[None]
```

```python
from contextlib import ExitStack

import numpy as np
import concourse.bass as bass
from concourse import mybir

F32 = mybir.dt.float32
F32R = mybir.dt.float32r
I32 = mybir.dt.int32
ACT = mybir.ActivationFunctionType
ALU = mybir.AluOpType
AX = mybir.AxisListType

P = 128
S = 1024
D = 1024
NT = D // P
NB = S // P
HALF = 512
EPS = 1e-6
LN_EPS = 1e-5

HEADS, HD, TOPK = 8, 64, 256
IDX_HEADS = 4
BUCKETS, MAX_DIST = 32, 128
HG_HEADS = 4
LEVELS = 7
CONV_T = 4
D_FF = 4096
MLA_HEADS = 4
POOL_WINDOWS = (2, 4, 8, 16)
ROPE_HALF = 32

NEG = -1.0e30
FILL = -1.0e38
PICKED = -3.0e38
TWO_PI = 2.0 * np.pi
MAGIC = 1.5 * 2.0 ** 23

N_QK, N_CONV, N_HG, N_GATE = 9, 12, 16, 24
N_IN = N_QK + N_CONV + N_HG + N_GATE
N_UP = 24
N_OUT = 8
N_GROUP = 4
N_MLP = 16 * N_GROUP
N_IN2 = 19
N_UQ = 6
N_UKV = 8
N_OUT2 = 8
FIRST = {}
_n = 0
for _name, _count in (("in", N_IN), ("up", N_UP), ("out", N_OUT), ("mlp", N_MLP), ("in2", N_IN2),
                      ("uq", N_UQ), ("ukv", N_UKV), ("out2", N_OUT2)):
    FIRST[_name] = _n
    _n += _count
N_UNITS = _n

CST = {}
_c = 0
for _name, _w in (("ident", P), ("mean64", P), ("mean128", P), ("mean256", P), ("mean512", P),
                  ("mean1024", P), ("causal", P), ("causal_neg", P), ("reset", S), ("bucket", 384),
                  ("pool", 4 * 16), ("rope", 8), ("swap", P)):
    CST[_name] = (_c, _w)
    _c += _w
N_CST = _c


def shape_constants():
    c = np.zeros((P, N_CST), np.float32)

    def put(name, value):
        a, w = CST[name]
        c[:value.shape[0], a:a + w] = value

    i = np.arange(P)
    put("ident", np.eye(P, dtype=np.float32))
    put("mean64", ((i[:, None] // 64) == (i[None, :] // 64)) / np.float32(64))
    for n in (128, 256, 512, 1024):
        put(f"mean{n}", np.full((P, P), 1.0 / n, np.float32))
    put("causal", np.where(i[None, :] > i[:, None], FILL, 0.0).astype(np.float32))
    put("causal_neg", np.where(i[None, :] > i[:, None], NEG, 0.0).astype(np.float32))
    put("reset", np.broadcast_to((np.arange(S) % P != 0).astype(np.float32), (P, S)))
    j = np.arange(384)
    d = np.maximum(255 - j, 0)
    half = BUCKETS // 2
    far = half + (np.log(np.maximum(d, 1).astype(np.float32) / np.float32(half))
                  / np.float32(np.log(MAX_DIST / half)) * np.float32(BUCKETS - half)).astype(np.int32)
    b = np.where(d < half, d, np.minimum(far, BUCKETS - 1))
    hot = np.zeros((BUCKETS, 384), np.float32)
    hot[b, j] += 1.0
    hot[BUCKETS - 1, :] -= 1.0
    put("bucket", hot)
    pool = np.zeros((P, 4, 16), np.float32)
    for g, w in enumerate(POOL_WINDOWS):
        pool[:, g, :] = 1.0 / np.minimum(np.arange(16) + 1, w)
    put("pool", pool.reshape(P, 64))
    rope = np.zeros((P, 8), np.float32)
    rope[:, 0] = (np.float32(10000.0) ** (-(i % ROPE_HALF).astype(np.float32) / ROPE_HALF))
    rope[:, 1] = EPS
    rope[:, 2] = LN_EPS
    put("rope", rope)
    swap = np.zeros((P, P), np.float32)
    for o in range(P):
        swap[o ^ ROPE_HALF, o] = 1.0 if o & ROPE_HALF else -1.0
    put("swap", swap)
    masks = np.zeros((P, LEVELS + 1, P), np.int32)
    for lv in range(LEVELS):
        m = 64 >> lv
        same = (i[:, None] // (2 * m)) == (i[None, :] // (2 * m))
        masks[:, lv, :] = same & ((i[:, None] // m) % 2 == 0) & ((i[None, :] // m) % 2 == 1)
    masks[:, LEVELS, :] = np.eye(P, dtype=np.int32)
    return c, masks.reshape(P, -1)


SMALL = {}
_c = 0
for _name, _w in (("ln_mix", 8), ("ln_mlp", 8), ("hg_norm", 1), ("q_norm", 1), ("k_norm", 1), ("conv", 12),
                  ("pool_scale", 4), ("q_norm_2", 4), ("kv_norm_2", 2), ("ln_g", 8), ("ln_b", 8)):
    SMALL[_name] = (_c, _w)
    _c += _w
N_SMALL = _c



PEN_FIRST = 3


def attention_uses(st, heads):
    uses, n = [("qk", st, 0)], NB * heads
    for i in range(n + 3):
        uses += [("qk", st, i + 1)] * (i + 1 < n)
        uses += [("yT", st, (i - 2) // heads - 1)] * (i >= 3 and (i - 2) % heads == 0)
    return uses


def gate_phase():
    order = [("G",)] * 5 + [("iT", 0)]
    for h in range(HG_HEADS):
        order += [("lv", h, 0), ("lv", h, 1), ("G",), ("lv", h, 2), ("lv", h, 3), ("G",)]
        order += [("lv", h, 4), ("lv", h, 5), ("G",), ("lv", h, 6), ("lv", h, 7), ("kT", h), ("G",)]
        order += [("dS", h)] + [("G",)] * (h + 1 < HG_HEADS - 1) + [("o", h)]
        order += [("iT", h + 1)] * (h + 1 < HG_HEADS) + [("stat", "hg", h)]
    order += [("G",)]
    assert order.count(("G",)) == N_GATE
    return order


GATE_PHASE = gate_phase()


def misc_plan():
    uses = [("stat", "x"), "iwT"]
    uses += [("idx", b, h) for b in range(2, NB) for h in range(IDX_HEADS)]
    uses += ["vT"] + [("bias", h) for h in range(HEADS)]
    uses += [("stat", "qk", j) for j in range(5)]
    uses += [key for key in GATE_PHASE if key[0] != "G"]
    uses += attention_uses(0, HEADS)
    uses += ["ss1"]
    uses += [("pool", g) for g in range(4)]
    uses += [("stat", "xq"), ("stat", "xkv"), ("swap", 0), ("swap", 1), ("swap", 2)]
    uses += [("v2T", h) for h in range(MLA_HEADS)]
    uses += attention_uses(1, MLA_HEADS)
    uses += ["mu", ("stat", "var")]
    plan, ready, free = {}, [0, 0], [0, 0]
    for m, key in enumerate(uses):
        s = m % 2
        ready[s] += not (isinstance(key, tuple) and key[0] == "stat")
        plan[key] = (s, ready[s], free[s])
        free[s] += 1
    return plan


STATS = [("x", NT)] + [(("qk", j), 1) for j in range(5)] + [(("hg", h), 1) for h in range(HG_HEADS)]
STATS += [("xq", 4), ("xkv", 2), ("var", NT)]
STAT_BASE, STAT_NO = {}, {}
_c = 0
for _i, (_k, _w) in enumerate(STATS):
    STAT_BASE[_k], STAT_NO[_k] = _c, _i
    _c += _w


def build(nc, t):
    with ExitStack() as ctx:
        BASE = 16512
        MISC = misc_plan()

        def sem(name):
            return ctx.enter_context(nc.semaphore(name))

        def at(name, kb, shape, dt=F32):
            return nc.alloc_sbuf_tensor_at(name, shape, dt, offset=BASE + int(kb * 1024))

        raw = at("raw", 0, [P, 2, 1024])
        w_hi = at("w_hi", 8, [P, 2, 1024], F32R)
        w_lo = at("w_lo", 16, [P, 2, 1024], F32R)
        actA = at("actA", 24, [P, 2, NT, S], F32R)
        X0 = at("X0", 88, [P, NT, S])
        att = at("att", 88, [P, N_QK, S])
        pen = at("pen", 124, [P, 4608])
        toep = at("toep", 142, [P, HEADS, 256])
        V1 = at("V1", 152, [P, NB, P])
        ik_up = at("ik_up", 154, [P, S])
        stage = at("stage", 158, [P, 4, S])
        sq = at("sq", 176, [P, 2, S])
        cst = at("cst", 184, [P, N_CST])
        small = at("small", 194.5, [P, N_SMALL])
        iw = at("iw", 195, [P, NB, IDX_HEADS])
        tiny = at("tiny", 195.125, [P, 32])
        top8 = at("top8", 195.25, [P, 8])
        rb = at("rb", 195.3125, [BUCKETS, HEADS])
        hmask = at("hmask", 195.5, [P, LEVELS + 1, P], I32)
        rstd = at("rstd", 199.5, [P, S])
        assert 184 * 1024 + N_CST * 4 <= 194.5 * 1024 and N_SMALL * 4 <= 512
        hq = at("hq", 88, [P, 4, S])
        hG = at("hG", 104, [P, S])
        hk = at("hk", 108, [P, S])
        hE = at("hE", 112, [P, 2, S])
        hW = at("hW", 120, [P, 2, S])
        hattn = at("hattn", 128, [P, NB, P])
        hiT = at("hiT", 132, [P, NB, P])
        hkT = at("hkT", 136, [P, NB, P])
        hS = at("hS", 140, [P, NB, P])
        hqG = at("hqG", 144, [P, S])
        hy = at("hy", 203.5, [P, S])
        cin = at("cin", 88, [P, 3 * CONV_T, S])
        cu = sq[:, 0, :]
        cy = at("cy", 142, [P, 2, S])
        qk_rstd = [att[:, j, :] for j in range(3)] + [cy[:, j, :] for j in range(2)]
        at1 = dict(L=at("a_L", 176, [P, 2, S]), Pm=at("a_P", 88, [P, 2, S]), PT=at("a_PT", 195.5, [P, 2, S]),
                   O=[at("a_O0", 156, [P, HALF]), at("a_O1", 174, [P, HALF])])
        yT = at("yT", 158, [P, 4, S])
        ysp = at("ysp", 24, [P, 12, 2, S], F32R)
        yin = [at("yin0", 96, [P, S]), at("yin1", 203.5, [P, S])]
        gates = at("gates", 120, [P, 2, 3, S])
        prod = at("prod", 144, [P, 2, S])
        mixed = at("mixed", 152, [P, NT, S])
        xB = at("xB", 88, [P, NT, S])
        tmpn = at("tmpn", 158, [P, 2, S])
        actB = at("actB", 120, [P, 2, NT, S], F32R)
        mt = [at("mt0", 195.5, [P, S]), at("mt1", 203.5, [P, S])]
        sq2 = at("sq2", 80, [P, 2, S])
        u2 = at("u2", 24, [P, 4, S])
        gb = at("gb", 40, [P, 4, S])
        xq = at("xq", 56, [P, 4, S])
        xkv = at("xkv", 72, [P, 2, S])
        poolw = at("poolw", 195.5, [P, 4, P])
        kr = at("kr", 195.5, [P, S])
        posb = at("posb", 203.5, [P, S])
        posi = at("posi", 203.5, [P, S], I32)
        xqS = at("xqS", 120, [P, 2, 4, S], F32R)
        xkvS = at("xkvS", 152, [P, 2, 2, S], F32R)
        tmp2 = at("tmp2", 168, [P, 2, S])
        kn = at("kn", 168, [P, 4, S])
        v4 = at("v4", 120, [P, 4, S])
        V2 = at("V2", 136, [P, NB, HALF])
        qr = at("qr", 80, [P, 2, S])
        cs = at("cs", 72, [P, 2, S])
        pen2 = at("pen2", 72, [P, 2, S])
        ang = at("ang", 176, [P, 2, S])
        at2 = dict(L=at("b_L", 152, [P, 2, S]), Pm=at("b_P", 160, [P, 2, S]), PT=at("b_PT", 120, [P, 2, S]),
                   O=[at("b_O0", 128, [P, HALF]), at("b_O1", 130, [P, HALF])])
        fin = at("fin", 120, [P, 2, S])
        rtmp = at("rtmp", 136, [P, S])
        mu = at("mu", 24, [P, S])
        pad = at("pad", 195.46875, [P, 2])
        posqi = at("posqi", 195.375, [P, NB], I32)
        posqf = at("posqf", 195.4375, [P, NB])
        pair = [ctx.enter_context(nc.psum_tensor(f"pair{i}", [P, 2 * HALF], F32)) for i in range(4)]

        proj = nc.dram_tensor("proj", (N_CONV + N_HG + N_GATE, P, S), F32, kind="Internal").ap()
        ydram = nc.dram_tensor("ydram", (8, P, S), F32, kind="Internal").ap()
        att_dram = nc.dram_tensor("att_dram", (P, 5 * S), F32, kind="Internal").ap()
        pen_dram = nc.dram_tensor("pen_dram", (P, 4608), F32, kind="Internal").ap()
        skew = nc.dram_tensor("skew", (HEADS, P, 384), F32, kind="Internal")

        consts_in = sem("consts_in")
        x_tile_in = [sem(f"x_tile_in{j}") for j in range(NT)]
        x_in = sem("x_in")
        masks_in = sem("masks_in")
        w_in = [sem("w_in0"), sem("w_in1")]
        w_split = sem("w_split")
        w_hi_ok = sem("w_hi_ok")
        unit_mm = sem("unit_mm")
        unit_out = [sem("unit_out0"), sem("unit_out1")]
        ready = [sem("ready0"), sem("ready1")]
        free = [sem("free0"), sem("free1")]
        spilled = [sem(f"spilled{i}") for i in range(4)]
        squares = sem("squares")
        squares_used = sem("squares_used")
        rstd_ok = sem("rstd_ok")
        rstd_used = sem("rstd_used")
        dve_step = sem("dve_step")
        act_step = sem("act_step")
        pool_step = sem("pool_step")
        nrm = sem("nrm")
        hi_ok = sem("hi_ok")
        lo_ok = sem("lo_ok")
        ik_copied = sem("ik_copied")
        idx_used = sem("idx_used")
        topk = sem("topk")
        pen_ok = sem("pen_ok")
        skew_out = sem("skew_out")
        toep_in = sem("toep_in")
        parked = sem("parked")
        pen_parked = sem("pen_parked")
        att_in = sem("att_in")
        pen_in = [sem("pen_in0"), sem("pen_in1")]
        gate_ok = sem("gate_ok")
        ss_sq = sem("ss_sq")
        ss_sum = sem("ss_sum")
        mu_sum = sem("mu_sum")
        mix_step = sem("mix_step")
        conv_in = [sem(f"conv_in{i}") for i in range(CONV_T)]
        zi_in = sem("zi_in")
        q_in = sem("q_in")
        g_in = sem("g_in")
        y_out = [sem("y_out0"), sem("y_out1")]
        y_made = sem("y_made")
        lsg = sem("lsg")
        hk_raw = sem("hk_raw")
        hk_ok = sem("hk_ok")
        expo = sem("expo")
        decay = sem("decay")
        weighted = sem("weighted")
        hfin = sem("hfin")
        l_ok = sem("l_ok")
        nm_ok = sem("nm_ok")
        p_ok = sem("p_ok")
        pT_ps = sem("pT_ps")
        pT_ok = sem("pT_ok")
        pv_ok = sem("pv_ok")
        o_ok = sem("o_ok")
        yin_in = [sem("yin_in0"), sem("yin_in1")]
        branch_hi = sem("branch_hi")
        branch_lo = sem("branch_lo")
        gates_in = [sem("gates_in0"), sem("gates_in1")]
        mixed_ok = sem("mixed_ok")
        relu_ok = sem("relu_ok")
        u_ok = sem("u_ok")
        pooled_ok = sem("pooled_ok")
        poolw_in = sem("poolw_in")
        pos_in = sem("pos_in")
        trig = sem("trig")
        trig_in = sem("trig_in")
        roped = sem("roped")
        pen2_ok = sem("pen2_ok")
        centred = sem("centred")
        scaled = sem("scaled")
        fin_ok = sem("fin_ok")
        fin_out = [sem("fin_out0"), sem("fin_out1")]

        def C(name, rows=P):
            a, w = CST[name]
            return cst[0:rows, a:a + w]

        def SM(name, j=0):
            a = SMALL[name][0]
            return small[:, a + j:a + j + 1]

        EPSV = C("rope")[:, 1:2]
        LNEPSV = C("rope")[:, 2:3]

        def squared(c):
            return (sq2 if c >= STAT_BASE["xq"] else sq)[:, c % 2, :]

        def mpair(key):
            return pair[2 + MISC[key][0]]

        def wait_ready(eng, key):
            s, r, _ = MISC[key]
            eng.wait_ge(ready[s], r)

        def wait_done(eng, key):
            s, _, f = MISC[key]
            eng.wait_ge(free[s], f + 1)

        def wait_room(pe, key):
            s, _, f = MISC[key]
            if f > 0:
                pe.wait_ge(free[s], f)

        def R(key):
            return ready[MISC[key][0]]

        def F(key):
            return free[MISC[key][0]]

        def units(eng, first, count, width, body):
            k = count % width
            for n in range(first, first + k):
                body(n, n % 2, n // 2, n - first)
            start = first + k
            with eng.Fori(0, (count - k) // width) as i:
                for u in range(width):
                    n = start + u
                    if width % 2 == 0:
                        body(i * width + n, n % 2, i * (width // 2) + n // 2, i * width + (k + u))

        block = ctx.enter_context(nc.Block())

        @block.sync
        def _(sp):
            def load_units(name, first, count, kt, done=0):
                src = t[name][done:]
                first, count = first + done, count - done

                def body(n, par, hn, rel):
                    if isinstance(n, int) and n < 2:
                        pass
                    else:
                        sp.wait_ge(w_split, n - 1)
                    row = src[rel, :, :] if isinstance(rel, int) else \
                        src[bass.ds(rel, 1), :, :].rearrange("a p n -> p (a n)")
                    sp.dma_start(raw[:, par, 0:kt * P], row).then_inc(w_in[par], 16)
                units(sp, first, count, 2, body)

            sp.dma_start(cst[:, :], t["cst"]).then_inc(consts_in, 16)
            sp.dma_start(small[:, :], t["small"]).then_inc(consts_in, 16)
            sp.dma_start(rb[:, :], t["rel_bias"]).then_inc(consts_in, 16)
            for j in range(NT):
                sp.dma_start(X0[:, j, :], t["xT"][j * P:(j + 1) * P, :]).then_inc(x_tile_in[j], 16)
            sp.dma_start(hmask[:, :, :].rearrange("p a b -> p (a b)"), t["masks"]).then_inc(masks_in, 16)
            load_units("w_in", 0, N_IN, 8)
            last = HG_HEADS - 1
            wait_ready(sp, ("kT", last))
            sp.dma_start(att[:, 4:8, :].rearrange("p a b -> p (a b)"), att_dram[:, S:5 * S]) \
              .then_inc(att_in, 16)
            sp.wait_ge(skew_out, 16 * HEADS)
            wait_ready(sp, ("o", last))
            for h in range(HEADS):
                src = bass.AP(skew, h * P * 384 + 127, [[383, P], [1, 256]])
                sp.dma_start(toep[:, h, :], src).then_inc(toep_in, 16)
            cut = P * PEN_FIRST * (PEN_FIRST + 1) // 2
            sp.dma_start(pen[:, 0:cut], pen_dram[:, 0:cut]).then_inc(pen_in[0], 16)
            sp.wait_ge(y_made, CONV_T + HG_HEADS)
            sp.dma_start(att[:, 3, :], att_dram[:, 0:S]).then_inc(att_in, 16)
            sp.dma_start(pen[:, cut:4608], pen_dram[:, cut:4608]).then_inc(pen_in[1], 16)
            for par in range(2):
                sp.wait_ge(y_out[par], 16 * ((CONV_T + HG_HEADS) // 2))
            for k in range(8):
                if k >= 2:
                    sp.wait_ge(branch_lo, k - 1)
                sp.dma_start(yin[k % 2][:, :], ydram[k]).then_inc(yin_in[k % 2], 16)
            load_units("w_up", FIRST["up"], N_UP, 4)
            load_units("w_out", FIRST["out"], 2, 8)
            sp.wait_ge(mixed_ok, NT)
            for j in range(NT):
                sp.dma_start(xB[:, j, :], t["xT"][j * P:(j + 1) * P, :]).then_inc(x_in, 16)
            load_units("w_out", FIRST["out"], N_OUT, 8, 2)
            load_units("w_mlp", FIRST["mlp"], N_MLP, 8)
            load_units("w_in2", FIRST["in2"], N_IN2, 8)
            load_units("w_uq", FIRST["uq"], N_UQ, 4)
            load_units("w_ukv", FIRST["ukv"], N_UKV, 2)
            load_units("w_out2", FIRST["out2"], N_OUT2, 8)
            for k in range(NT):
                sp.wait_ge(fin_ok, k + 1)
                sp.dma_start(t["outT"][k * P:(k + 1) * P, :], fin[:, k % 2, :]).then_inc(fin_out[k % 2], 16)
            for k in range(2):
                sp.wait_ge(fin_out[k], 16 * (NT // 2))

        @block.gpsimd
        def _(pool):
            def split_units(first, count, kt):
                def body(n, par, hn, rel):
                    pool.wait_ge(w_in[par], (hn + 1) * 16)
                    if not isinstance(n, int) or n >= 2:
                        pool.wait_ge(unit_mm, n - 1)
                    nc.gpsimd.tensor_tensor(pad[:, 0:1], pad[:, 1:2], pad[:, 1:2], ALU.add)
                    w = kt * P
                    nc.gpsimd.tensor_copy(w_hi[:, par, 0:w], raw[:, par, 0:w]).then_inc(w_hi_ok, 1)
                    pool.wait_ge(w_hi_ok, n + 1)
                    nc.gpsimd.tensor_tensor(w_lo[:, par, 0:w], raw[:, par, 0:w],
                                            w_hi[:, par, 0:w].bitcast(F32), ALU.subtract).then_inc(w_split, 1)
                units(pool, first, count, 2, body)

            nc.gpsimd.memset(pad[:, :], 0.0).then_inc(pool_step, 1)
            pool.wait_ge(pool_step, 1)
            split_units(0, N_IN, 8)
            pool.wait_ge(unit_mm, N_IN)
            for k in range(8):
                pool.wait_ge(yin_in[k % 2], 16 * (k // 2 + 1))
                nc.gpsimd.tensor_copy(ysp[:, k, 0, :], yin[k % 2][:, :]).then_inc(branch_hi, 1)
                pool.wait_ge(branch_hi, k + 1)
                nc.gpsimd.tensor_tensor(ysp[:, k, 1, :], yin[k % 2][:, :], ysp[:, k, 0, :].bitcast(F32),
                                        ALU.subtract).then_inc(branch_lo, 1)
            split_units(FIRST["up"], N_UP, 4)
            split_units(FIRST["out"], N_OUT + N_MLP + N_IN2, 8)
            split_units(FIRST["uq"], N_UQ, 4)
            split_units(FIRST["ukv"], N_UKV, 2)
            split_units(FIRST["out2"], N_OUT2, 8)

        @block.tensor
        def _(pe):
            def product(n, par, hn, kt, hi, lo):
                pe.wait_ge(w_split, n + 1)
                if not isinstance(n, int) or n >= 2:
                    pe.wait_ge(unit_out[par], hn)
                last = None
                for half in range(2):
                    cols = slice(half * HALF, (half + 1) * HALF)
                    for k in range(kt):
                        wk = slice(k * P, (k + 1) * P)
                        for i, (w, x) in enumerate(((w_hi, hi(k)), (w_hi, lo(k)), (w_lo, hi(k)))):
                            last = nc.tensor.matmul(pair[par][:, cols], w[:, par, wk], x[:, cols],
                                                    start=(k == 0 and i == 0), stop=(k == kt - 1 and i == 2))
                last.then_inc(unit_mm, 1)

            def product_first(n, kt, hi, lo, ok, base):
                par = n % 2
                pe.wait_ge(w_split, n + 1)
                if n >= 2:
                    pe.wait_ge(unit_out[par], n // 2)
                last = None
                for k in range(kt):
                    pe.wait_ge(ok, base + k + 1)
                    wk = slice(k * P, (k + 1) * P)
                    for half in range(2):
                        cols = slice(half * HALF, (half + 1) * HALF)
                        for i, (w, x) in enumerate(((w_hi, hi(k)), (w_hi, lo(k)), (w_lo, hi(k)))):
                            last = nc.tensor.matmul(pair[par][:, cols], w[:, par, wk], x[:, cols],
                                                    start=(k == 0 and i == 0), stop=(k == kt - 1 and i == 2))
                last.then_inc(unit_mm, 1)

            def products(first, count, kt, hi, lo, width=2):
                units(pe, first, count, width, lambda n, par, hn, rel: product(n, par, hn, kt, hi, lo))

            def stat(key, name, srcs_n):
                base = STAT_BASE[key]
                wait_room(pe, stat_key(key))
                for k in range(srcs_n):
                    c = base + k
                    pe.wait_ge(squares, c + 1)
                    for half in range(2):
                        cols = slice(half * HALF, (half + 1) * HALF)
                        mm = nc.tensor.matmul(mpair(stat_key(key))[:, cols], C(name), squared(c)[:, cols],
                                              start=(k == 0), stop=(k == srcs_n - 1))
                    mm.then_inc(squares_used, 1)

            def transposes(key, src, count):
                wait_room(pe, key)
                for c in range(count):
                    mm = nc.tensor.transpose(mpair(key)[:, c * P:(c + 1) * P], src(c), C("ident"))
                mm.then_inc(R(key), 1)

            hA = lambda k: actA[:, 0, k, :]
            lA = lambda k: actA[:, 1, k, :]
            pe.wait_ge(consts_in, 48)
            stat("x", "mean1024", NT)
            product_first(0, 8, hA, lA, lo_ok, 0)
            for n in range(1, 3):
                product(n, n % 2, n // 2, 8, hA, lA)
            pe.wait_ge(unit_out[0], 2)
            pe.wait_ge(unit_out[1], 1)
            transposes("iwT", lambda c: att[:, 0, c * P:(c + 1) * P], NB)
            pe.wait_ge(ik_copied, 16)
            for b in range(2, NB):
                for h in range(IDX_HEADS):
                    key = ("idx", b, h)
                    wait_room(pe, key)
                    lo_p = (h % 2) * 64
                    ks = att[0:64, 0, :] if h % 2 == 0 else ik_up[64:128, :]
                    for c0 in range(0, P * (b + 1), HALF):
                        c1 = min(c0 + HALF, P * (b + 1))
                        mm = nc.tensor.matmul(mpair(key)[:, c0:c1],
                                              att[lo_p:lo_p + 64, 1 + h // 2, b * P:(b + 1) * P],
                                              ks[:, c0:c1], start=True, stop=True)
                    mm.then_inc(R(key), 1)
            for n in range(3, N_QK):
                product(n, n % 2, n // 2, 8, hA, lA)
            pe.wait_ge(unit_out[0], 5)
            transposes("vT", lambda c: att[:, 8, c * P:(c + 1) * P], NB)
            for h in range(HEADS):
                key = ("bias", h)
                wait_room(pe, key)
                nc.tensor.matmul(mpair(key)[:, 0:384], rb[:, h:h + 1].broadcast_to([BUCKETS, P]),
                                 C("bucket", BUCKETS), start=True, stop=True).then_inc(R(key), 1)
            products(N_QK, N_CONV, 8, hA, lA, 4)
            for j in range(4):
                n = N_QK + N_CONV + j
                product(n, n % 2, n // 2, 8, hA, lA)
                stat(("qk", j), "mean64", 1)
            stat(("qk", 4), "mean64", 1)
            products(N_QK + N_CONV + 4, N_HG - 4, 8, hA, lA, 4)
            n = N_IN - N_GATE
            for key in GATE_PHASE:
                h = key[1] if len(key) > 1 else None
                if key[0] == "G":
                    product(n, n % 2, n // 2, 8, hA, lA)
                    n += 1
                elif key[0] == "stat":
                    stat(("hg", key[2]), "mean128", 1)
                elif key[0] == "iT":
                    pe.wait_ge(zi_in, 16 * (h + 1))
                    transposes(key, lambda c: hq[:, 2, c * P:(c + 1) * P], NB)
                elif key[0] == "lv":
                    lv = key[2]
                    if lv < LEVELS:
                        pe.wait_ge(weighted, h * (LEVELS + 1) + lv + 1)
                        ks, qs = hW[:, lv % 2, :], hW[:, lv % 2, :]
                    else:
                        pe.wait_ge(hk_ok, h + 1)
                        ks, qs = hk[:, :], hq[:, 0, :]
                    wait_room(pe, key)
                    for c in range(NB):
                        cc = slice(c * P, (c + 1) * P)
                        mm = nc.tensor.matmul(mpair(key)[:, cc], ks[:, cc], qs[:, cc], start=True, stop=True)
                    mm.then_inc(R(key), 1)
                elif key[0] == "kT":
                    pe.wait_ge(weighted, (h + 1) * (LEVELS + 1))
                    transposes(key, lambda c: hW[:, 1, c * P:(c + 1) * P], NB)
                elif key[0] == "dS":
                    wait_done(pe, ("kT", h))
                    wait_done(pe, ("iT", h))
                    wait_room(pe, key)
                    for c in range(NB - 1):
                        mm = nc.tensor.matmul(mpair(key)[:, c * P:(c + 1) * P], hkT[:, c, :], hiT[:, c, :],
                                              start=True, stop=True)
                    mm.then_inc(R(key), 1)
                elif key[0] == "o":
                    wait_done(pe, ("dS", h))
                    wait_done(pe, ("lv", h, LEVELS))
                    wait_done(pe, ("lv", h, LEVELS - 1))
                    pe.wait_ge(hfin, h + 1)
                    wait_room(pe, key)
                    for c in range(NB):
                        out = mpair(key)[:, c * P:(c + 1) * P]
                        mm = nc.tensor.matmul(out, hiT[:, c, :], hattn[:, c, :], start=True, stop=(c == 0))
                        if c:
                            mm = nc.tensor.matmul(out, hS[:, c, :], hqG[:, c * P:(c + 1) * P],
                                                  start=False, stop=True)
                    mm.then_inc(R(key), 1)

            def attention(st, heads, dv, buf, logits, values, i0, b0):
                N = NB * heads

                def qk(i):
                    key = ("qk", st, i)
                    wait_room(pe, key)
                    logits(i // heads, i % heads, mpair(key)).then_inc(R(key), 1)

                def turn(i):
                    pe.wait_ge(p_ok, i0 + i + 1)
                    if i0 + i > 0:
                        pe.wait_ge(pT_ok, i0 + i)
                    for kb in range(n_keys(st, i // heads) // P):
                        mm = nc.tensor.transpose(pair[0][:, kb * P:(kb + 1) * P],
                                                 buf["Pm"][:, i % 2, kb * P:(kb + 1) * P], C("ident"))
                    mm.then_inc(pT_ps, 1)

                def pv(i):
                    b, h = i // heads, i % heads
                    pe.wait_ge(pT_ok, i0 + i + 1)
                    if i0 + i >= 2:
                        pe.wait_ge(o_ok, i0 + i - 1)
                    nk = n_keys(st, b) // P
                    for kb in range(nk):
                        a = (i % 2) * HALF
                        mm = nc.tensor.matmul(pair[1][:, a:a + dv], buf["PT"][:, i % 2, kb * P:(kb + 1) * P],
                                              values(kb, h), start=(kb == 0), stop=(kb == nk - 1))
                    mm.then_inc(pv_ok, 1)

                def turn_out(b):
                    pe.wait_ge(o_ok, i0 + (b + 1) * heads)
                    transposes(("yT", st, b), lambda c: buf["O"][b % 2][:, c * P:(c + 1) * P], 4)

                qk(0)
                for i in range(N + 3):
                    if i + 1 < N:
                        qk(i + 1)
                    if i < N:
                        turn(i)
                    if 1 <= i <= N:
                        pv(i - 1)
                    if 3 <= i and (i - 2) % heads == 0:
                        turn_out((i - 2) // heads - 1)

            def logits1(b, h, out):
                n, lo_p = P * (b + 1), (h // 4) * 64
                w = min(n, 2 * P)
                for c0 in range(0, n, HALF):
                    c1 = min(c0 + HALF, n)
                    near = max(c0, n - w)
                    mm = nc.tensor.matmul(out[:, c0:c1], att[lo_p:lo_p + 64, 3 + h % 4, b * P:(b + 1) * P],
                                          att[lo_p:lo_p + 64, 7, c0:c1], start=True, stop=(near >= c1))
                    if near < c1:
                        a = near - n + 2 * P
                        mm = nc.tensor.matmul(out[:, near:c1], C("ident"), toep[:, h, a:a + c1 - near],
                                              start=False, stop=True)
                return mm

            pe.wait_ge(att_in, 32)
            pe.wait_ge(toep_in, 16 * HEADS)
            wait_done(pe, "vT")
            pe.wait_ge(unit_out[0], (N_IN + 1) // 2)
            pe.wait_ge(unit_out[1], N_IN // 2)
            attention(0, HEADS, HD, at1, logits1, lambda kb, h: V1[:, kb, (h // 4) * 64:(h // 4) * 64 + 64], 0, 0)

            base = NT + 4
            yh = lambda br: lambda k: ysp[:, 4 * br + k, 0, :]
            yl = lambda br: lambda k: ysp[:, 4 * br + k, 1, :]
            for u in range(3):
                ok, first = (branch_lo, 4 * u) if u < 2 else (lo_ok, NT)
                product_first(FIRST["up"] + u, 4, yh(u), yl(u), ok, first)
            for u in range(3, 6):
                n = FIRST["up"] + u
                product(n, n % 2, n // 2, 4, yh(u % 3), yl(u % 3))
            with pe.Fori(1, N_UP // 6) as i:
                for u in range(6):
                    n = FIRST["up"] + u
                    product(i * 6 + n, n % 2, i * 3 + n // 2, 4, yh(u % 3), yl(u % 3))
            product_first(FIRST["out"], 8, hA, lA, lo_ok, base)
            products(FIRST["out"] + 1, N_OUT - 1, 8, hA, lA)
            hB = lambda k: actB[:, 0, k, :]
            lB = lambda k: actB[:, 1, k, :]
            for g in range(N_GROUP):
                n0 = FIRST["mlp"] + 16 * g
                if g == 0:
                    product_first(n0, 8, hB, lB, lo_ok, base + NT)
                    pe.wait_ge(ss_sum, NT + 1)
                    wait_room(pe, "ss1")
                    for half in range(2):
                        cols = slice(half * HALF, (half + 1) * HALF)
                        mm = nc.tensor.matmul(mpair("ss1")[:, cols], C("mean1024"), mt[1][:, cols],
                                              start=True, stop=True)
                    mm.then_inc(R("ss1"), 1)
                    products(n0 + 1, 7, 8, hB, lB)
                else:
                    products(n0, 8, 8, hB, lB)
                product_first(n0 + 8, 8, hA, lA, u_ok, 8 * g)
                products(n0 + 9, 7, 8, hA, lA)
            base += 3 * NT
            product_first(FIRST["in2"], 8, hB, lB, lo_ok, base - NT)
            products(FIRST["in2"] + 1, 13, 8, hB, lB)
            pe.wait_ge(poolw_in, 16)
            for g in range(4):
                key = ("pool", g)
                pe.wait_ge(pooled_ok, g + 1)
                wait_room(pe, key)
                for half in range(2):
                    cols = slice(half * HALF, (half + 1) * HALF)
                    mm = nc.tensor.matmul(mpair(key)[:, cols], poolw[:, g, :], u2[:, g, cols],
                                          start=True, stop=True)
                mm.then_inc(R(key), 1)
            n = FIRST["in2"] + 14
            product(n, n % 2, n // 2, 8, hB, lB)
            stat("xq", "mean512", 4)
            products(FIRST["in2"] + 15, 4, 8, hB, lB)
            qh, ql = (lambda k: xqS[:, 0, k, :]), (lambda k: xqS[:, 1, k, :])
            product_first(FIRST["uq"], 4, qh, ql, lo_ok, base)
            stat("xkv", "mean256", 2)
            products(FIRST["uq"] + 1, N_UQ - 1, 4, qh, ql)
            pe.wait_ge(lo_ok, base + 6)
            products(FIRST["ukv"], N_UKV, 2, lambda k: xkvS[:, 0, k, :], lambda k: xkvS[:, 1, k, :])
            for par in range(2):
                pe.wait_ge(unit_out[par], (FIRST["ukv"] + 1 - par) // 2)
            for r in range(3):
                key = ("swap", r)
                src = qr[:, r, :] if r < 2 else kr[:, :]
                wait_room(pe, key)
                for half in range(2):
                    cols = slice(half * HALF, (half + 1) * HALF)
                    mm = nc.tensor.matmul(mpair(key)[:, cols], C("swap"), src[:, cols], start=True, stop=True)
                mm.then_inc(R(key), 1)
            for par in range(2):
                pe.wait_ge(unit_out[par], (FIRST["out2"] + 1 - par) // 2)
            for h in range(MLA_HEADS):
                transposes(("v2T", h), lambda c: v4[:, h, c * P:(c + 1) * P], NB)

            def logits2(b, h, out):
                lo_p = (h % 2) * 64
                q = slice(b * P, (b + 1) * P)
                for half in range(2):
                    cols = slice(half * HALF, (half + 1) * HALF)
                    nc.tensor.matmul(out[:, cols], xq[:, h, q], kn[:, h, cols], start=True, stop=False)
                    mm = nc.tensor.matmul(out[:, cols], qr[lo_p:lo_p + 64, h // 2, q],
                                          kr[lo_p:lo_p + 64, cols], start=False, stop=True)
                return mm

            pe.wait_ge(roped, 3)
            for h in range(2, 4):
                wait_done(pe, ("v2T", h))
            attention(1, MLA_HEADS, P, at2, logits2, lambda kb, h: V2[:, kb, h * P:(h + 1) * P],
                      NB * HEADS, NB)
            product_first(FIRST["out2"], 8, hB, lB, lo_ok, base + 6)
            products(FIRST["out2"] + 1, N_OUT2 - 1, 8, hB, lB)
            pe.wait_ge(mu_sum, NT)
            wait_room(pe, "mu")
            for half in range(2):
                cols = slice(half * HALF, (half + 1) * HALF)
                mm = nc.tensor.matmul(mpair("mu")[:, cols], C("mean1024"), mu[:, cols], start=True, stop=True)
            mm.then_inc(R("mu"), 1)
            stat("var", "mean1024", NT)

        @block.scalar
        def _(act):
            steps = [0]

            def step(ins):
                steps[0] += 1
                ins.then_inc(act_step, 1)
                act.wait_ge(act_step, steps[0])

            def square(c, src):
                if c >= 2:
                    act.wait_ge(squares_used, c - 1)
                nc.scalar.activation(squared(c), src, ACT.Square).then_inc(squares, 1)

            def stat(key, srcs, room, eps=EPSV, src_ok=None):
                base = STAT_BASE[key]
                for k, src in enumerate(srcs):
                    if src_ok:
                        act.wait_ge(src_ok[0], src_ok[1] + k)
                    square(base + k, src)
                act.wait_ge(squares_used, base + len(srcs))
                root(stat_key(key), room, eps)

            def root(mk, room, eps, dst=rstd[:, :]):
                if room:
                    act.wait_ge(*room)
                nc.scalar.activation(dst, mpair(mk)[:, :], ACT.Ln, bias=eps).then_inc(F(mk), 1)
                wait_done(act, mk)
                nc.scalar.activation(dst, dst, ACT.Exp, scale=-0.5).then_inc(rstd_ok, 1)

            def his(c0, dsts, srcs, src_ok):
                for k, (d, s) in enumerate(zip(dsts, srcs)):
                    if src_ok:
                        act.wait_ge(src_ok[0], src_ok[1] + k)
                    nc.scalar.copy(d, s).then_inc(hi_ok, 1)

            act.wait_ge(consts_in, 48)
            for j in range(NT):
                act.wait_ge(x_tile_in[j], 16)
                square(STAT_BASE["x"] + j, X0[:, j, :])
            act.wait_ge(squares_used, NT)
            root(("stat", "x"), None, EPSV)
            his(0, [actA[:, 0, j, :] for j in range(NT)], [tmpn[:, j % 2, :] for j in range(NT)], (nrm, 1))

            def read_unit(n, par, hn, dst, func):
                act.wait_ge(unit_mm, n + 1)
                nc.scalar.activation(dst, pair[par][:, :], func).then_inc(unit_out[par], 1)

            for n in range(N_QK):
                if n == 0:
                    act.wait_ge(lo_ok, NT)
                read_unit(n, n % 2, n // 2, att[:, n, :], ACT.Copy)
                if n == 0:
                    act.wait_ge(unit_out[0], 1)
                    act.dma_start(ik_up[64:128, :], att[0:64, 0, :]).then_inc(ik_copied, 16)
                if n == 2:
                    c = 0
                    for b in range(2, NB):
                        for h in range(IDX_HEADS):
                            wait_ready(act, ("idx", b, h))
                            if c >= 2:
                                act.wait_ge(idx_used, c - 1)
                            w = P * (b + 1)
                            nc.scalar.activation(sq[:, c % 2, 0:w], mpair(("idx", b, h))[:, 0:w], ACT.Relu) \
                              .then_inc(F(("idx", b, h)), 1)
                            c += 1
            wait_ready(act, "vT")
            nc.scalar.copy(V1[:, :, :].rearrange("p a b -> p (a b)"), mpair("vT")[:, :]).then_inc(F("vT"), 1)
            act.wait_ge(idx_used, 6 * IDX_HEADS)
            for h in range(HEADS):
                key = ("bias", h)
                wait_ready(act, key)
                if h >= 2:
                    act.wait_ge(skew_out, 16 * h)
                nc.scalar.mul(sq[:, h % 2, 0:384], mpair(key)[:, 0:384], float(HD) ** 0.5).then_inc(F(key), 1)
                wait_done(act, key)
                act.dma_start(skew.ap()[h], sq[:, h % 2, 0:384]).then_inc(skew_out, 16)

            def spill(first, quads, funcs, peel, between=None):
                def quad(i, q, between=None):
                    for s in range(4):
                        n = first + s
                        a = i * 4 + n
                        rel = i * 4 + (n - N_QK)
                        if q != 0:
                            act.wait_ge(spilled[s], (i + (first - N_QK) // 4) * 16)
                        par, hn = n % 2, i * 2 + n // 2
                        read_unit(a, par, hn, stage[:, s, :], funcs[s])
                        act.wait_ge(unit_out[par], hn + 1)
                        dst = proj[rel, :, :] if isinstance(rel, int) else \
                            proj[bass.ds(rel, 1), :, :].rearrange("a p n -> p (a n)")
                        act.dma_start(dst, stage[:, s, :]).then_inc(spilled[s], 16)
                        if between:
                            between(s)
                if peel:
                    quad(0, 0 if first == N_QK else None, between)
                if between:
                    between(4)
                with act.Fori(int(peel), quads) as i:
                    quad(i, None)

            spill(N_QK, N_CONV // 4, [ACT.Copy] * 4, True)
            act.wait_ge(skew_out, 16 * HEADS)

            def norm_qk(j):
                c = STAT_BASE[("qk", j)]
                if j < 4:
                    square(c + 1, att[:, 3 + j + 1, :])
                act.wait_ge(squares_used, c + 1)
                root(("stat", "qk", j), None, EPSV, qk_rstd[j])
            square(STAT_BASE[("qk", 0)], att[:, 3, :])
            spill(N_QK + N_CONV, N_HG // 4, [ACT.Copy] * 3 + [ACT.Silu], True, norm_qk)

            def load_head(h, first, count, landed):
                a = N_CONV + 4 * h + first
                act.dma_start(hq[:, first:first + count, :], proj[a:a + count].rearrange("a p n -> p a n")) \
                   .then_inc(landed, 16)

            def store_y(j):
                act.wait_ge(y_made, j + 1)
                if j < CONV_T:
                    act.dma_start(ydram[4 + j], cy[:, j % 2, :]).then_inc(y_out[j % 2], 16)
                else:
                    act.dma_start(ydram[j - CONV_T], hy[:, :]).then_inc(y_out[j % 2], 16)

            def before_levels(h):
                act.wait_ge(zi_in, 16 * (h + 1))
                step(nc.scalar.activation(hE[:, 1, :], hq[:, 1, :], ACT.Abs))
                step(nc.scalar.activation(hE[:, 1, :], hE[:, 1, :], ACT.Exp, scale=-1.0))
                nc.scalar.activation(hE[:, 1, :], hE[:, 1, :], ACT.Ln, bias=1.0).then_inc(lsg, 1)
                act.wait_ge(hk_raw, h + 1)
                nc.scalar.activation(hk[:, :], hk[:, :], ACT.Exp, scale=-1.0).then_inc(hk_ok, 1)
                for lv in range(2):
                    act.wait_ge(expo, h * (LEVELS + 1) + lv + 1)
                    nc.scalar.activation(hE[:, lv % 2, :], hE[:, lv % 2, :], ACT.Exp).then_inc(decay, 1)

            def load_conv(j):
                act.dma_start(cin[:, 3 * j:3 * j + 3, :],
                              proj[3 * j:3 * j + 3].rearrange("a p n -> p a n")).then_inc(conv_in[j], 16)

            n, quads, gates_read = N_IN - N_GATE, (N_CONV + N_HG) // 4, 0
            act.wait_ge(rstd_used, 5)
            act.dma_start(att_dram, att[:, 3:8, :].rearrange("p a b -> p (a b)")).then_inc(parked, 16)
            for key in GATE_PHASE:
                h = key[1] if len(key) > 1 else None
                if key[0] == "G":
                    s = (n - N_QK) % 4
                    act.wait_ge(spilled[s], 16 * ((n - N_QK) // 4))
                    read_unit(n, n % 2, n // 2, stage[:, s, :], ACT.Copy)
                    act.wait_ge(unit_out[n % 2], n // 2 + 1)
                    n += 1
                    gates_read += 1
                    if gates_read == 1:
                        for i in range(4):
                            act.wait_ge(spilled[i], 16 * quads)
                        act.wait_ge(parked, 16)
                        for j in range(CONV_T - 1):
                            load_conv(j)
                        act.wait_ge(pen_ok, 9)
                        act.dma_start(pen_dram, pen[:, :]).then_inc(pen_parked, 16)
                    act.dma_start(proj[n - 1 - N_QK], stage[:, s, :]).then_inc(spilled[s], 16)
                    if gates_read == 2:
                        act.wait_ge(pen_parked, 16)
                        load_conv(CONV_T - 1)
                    if gates_read in (2, 3, 4):
                        store_y(gates_read - 2)
                    if gates_read == 3:
                        load_head(0, 1, 2, zi_in)
                        load_head(0, 0, 1, q_in)
                        load_head(0, 3, 1, g_in)
                    if gates_read == 5:
                        store_y(CONV_T - 1)
                        before_levels(0)
                elif key[0] == "stat":
                    h = key[2]
                    stat(("hg", h), [mpair(("o", h))[:, :]], (rstd_used, 5) if h == 0 else (y_made, CONV_T + h))
                    store_y(CONV_T + h)
                    if h < HG_HEADS - 1:
                        load_head(h + 1, 3, 1, g_in)
                elif key[0] == "iT":
                    wait_ready(act, key)
                    if h:
                        wait_ready(act, ("o", h - 1))
                    nc.scalar.copy(hiT[:, :, :].rearrange("p a b -> p (a b)"), mpair(key)[:, :]) \
                      .then_inc(F(key), 1)
                elif key[0] == "lv":
                    lv = key[2]
                    if lv == 2 and h < HG_HEADS - 1:
                        act.wait_ge(expo, h * (LEVELS + 1) + 1)
                        wait_ready(act, ("iT", h))
                        load_head(h + 1, 1, 2, zi_in)
                    lv += 2
                    if lv < LEVELS:
                        act.wait_ge(expo, h * (LEVELS + 1) + lv + 1)
                        nc.scalar.activation(hE[:, lv % 2, :], hE[:, lv % 2, :], ACT.Exp).then_inc(decay, 1)
                    elif lv == LEVELS:
                        if h == 0:
                            for par in range(2):
                                act.wait_ge(y_out[par], 16 * (CONV_T // 2))
                        nc.scalar.activation(hqG[:, :], hG[:, :], ACT.Exp).then_inc(decay, 1)
                        act.wait_ge(expo, (h + 1) * (LEVELS + 1))
                        nc.scalar.activation(hE[:, 1, :], hE[:, 1, :], ACT.Exp).then_inc(decay, 1)
                elif key[0] == "kT":
                    wait_ready(act, key)
                    nc.scalar.copy(hkT[:, :, :].rearrange("p a b -> p (a b)"), mpair(key)[:, :]) \
                      .then_inc(F(key), 1)
                    if h < HG_HEADS - 1:
                        act.wait_ge(hfin, h + 1)
                        wait_ready(act, ("lv", h, LEVELS))
                        load_head(h + 1, 0, 1, q_in)
                        before_levels(h + 1)
                elif key[0] == "o":
                    wait_ready(act, key)

            def attention(st, heads, buf, i0):
                N = NB * heads
                for i in range(N + 1):
                    if i < N:
                        w = n_keys(st, i // heads)
                        act.wait_ge(nm_ok, i0 + i + 1)
                        if i >= 2:
                            act.wait_ge(pT_ps, i0 + i - 1)
                        nc.scalar.activation(buf["Pm"][:, i % 2, 0:w], buf["L"][:, i % 2, 0:w], ACT.Exp,
                                             bias=tiny[:, 12 + i % 4:13 + i % 4],
                                             accum_out=tiny[:, 16 + i % 4:17 + i % 4]).then_inc(p_ok, 1)
                    if i >= 1:
                        w = n_keys(st, (i - 1) // heads)
                        act.wait_ge(pT_ps, i0 + i)
                        if i >= 3:
                            act.wait_ge(pv_ok, i0 + i - 2)
                        nc.scalar.copy(buf["PT"][:, (i - 1) % 2, 0:w], pair[0][:, 0:w]).then_inc(pT_ok, 1)

            attention(0, HEADS, at1, 0)
            for b in (NB - 2, NB - 1):
                wait_done(act, ("yT", 0, b))
            def load_gates(j):
                for b in range(3):
                    g = (b + 1) % 3
                    act.dma_start(gates[:, j % 2, b, :], proj[N_CONV + N_HG + 8 * g + j]) \
                       .then_inc(gates_in[j % 2], 16)

            load_gates(0)
            load_gates(1)
            act.wait_ge(branch_lo, 8)
            his(0, [ysp[:, 8 + k, 0, :] for k in range(4)], [yT[:, k, :] for k in range(4)], None)
            for j in range(NT):
                act.wait_ge(gates_in[j % 2], 48 * (j // 2 + 1))
                nc.scalar.activation(gates[:, j % 2, :, :], gates[:, j % 2, :, :], ACT.Sigmoid).then_inc(gate_ok, 1)
                act.wait_ge(mixed_ok, j + 1)
                if j + 2 < NT:
                    load_gates(j + 2)
            his(0, [actA[:, 0, j, :] for j in range(NT)], [mixed[:, j, :] for j in range(NT)],
                None)
            for j in range(NT):
                n = FIRST["out"] + j
                act.wait_ge(unit_out[n % 2], n // 2 + 1)
                nc.scalar.activation(actB[:, 0, j, :], xB[:, j, :], ACT.Copy, scale=SM("ln_mlp", j)) \
                  .then_inc(hi_ok, 1)
            wait_ready(act, "ss1")
            root("ss1", None, EPSV)

            def square_relu(n, par, hn, rel):
                act.wait_ge(unit_out[par], hn + 1)
                nc.scalar.activation(mt[par][:, :], mt[par][:, :], ACT.Square).then_inc(relu_ok, 1)
            for g in range(N_GROUP):
                units(act, FIRST["mlp"] + 16 * g, 8, 2, square_relu)
            base = 3 * NT + 4

            def high_x(n, par, hn, rel):
                act.wait_ge(unit_out[par], hn + 1)
                dst, src = tile(actB, rel, 0), tile(xB, rel)
                nc.scalar.copy(dst, src).then_inc(hi_ok, 1)
            units(act, FIRST["mlp"] + N_MLP - 8, 8, 2, high_x)
            act.wait_ge(u_ok, 8 * N_GROUP)
            act.dma_start(poolw[:, :, :], t["pool_w"]).then_inc(poolw_in, 16)
            act.dma_start(posqi[:, :], t["pos_q"]).then_inc(pos_in, 16)
            base += NT
            n = FIRST["in2"]
            outs = [(u2[:, g, :], ACT.Copy) for g in range(4)] + [(gb[:, g, :], ACT.Silu) for g in range(4)]
            outs += [(xq[:, g, :], ACT.Copy) for g in range(4)] + [(xkv[:, g, :], ACT.Copy) for g in range(2)]
            outs += [(u2[:, g, :], ACT.Silu) for g in range(4)] + [(kr[:, :], ACT.Copy)]
            for dst, func in outs:
                if n == FIRST["in2"] + 14:
                    for g in range(4):
                        wait_ready(act, ("pool", g))
                read_unit(n, n % 2, n // 2, dst, func)
                n += 1
                if n == FIRST["in2"] + 15:
                    stat("xq", [xq[:, g, :] for g in range(4)], None)
            act.dma_start(posi[:, :], t["pos_row"].partition_broadcast(P)).then_inc(pos_in, 16)
            his(0, [xqS[:, 0, g, :] for g in range(4)], [tmp2[:, g % 2, :] for g in range(4)], (nrm, NT + 1))
            stat("xkv", [xkv[:, g, :] for g in range(2)], (rstd_used, 6))
            his(0, [xkvS[:, 0, g, :] for g in range(2)], [tmp2[:, g % 2, :] for g in range(2)], (nrm, NT + 5))
            n = FIRST["uq"]
            act.wait_ge(lo_ok, base + 6)
            for dst in [xq[:, h, :] for h in range(4)] + [qr[:, r, :] for r in range(2)]:
                read_unit(n, n % 2, n // 2, dst, ACT.Copy)
                n += 1
            act.wait_ge(trig_in, 2)
            nc.scalar.activation(cs[:, 0, :], cs[:, 0, :], ACT.Sin).then_inc(trig, 1)
            nc.scalar.activation(cs[:, 1, :], cs[:, 1, :], ACT.Sin).then_inc(trig, 1)
            for dst in [kn[:, h, :] for h in range(4)] + [v4[:, h, :] for h in range(4)]:
                read_unit(n, n % 2, n // 2, dst, ACT.Copy)
                n += 1
            for h in range(MLA_HEADS):
                key = ("v2T", h)
                wait_ready(act, key)
                if h == 0:
                    act.wait_ge(roped, 3)
                nc.scalar.copy(V2[:, :, h * P:(h + 1) * P],
                               mpair(key)[:, :].rearrange("p (a b) -> p a b", b=P)).then_inc(F(key), 1)
            attention(1, MLA_HEADS, at2, NB * HEADS)
            for b in (NB - 2, NB - 1):
                wait_done(act, ("yT", 1, b))
            his(0, [actB[:, 0, j, :] for j in range(NT)],
                [u2[:, j, :] for j in range(4)] + [gb[:, j, :] for j in range(4)], None)
            stat("var", [xB[:, j, :] for j in range(NT)], (roped, 3), LNEPSV, (centred, 1))
            for j in range(NT):
                act.wait_ge(scaled, j + 1)
                if j >= 2:
                    act.wait_ge(fin_out[j % 2], 16 * (j // 2))
                nc.scalar.activation(fin[:, j % 2, :], xB[:, j, :], ACT.Identity, bias=SM("ln_b", j),
                                     scale=SM("ln_g", j)).then_inc(fin_ok, 1)

        @block.vector
        def _(dve):
            steps = [0]

            def step(ins):
                steps[0] += 1
                ins.then_inc(dve_step, 1)
                dve.wait_ge(dve_step, steps[0])

            V = nc.vector

            def low(c, dst, src, hi):
                dve.wait_ge(hi_ok, c + 1)
                V.tensor_tensor(dst, src, hi.bitcast(F32), ALU.subtract).then_inc(lo_ok, 1)

            def norm_split(c0, q0, tiles, gains, tmp, dst):
                for k in range(len(tiles) + 1):
                    if k < len(tiles):
                        if k >= 2:
                            dve.wait_ge(lo_ok, c0 + k - 1)
                        V.scalar_tensor_tensor(tmp[:, k % 2, :], tiles[k], gains[k], rstd[:, :],
                                               ALU.mult, ALU.mult).then_inc(nrm, 1)
                    if k >= 1:
                        dve.wait_ge(nrm, q0 + k)
                        low(c0 + k - 1, dst[:, 1, k - 1, :], tmp[:, (k - 1) % 2, :], dst[:, 0, k - 1, :])

            dve.wait_ge(consts_in, 48)
            for j in range(NT):
                dve.wait_ge(x_tile_in[j], 16)
            dve.wait_ge(rstd_ok, 1)
            norm_split(0, 0, [X0[:, j, :] for j in range(NT)], [SM("ln_mix", j) for j in range(NT)], tmpn, actA)
            wait_ready(dve, "iwT")
            V.tensor_scalar(iw[:, :, :], mpair("iwT")[:, :].rearrange("p (a b) -> p a b", b=P)[:, :, 64:68],
                            float(IDX_HEADS) ** -0.5 * float(HD) ** -0.5, None, ALU.mult).then_inc(F("iwT"), 1)
            wait_done(dve, "iwT")
            c = 0
            off = lambda b: P * b * (b + 1) // 2
            for b in range(2, NB):
                w = P * (b + 1)
                sc = pen[:, off(b):off(b) + w]
                for h in range(IDX_HEADS):
                    wait_done(dve, ("idx", b, h))
                    src = sq[:, c % 2, 0:w]
                    if h == 0:
                        V.tensor_scalar(sc, src, iw[:, b, h:h + 1], None, ALU.mult).then_inc(idx_used, 1)
                    else:
                        dve.wait_ge(idx_used, c)
                        V.scalar_tensor_tensor(sc, src, iw[:, b, h:h + 1], sc, ALU.mult, ALU.add) \
                         .then_inc(idx_used, 1)
                    c += 1
                dve.wait_ge(idx_used, c)
                step(V.tensor_tensor(sc[:, w - P:w], sc[:, w - P:w], C("causal"), ALU.add))
            V.tensor_copy(pen[:, 0:P], C("causal_neg")).then_inc(pen_ok, 1)
            V.memset(pen[:, P:2 * P], 0.0).then_inc(pen_ok, 1)
            V.tensor_copy(pen[:, 2 * P:3 * P], C("causal_neg")).then_inc(pen_ok, 1)
            def norm_qk():
                for j in range(5):
                    dve.wait_ge(rstd_ok, 2 + j)
                    g = SM("q_norm") if j < 4 else SM("k_norm")
                    V.scalar_tensor_tensor(att[:, 3 + j, :], att[:, 3 + j, :], g, qk_rstd[j],
                                           ALU.mult, ALU.mult).then_inc(rstd_used, 1)

            rounds = TOPK // 8
            for b in range(2, NB):
                w = P * (b + 1)
                sc = pen[:, off(b):off(b) + w]
                if b == NB - 1:
                    norm_qk()
                done = (b - 2) * 2 * rounds
                for u in range(rounds):
                    V.max(top8[:, :], sc).then_inc(topk, 1)
                    dve.wait_ge(topk, done + 2 * u + 1)
                    V.match_replace(sc, top8[:, :], sc, PICKED).then_inc(topk, 1)
                    dve.wait_ge(topk, done + 2 * u + 2)
                V.tensor_scalar(sc, sc, 2 * FILL, NEG, ALU.is_gt, ALU.mult).then_inc(pen_ok, 1)
            dve.wait_ge(rstd_used, 5)
            for j in range(CONV_T):
                dve.wait_ge(conv_in[j], 16)
                y = cy[:, j % 2, :]
                step(V.tensor_tensor(cu[:, :], cin[:, 3 * j, :], cin[:, 3 * j + 1, :], ALU.mult))
                if j >= 2:
                    dve.wait_ge(y_out[j % 2], 16 * (j // 2))
                step(V.tensor_scalar(y, cu[:, :], SM("conv", 2 * 4 + j), None, ALU.mult))
                for d in (1, 2):
                    step(V.scalar_tensor_tensor(y[:, d:S], cu[:, 0:S - d], SM("conv", (2 - d) * 4 + j),
                                                y[:, d:S], ALU.mult, ALU.add))
                V.tensor_tensor(y, y, cin[:, 3 * j + 2, :], ALU.mult).then_inc(y_made, 1)
                dve.wait_ge(y_made, j + 1)
            step(V.memset(hattn[:, :, :], 0.0))
            def exponents(lv):
                dst = hE[:, lv % 2, :]
                if lv < LEVELS:
                    m = 64 >> lv
                    gv = hG[:, :].rearrange("p (n x m) -> p n x m", x=2, m=m)
                    dv = dst.rearrange("p (n x m) -> p n x m", x=2, m=m)
                    mid = gv[:, :, 0, m - 1:m].broadcast_to([P, S // (2 * m), m])
                    V.tensor_tensor(dv[:, :, 1, :], gv[:, :, 1, :], mid, ALU.subtract)
                    V.tensor_tensor(dv[:, :, 0, :], mid, gv[:, :, 0, :], ALU.subtract).then_inc(expo, 1)
                else:
                    gv = hG[:, :].rearrange("p (n m) -> p n m", m=P)
                    V.tensor_tensor(dst.rearrange("p (n m) -> p n m", m=P),
                                    gv[:, :, P - 1:P].broadcast_to([P, NB, P]), gv,
                                    ALU.subtract).then_inc(expo, 1)

            def keep(h, lv):
                key = ("lv", h, lv)
                wait_ready(dve, key)
                if lv:
                    wait_done(dve, ("lv", h, lv - 1))
                V.copy_predicated(hattn[:, :, :], hmask[:, lv:lv + 1, :].broadcast_to([P, NB, P]),
                                  mpair(key)[:, :].rearrange("p (a b) -> p a b", b=P)).then_inc(F(key), 1)

            def before_levels(h):
                dve.wait_ge(lsg, h + 1)
                dve.wait_ge(zi_in, 16 * (h + 1))
                V.scalar_tensor_tensor(hk[:, :], hq[:, 1, :], 0.0, hE[:, 1, :], ALU.max, ALU.add) \
                 .then_inc(hk_raw, 1)
                step(V.scalar_tensor_tensor(hE[:, 0, :], hq[:, 1, :], 0.0, hE[:, 1, :],
                                            ALU.min, ALU.subtract))
                dve.wait_ge(hk_raw, h + 1)
                step(V.tensor_tensor_scan(hG[:, :], C("reset"), hE[:, 0, :], 0.0, ALU.mult, ALU.add))
                exponents(0)
                exponents(1)

            def finish(h):
                key = ("o", h)
                wait_ready(dve, key)
                dve.wait_ge(squares, STAT_BASE[("hg", h)] + 1)
                if h:
                    j = CONV_T + h - 1
                    dve.wait_ge(y_out[j % 2], 16 * (j // 2 + 1))
                dve.wait_ge(g_in, 16 * (h + 1))
                V.scalar_tensor_tensor(hy[:, :], mpair(key)[:, :], SM("hg_norm"), hq[:, 3, :],
                                       ALU.mult, ALU.mult).then_inc(F(key), 1)
                wait_done(dve, key)
                dve.wait_ge(rstd_ok, 7 + h)
                V.tensor_tensor(hy[:, :], hy[:, :], rstd[:, :], ALU.mult).then_inc(y_made, 1)

            before_levels(0)
            dve.wait_ge(masks_in, 16)
            for h in range(HG_HEADS):
                e0 = h * (LEVELS + 1)
                dve.wait_ge(hk_ok, h + 1)
                dve.wait_ge(q_in, 16 * (h + 1))
                for lv in range(LEVELS):
                    dve.wait_ge(decay, h * (LEVELS + 2) + lv + 1)
                    if lv >= 2:
                        wait_ready(dve, ("lv", h, lv - 2))
                    elif h:
                        wait_ready(dve, ("lv", h - 1, LEVELS - 1) if lv == 0 else ("kT", h - 1))
                    m = 64 >> lv
                    v = lambda a: a.rearrange("p (n x m) -> p n x m", x=2, m=m)
                    wv, ev = v(hW[:, lv % 2, :]), v(hE[:, lv % 2, :])
                    V.tensor_tensor(wv[:, :, 1, :], v(hq[:, 0, :])[:, :, 1, :], ev[:, :, 1, :], ALU.mult)
                    V.tensor_tensor(wv[:, :, 0, :], v(hk[:, :])[:, :, 0, :], ev[:, :, 0, :],
                                    ALU.mult).then_inc(weighted, 1)
                    if lv + 2 <= LEVELS:
                        dve.wait_ge(weighted, e0 + lv + 1)
                        exponents(lv + 2)
                    if lv == 1 and h:
                        finish(h - 1)
                    if lv >= 1:
                        keep(h, lv - 1)
                dve.wait_ge(decay, h * (LEVELS + 2) + LEVELS + 1)
                step(V.tensor_copy(tiny[:, 0:8], hqG[:, P - 1:S:P]))
                V.tensor_tensor(hqG[:, :], hqG[:, :], hq[:, 0, :], ALU.mult).then_inc(hfin, 1)
                dve.wait_ge(decay, (h + 1) * (LEVELS + 2))
                wait_ready(dve, ("lv", h, LEVELS - 2))
                V.tensor_tensor(hW[:, 1, :], hk[:, :], hE[:, 1, :], ALU.mult).then_inc(weighted, 1)
                keep(h, LEVELS - 1)
                keep(h, LEVELS)
                if h + 1 < HG_HEADS:
                    dve.wait_ge(weighted, e0 + LEVELS + 1)
                    before_levels(h + 1)
                wait_ready(dve, ("dS", h))
                dS = mpair(("dS", h))
                step(V.tensor_copy(hS[:, 1, :], dS[:, 0:P]))
                for c in range(1, NB - 1):
                    ins = V.scalar_tensor_tensor(hS[:, c + 1, :], hS[:, c, :], tiny[:, c:c + 1],
                                                 dS[:, c * P:(c + 1) * P], ALU.mult, ALU.add)
                    if c < NB - 2:
                        step(ins)
                    else:
                        ins.then_inc(F(("dS", h)), 1)
            finish(HG_HEADS - 1)

            def attention(st, heads, dv, scale, buf, i0, b0, mask, write):
                N = NB * heads
                for i in range(N + 4):
                    if i < N:
                        b, h = i // heads, i % heads
                        w, key = n_keys(st, b), ("qk", st, i)
                        m = mask(b, h)
                        wait_ready(dve, key)
                        if i >= 2:
                            dve.wait_ge(p_ok, i0 + i - 1)
                        V.tensor_tensor_reduce(buf["L"][:, i % 2, 0:w], mpair(key)[:, 0:w], m, scale, -3.0e38,
                                               ALU.add, ALU.max, tiny[:, 8 + i % 4:9 + i % 4]) \
                         .then_inc(F(key), 1)
                        wait_done(dve, key)
                        V.tensor_scalar(tiny[:, 12 + i % 4:13 + i % 4], tiny[:, 8 + i % 4:9 + i % 4], -1.0,
                                        None, ALU.mult).then_inc(nm_ok, 1)
                    if 2 <= i < N + 2:
                        j = i - 2
                        b, h = j // heads, j % heads
                        dve.wait_ge(p_ok, i0 + j + 1)
                        step(V.reciprocal(tiny[:, 20 + j % 4:21 + j % 4], tiny[:, 16 + j % 4:17 + j % 4]))
                        dve.wait_ge(pv_ok, i0 + j + 1)
                        if h == 0 and b >= 2:
                            wait_ready(dve, ("yT", st, b - 2))
                        a = (j % 2) * HALF
                        V.tensor_scalar(buf["O"][b % 2][:, h * dv:(h + 1) * dv], pair[1][:, a:a + dv],
                                        tiny[:, 20 + j % 4:21 + j % 4], None, ALU.mult).then_inc(o_ok, 1)
                    if i >= 4 and (i - 3) % heads == 0:
                        b = (i - 3) // heads - 1
                        key = ("yT", st, b)
                        wait_ready(dve, key)
                        src = mpair(key)[:, 0:HALF].rearrange("p (a b) -> p a b", b=P)
                        write(b, src).then_inc(F(key), 1)

            dve.wait_ge(pen_in[0], 16)
            for s in range(4):
                dve.wait_ge(spilled[s], 16 * (N_CONV + N_HG + N_GATE) // 4)

            def mask1(b, h):
                if b == PEN_FIRST and h == 0:
                    dve.wait_ge(pen_in[1], 16)
                return pen[:, off(b):off(b) + P * (b + 1)]
            attention(0, HEADS, HD, float(HD) ** -0.5, at1, 0, 0,
                      mask1,
                      lambda b, src: V.tensor_copy(yT[:, :, b * P:(b + 1) * P], src))
            for b in (NB - 2, NB - 1):
                wait_done(dve, ("yT", 0, b))
            for k in range(4):
                low(NT + k, ysp[:, 8 + k, 1, :], yT[:, k, :], ysp[:, 8 + k, 0, :])
            first = FIRST["up"]
            with dve.Fori(0, 4) as i:
                for jj in range(2):
                    mx = mixed[:, bass.ds(i * 2 + jj, 1), :].rearrange("p a n -> p (a n)")
                    for br in range(3):
                        n = first + 3 * jj + br
                        par, hn = n % 2, i * 3 + n // 2
                        dve.wait_ge(unit_mm, i * 6 + (n + 1))
                        if br == 0:
                            dve.wait_ge(gate_ok, i * 2 + (jj + 1))
                        dst = mx if br == 0 else prod[:, br - 1, :]
                        V.tensor_tensor(dst, pair[par][:, :], gates[:, jj, br, :], ALU.mult) \
                         .then_inc(unit_out[par], 1)
                        dve.wait_ge(unit_out[par], hn + 1)
                        if br == 1:
                            V.tensor_tensor(mx, mx, prod[:, 0, :], ALU.add).then_inc(mix_step, 1)
                        if br == 2:
                            dve.wait_ge(mix_step, i * 2 + (jj + 1))
                            V.tensor_tensor(mx, mx, prod[:, 1, :], ALU.add).then_inc(mixed_ok, 1)
            base = NT + 4
            dve.wait_ge(mixed_ok, NT)
            for j in range(NT):
                low(base + j, actA[:, 1, j, :], mixed[:, j, :], actA[:, 0, j, :])
            dve.wait_ge(x_in, 16 * NT)

            def add_x(n, par, hn, rel):
                dve.wait_ge(unit_mm, n + 1)
                x = tile(xB, rel)
                V.tensor_tensor(x, pair[par][:, :], x, ALU.add).then_inc(unit_out[par], 1)
            V.memset(mt[1][:, :], 0.0).then_inc(ss_sum, 1)
            base += NT
            for j in range(NT):
                n = FIRST["out"] + j
                add_x(n, n % 2, n // 2, j)
                dve.wait_ge(unit_out[n % 2], n // 2 + 1)
                x = xB[:, j, :]
                dve.wait_ge(ss_sum, j + 1)
                V.tensor_tensor(mt[0][:, :], x, x, ALU.mult).then_inc(ss_sq, 1)
                dve.wait_ge(hi_ok, base + j + 1)
                V.scalar_tensor_tensor(actB[:, 1, j, :], x, SM("ln_mlp", j), actB[:, 0, j, :].bitcast(F32),
                                       ALU.mult, ALU.subtract).then_inc(lo_ok, 1)
                dve.wait_ge(ss_sq, j + 1)
                V.tensor_tensor(mt[1][:, :], mt[1][:, :], mt[0][:, :], ALU.add).then_inc(ss_sum, 1)
            base += NT
            dve.wait_ge(lo_ok, base)
            dve.wait_ge(rstd_ok, 11)
            for g in range(N_GROUP):
                n0 = FIRST["mlp"] + 16 * g
                if g:
                    dve.wait_ge(unit_mm, n0)

                def split_u(n, par, hn, rel):
                    c = n - (FIRST["mlp"] + 8 * g)
                    dve.wait_ge(unit_mm, n + 1)
                    if not isinstance(n, int) or c >= 2:
                        dve.wait_ge(u_ok, c - 1)
                    V.scalar_tensor_tensor(mt[par][:, :], pair[par][:, :], 0.0, rstd[:, :],
                                           ALU.max, ALU.mult).then_inc(unit_out[par], 1)
                    dve.wait_ge(relu_ok, c + 1)
                    V.tensor_copy(tile(actA, rel, 0), mt[par][:, :]).then_inc(hfin, 1)
                    dve.wait_ge(hfin, c + (HG_HEADS + 1))
                    V.tensor_tensor(tile(actA, rel, 1), mt[par][:, :], tile(actA, rel, 0).bitcast(F32),
                                    ALU.subtract).then_inc(u_ok, 1)
                if g == 0:
                    for n in range(n0, n0 + 8):
                        split_u(n, n % 2, n // 2, n - n0)
                else:
                    units(dve, n0, 8, 2, split_u)
                if g < N_GROUP - 1:
                    units(dve, n0 + 8, 8, 2, add_x)
                else:
                    def add_split(n, par, hn, rel):
                        add_x(n, par, hn, rel)
                        c = rel + base
                        dve.wait_ge(hi_ok, c + 1)
                        V.tensor_tensor(tile(actB, rel, 1), tile(xB, rel), tile(actB, rel, 0).bitcast(F32),
                                        ALU.subtract).then_inc(lo_ok, 1)
                    units(dve, n0 + 8, 8, 2, add_split)
            base += NT
            for g, win in enumerate(POOL_WINDOWS):
                n = FIRST["in2"] + g
                dve.wait_ge(unit_out[n % 2], n // 2 + 1)
                if g:
                    dve.wait_ge(pooled_ok, g)
                src = u2[:, g, :]
                for d in range(g + 1):
                    sh = 1 << d
                    dst = sq2[:, d % 2, :]
                    step(V.tensor_copy(dst[:, 0:sh], src[:, 0:sh]))
                    step(V.tensor_tensor(dst[:, sh:S], src[:, sh:S], src[:, 0:S - sh], ALU.add))
                    src = dst
                other = sq2[:, (g + 1) % 2, 0:16]
                a = CST["pool"][0] + 16 * g
                step(V.tensor_tensor(other, src[:, 0:16], cst[:, a:a + 16], ALU.mult))
                step(V.scalar_tensor_tensor(u2[:, g, 16:S], src[:, 16:S], 1.0 / win, u2[:, g, 16:S],
                                            ALU.mult, ALU.subtract))
                V.tensor_tensor(u2[:, g, 0:16], other, u2[:, g, 0:16], ALU.subtract).then_inc(pooled_ok, 1)
            for g in range(4):
                key = ("pool", g)
                wait_ready(dve, key)
                n = FIRST["in2"] + 4 + g
                dve.wait_ge(unit_out[n % 2], n // 2 + 1)
                V.scalar_tensor_tensor(gb[:, g, :], mpair(key)[:, :], SM("pool_scale", g), gb[:, g, :],
                                       ALU.mult, ALU.mult).then_inc(F(key), 1)
            dve.wait_ge(rstd_ok, 12)
            dve.wait_ge(unit_mm, FIRST["uq"])
            norm_split(base, NT, [xq[:, g, :] for g in range(4)], [SM("q_norm_2", g) for g in range(4)],
                       tmp2, xqS)
            dve.wait_ge(pos_in, 32)
            V.tensor_copy(posqf[:, :], posqi[:, :]).then_inc(rstd_used, 1)
            dve.wait_ge(rstd_ok, 13)
            dve.wait_ge(lo_ok, base + 4)
            norm_split(base + 4, NT + 4, [xkv[:, g, :] for g in range(2)],
                       [SM("kv_norm_2", g) for g in range(2)], tmp2, xkvS)
            step(V.tensor_copy(posb[:, :], posi[:, :]))
            a0, a1 = ang[:, 0, :], ang[:, 1, :]
            c1 = 6.28125
            c2 = float(np.float32(np.round((TWO_PI - c1) * 2 ** 22) / 2 ** 22))
            c3 = TWO_PI - c1 - c2
            step(V.tensor_scalar(a0, posb[:, :], C("rope")[:, 0:1], None, ALU.mult))
            step(V.tensor_scalar(a1, a0, 1.0 / TWO_PI, MAGIC, ALU.mult, ALU.add))
            step(V.tensor_scalar(a1, a1, -MAGIC, None, ALU.add))
            for cc in (c1, c2, c3):
                step(V.scalar_tensor_tensor(a0, a1, -cc, a0, ALU.mult, ALU.add))
            dve.wait_ge(lo_ok, base + 6)
            LIM = 3.1415925
            V.tensor_scalar(cs[:, 1, :], a0, -LIM, LIM, ALU.max, ALU.min).then_inc(trig_in, 1)
            step(V.tensor_scalar(a0, a0, float(np.pi / 2), None, ALU.add))
            step(V.tensor_scalar(a1, a0, float(np.pi), -TWO_PI, ALU.is_gt, ALU.mult))
            step(V.tensor_tensor(a0, a0, a1, ALU.add))
            V.tensor_scalar(cs[:, 0, :], a0, -LIM, LIM, ALU.max, ALU.min).then_inc(trig_in, 1)
            dve.wait_ge(trig, 2)
            for r in range(3):
                key = ("swap", r)
                x = qr[:, r, :] if r < 2 else kr[:, :]
                wait_ready(dve, key)
                V.tensor_tensor(rtmp[:, :], mpair(key)[:, :], cs[:, 1, :], ALU.mult).then_inc(F(key), 1)
                wait_done(dve, key)
                step(V.tensor_tensor(x, x, cs[:, 0, :], ALU.mult))
                V.tensor_tensor(x, x, rtmp[:, :], ALU.add).then_inc(roped, 1)
                dve.wait_ge(roped, r + 1)

            made = [0]

            def mask2(b, h):
                if h == 0:
                    made[0] += 1
                    V.tensor_scalar(pen2[:, b % 2, :], posb[:, :], posqf[:, b:b + 1], NEG,
                                    ALU.is_gt, ALU.mult).then_inc(pen2_ok, 1)
                    dve.wait_ge(pen2_ok, made[0])
                return pen2[:, b % 2, :]

            def gated(b, src):
                y = u2[:, :, b * P:(b + 1) * P]
                return V.tensor_tensor(y, src, y, ALU.mult)

            attention(1, MLA_HEADS, P, float(192) ** -0.5, at2, NB * HEADS, NB, mask2, gated)
            base += 6
            for b in (NB - 2, NB - 1):
                wait_done(dve, ("yT", 1, b))
            for j in range(NT):
                src = u2[:, j, :] if j < 4 else gb[:, j - 4, :]
                low(base + j, actB[:, 1, j, :], src, actB[:, 0, j, :])

            def add_scaled(n, par, hn, rel):
                dve.wait_ge(unit_mm, n + 1)
                x = tile(xB, rel)
                V.scalar_tensor_tensor(x, x, float(2.0 ** 0.25), pair[par][:, :], ALU.mult, ALU.add) \
                 .then_inc(unit_out[par], 1)
                dve.wait_ge(unit_out[par], hn + 1)
                if isinstance(rel, int) and rel == 0:
                    V.tensor_copy(mu[:, :], x).then_inc(mu_sum, 1)
                else:
                    dve.wait_ge(mu_sum, rel)
                    V.tensor_tensor(mu[:, :], mu[:, :], x, ALU.add).then_inc(mu_sum, 1)
            add_scaled(FIRST["out2"], FIRST["out2"] % 2, FIRST["out2"] // 2, 0)
            dve.wait_ge(lo_ok, base + NT)

            def add_rest(n, par, hn, rel):
                add_scaled(n, par, hn, rel + 1)
            units(dve, FIRST["out2"] + 1, N_OUT2 - 1, 2, add_rest)
            wait_ready(dve, "mu")
            V.tensor_copy(mu[:, :], mpair("mu")[:, :]).then_inc(F("mu"), 1)
            wait_done(dve, "mu")
            for j in range(NT):
                ins = V.tensor_tensor(xB[:, j, :], xB[:, j, :], mu[:, :], ALU.subtract)
                ins.then_inc(centred, 1)
            dve.wait_ge(centred, NT)
            dve.wait_ge(rstd_ok, 14)
            for j in range(NT):
                V.tensor_tensor(xB[:, j, :], xB[:, j, :], rstd[:, :], ALU.mult).then_inc(scaled, 1)


def n_keys(st, b):
    return P * (b + 1) if st == 0 else S


def stat_key(key):
    return ("stat",) + (key if isinstance(key, tuple) else (key,))


def tile(tensor, rel, part=None):
    if part is None:
        return tensor[:, rel, :] if isinstance(rel, int) else \
            tensor[:, bass.ds(rel, 1), :].rearrange("p a n -> p (a n)")
    return tensor[:, part, rel, :] if isinstance(rel, int) else \
        tensor[:, part, bass.ds(rel, 1), :].rearrange("p a n -> p (a n)")


def by_unit(w):
    k, n = w.shape
    return np.ascontiguousarray(w.reshape(k // P, P, n // P, P).transpose(2, 1, 0, 3)
                                .reshape(n // P, P, k))


def by_tile(v):
    return np.ascontiguousarray(v.reshape(-1, P).T)


def kernel(**inputs):
    import concourse.bacc as bacc
    from concourse.bass_utils import run_bass_kernel_spmd

    a = {k: np.asarray(v) for k, v in inputs.items()}
    w = a["w_in"][0]
    cut = np.cumsum([0, 512, 128, 128, 256, 64, 4, 512, 512, 512, 512, 512, 512, 512, 3072])
    aq, ak, av, iq, ik, iw, hq, hf, hi, hg, cb, cc, ch, gt = (w[:, cut[i]:cut[i + 1]] for i in range(14))
    pad = np.zeros((D, 60), np.float32)
    q_cols = [np.concatenate([aq[:, j * 64:(j + 1) * 64], aq[:, (j + 4) * 64:(j + 5) * 64]], 1) for j in range(4)]
    cols = [ik, iw, pad, iq] + q_cols + [ak, av]
    for j in range(4):
        s = slice(j * P, (j + 1) * P)
        cols += [cc[:, s], ch[:, s], cb[:, s]]
    for j in range(4):
        s = slice(j * P, (j + 1) * P)
        cols += [hq[:, s], hf[:, s], hi[:, s], hg[:, s]]
    cols += [gt]
    w_in = np.concatenate(cols, 1)
    ups = [by_unit(a[n][0]) for n in ("w_up_hgrn", "w_up_conv", "w_up_attn")]
    w_up = np.ascontiguousarray(np.stack(ups, 1).reshape(N_UP, P, HALF))
    up, down = by_unit(a["w_mlp_up"][0]), a["w_mlp_down"][0]
    mlp = []
    for g in range(N_GROUP):
        mlp += [up[8 * g:8 * g + 8], by_unit(down[D * g:D * (g + 1)])]
    w = a["w_in_2"]
    cut = np.cumsum([0, 512, 256, 64, 512, 512, 512])
    xq, xkv, kr, ga, up2, gb = (w[:, cut[i]:cut[i + 1]] for i in range(6))
    w_in2 = np.concatenate([up2, gb, xq, xkv, ga, kr, kr], 1)
    uq = a["w_uq_2"].reshape(512, MLA_HEADS, 192)
    uq = np.concatenate([uq[:, :, :P].reshape(512, -1), uq[:, :, P:].reshape(512, -1)], 1)
    ukv = a["w_ukv_2"].reshape(256, MLA_HEADS, 2 * P)
    ukv = np.concatenate([ukv[:, :, :P].reshape(256, -1), ukv[:, :, P:].reshape(256, -1)], 1)
    pos = a["positions_2"][0]
    small = [by_tile(a["ln_mix_g"][0]), by_tile(a["ln_mlp_g"][0]), by_tile(a["hgrn_norm_g"][0]),
             np.tile(a["q_norm_g"][0], 2)[:, None], np.tile(a["k_norm_g"][0], 2)[:, None],
             by_tile(a["conv_w"][0].reshape(-1)), by_tile(a["pool_scale_2"]), by_tile(a["q_norm_g_2"]),
             by_tile(a["kv_norm_g_2"]), by_tile(a["ln_g_2"][0]), by_tile(a["ln_b_2"][0])]
    cst, masks = shape_constants()
    arrays = {
        "xT": a["x"][0].T, "cst": cst, "masks": masks, "small": np.concatenate(small, 1),
        "rel_bias": a["rel_bias"], "w_in": by_unit(w_in), "w_up": w_up, "w_out": by_unit(a["w_out"][0]),
        "w_mlp": np.concatenate(mlp, 0), "w_in2": by_unit(w_in2), "w_uq": by_unit(uq), "w_ukv": by_unit(ukv),
        "w_out2": by_unit(a["w_out_2"]), "pool_w": a["pool_w_2"].transpose(1, 0, 2),
        "pos_row": pos[None, :], "pos_q": pos.reshape(NB, P).T,
    }
    arrays = {k: np.ascontiguousarray(v) for k, v in arrays.items()}
    nc = bacc.Bacc("TRN2", target_bir_lowering=False, num_devices=1)
    t = {k: nc.dram_tensor(k, v.shape, mybir.dt.from_np(v.dtype), kind="ExternalInput").ap()
         for k, v in arrays.items()}
    t["outT"] = nc.dram_tensor("outT", (D, S), F32, kind="ExternalOutput").ap()
    build(nc, t)
    r = run_bass_kernel_spmd(nc, [arrays], core_ids=[0])
    return np.ascontiguousarray(r.results[0]["outT"].T)[None]
```
